# Optimizing a Trainium2 kernel written in Bass

```python
import jax, jax.numpy as jnp
from jax import lax
import numpy as np
import math

D_MODEL = 1024
BATCH = 1
SEQ = 512
DEPTH = 1

D_POOL = D_MODEL // 2
POOL_WINDOWS = (2, 4, 8, 16)
N_POOL_GROUPS = len(POOL_WINDOWS)
POOL_GROUP_DIM = D_POOL // N_POOL_GROUPS
V_HEAD_DIM = 64
N_HEADS = (D_MODEL // 2) // V_HEAD_DIM
D_ATTN = N_HEADS * V_HEAD_DIM
D_MIX = D_POOL + D_ATTN
QK_NOPE_DIM = 64
QK_ROPE_DIM = 32
QK_DIM = QK_NOPE_DIM + QK_ROPE_DIM
Q_LORA_RANK = D_MODEL // 4
KV_LORA_RANK = D_MODEL // 8
ROPE_THETA = 10000.0
Q_BLOCK = 128
D_IN_PROJ = D_POOL + Q_LORA_RANK + KV_LORA_RANK + QK_ROPE_DIM
N_EXPERTS = 32
TOP_K = 4
D_EXPERT = D_MODEL
SWIGLU_ALPHA = 1.702
SWIGLU_LIMIT = 7.0
MOE_BLOCK = 128
RMS_EPS = 1e-6


def rmsnorm(x, g):
    xf = x.astype(jnp.float32)
    y = xf * lax.rsqrt(jnp.mean(xf * xf, axis=-1, keepdims=True) + RMS_EPS)
    return (y * g.astype(jnp.float32)).astype(x.dtype)

def rope_tables(positions):
    half = QK_ROPE_DIM // 2
    inv = ROPE_THETA ** (-jnp.arange(half, dtype=jnp.float32) / half)
    ang = positions.astype(jnp.float32)[..., None] * inv
    return jnp.cos(ang), jnp.sin(ang)

def apply_rope(x, cos, sin):
    half = QK_ROPE_DIM // 2
    xf = x.astype(jnp.float32)
    x1, x2 = xf[..., :half], xf[..., half:]
    out = jnp.concatenate([x1 * cos - x2 * sin, x2 * cos + x1 * sin], axis=-1)
    return out.astype(x.dtype)

def pool_mixer(u, w_pool, b_pool, pool_scale):
    B, S, _ = u.shape
    uf = u.reshape(B, S, N_POOL_GROUPS, POOL_GROUP_DIM).astype(jnp.float32)
    csum = jnp.pad(jnp.cumsum(uf, axis=1), ((0, 0), (1, 0), (0, 0), (0, 0)))
    t = jnp.arange(S)
    pooled = []
    for g, w in enumerate(POOL_WINDOWS):
        c = csum[:, :, g]
        lo = jnp.pad(c[:, :S + 1 - w], ((0, 0), (w - 1, 0), (0, 0)))
        cnt = jnp.minimum(t + 1, w).astype(jnp.float32)[None, :, None]
        pooled.append((c[:, 1:] - lo) / cnt)
    pooled = jnp.stack(pooled, axis=2)
    diff = (pooled - uf).astype(u.dtype)
    mixed = jnp.einsum('bsgc,gcd->bsgd', diff, w_pool) + b_pool
    return mixed.reshape(B, S, D_POOL) * pool_scale

def mla_attention(q_lat, kv_lat, k_rope_raw, cos, sin, g_q_a, w_q_b, g_kv_a, w_kv_b):
    B, S, _ = q_lat.shape
    q = (rmsnorm(q_lat, g_q_a) @ w_q_b).reshape(B, S, N_HEADS, QK_DIM)
    q_nope = q[..., :QK_NOPE_DIM]
    q_rope = apply_rope(q[..., QK_NOPE_DIM:], cos[:, :, None, :], sin[:, :, None, :])
    kv = (rmsnorm(kv_lat, g_kv_a) @ w_kv_b).reshape(B, S, N_HEADS, QK_NOPE_DIM + V_HEAD_DIM)
    k_nope, v = kv[..., :QK_NOPE_DIM], kv[..., QK_NOPE_DIM:]
    k_rope = apply_rope(k_rope_raw, cos, sin)
    scale = QK_DIM ** -0.5
    nb = S // Q_BLOCK
    qn_b = q_nope.reshape(B, nb, Q_BLOCK, N_HEADS, QK_NOPE_DIM).transpose(1, 0, 2, 3, 4)
    qr_b = q_rope.reshape(B, nb, Q_BLOCK, N_HEADS, QK_ROPE_DIM).transpose(1, 0, 2, 3, 4)
    k_idx = jnp.arange(S)

    def attend(args):
        qn, qr, blk = args
        s = (jnp.einsum('bqhd,bkhd->bhqk', qn, k_nope, preferred_element_type=jnp.float32)
             + jnp.einsum('bqhr,bkr->bhqk', qr, k_rope, preferred_element_type=jnp.float32)) * scale
        q_idx = blk * Q_BLOCK + jnp.arange(Q_BLOCK)
        s = jnp.where(k_idx[None, :] <= q_idx[:, None], s, -jnp.inf)
        p = jax.nn.softmax(s, axis=-1).astype(v.dtype)
        return jnp.einsum('bhqk,bkhd->bqhd', p, v)

    out = lax.map(attend, (qn_b, qr_b, jnp.arange(nb)))
    return out.transpose(1, 0, 2, 3, 4).reshape(B, S, D_ATTN)

def moe(h, w_router, b_router, w_gate_up, b_gate_up, w_down, b_down):
    B, S, D = h.shape
    T = B * S
    ht = h.reshape(T, D)
    logits = (ht @ w_router + b_router).astype(jnp.float32)
    top_vals, top_idx = lax.top_k(logits, TOP_K)
    gates = jax.nn.softmax(top_vals, axis=-1)
    n_assign = T * TOP_K
    e_flat = top_idx.reshape(-1).astype(jnp.int32)
    tok_flat = jnp.repeat(jnp.arange(T, dtype=jnp.int32), TOP_K)
    g_flat = gates.reshape(-1)
    order = jnp.argsort(e_flat)
    e_sorted = e_flat[order]
    counts = jnp.zeros((N_EXPERTS,), jnp.int32).at[e_flat].add(1)
    padded = ((counts + MOE_BLOCK - 1) // MOE_BLOCK) * MOE_BLOCK
    start = jnp.cumsum(counts) - counts
    pad_end = jnp.cumsum(padded)
    pad_start = pad_end - padded
    dest = pad_start[e_sorted] + (jnp.arange(n_assign, dtype=jnp.int32) - start[e_sorted])
    n_blocks = n_assign // MOE_BLOCK + N_EXPERTS
    n_rows = n_blocks * MOE_BLOCK
    row_tok = jnp.full((n_rows,), T, jnp.int32).at[dest].set(tok_flat[order])
    row_gate = jnp.zeros((n_rows,), jnp.float32).at[dest].set(g_flat[order])
    block_expert = jnp.minimum(
        jnp.searchsorted(pad_end, jnp.arange(n_blocks, dtype=jnp.int32) * MOE_BLOCK, side='right'),
        N_EXPERTS - 1)
    h_pad = jnp.concatenate([ht, jnp.zeros((1, D), ht.dtype)], axis=0)
    xb = h_pad[row_tok].reshape(n_blocks, MOE_BLOCK, D)

    def expert_block(args):
        xblk, e = args
        gu = xblk @ w_gate_up[e] + b_gate_up[e]
        gate = jnp.minimum(gu[:, :D_EXPERT], SWIGLU_LIMIT)
        up = jnp.clip(gu[:, D_EXPERT:], -SWIGLU_LIMIT, SWIGLU_LIMIT)
        act = gate * jax.nn.sigmoid(SWIGLU_ALPHA * gate) * (up + 1)
        return act @ w_down[e] + b_down[e]

    yb = lax.map(expert_block, (xb, block_expert)).reshape(n_rows, D)
    y = jnp.zeros((T + 1, D), h.dtype).at[row_tok].add(row_gate[:, None].astype(h.dtype) * yb)
    return y[:T].reshape(B, S, D)

def first_inputs(seed: int = 0) -> dict:
    key = jax.random.key(seed)
    ks = jax.random.split(key, 24)
    L, D, E, F = DEPTH, D_MODEL, N_EXPERTS, D_EXPERT
    nrm = lambda k, shape, fan_in: jax.random.normal(k, shape, jnp.float32) * (fan_in ** -0.5)
    gain = lambda k, shape: 1.0 + 0.05 * jax.random.normal(k, shape, jnp.float32)
    small = lambda k, shape: 0.01 * jax.random.normal(k, shape, jnp.float32)
    x = jax.random.normal(ks[0], (BATCH, SEQ, D), jnp.float32)
    positions = jnp.broadcast_to(jnp.arange(SEQ, dtype=jnp.int32), (BATCH, SEQ))
    return {
        'x': x,
        'positions': positions,
        'g_attn_norm': gain(ks[1], (L, D)),
        'w_in': nrm(ks[2], (L, D, D_IN_PROJ), D),
        'w_pool': nrm(ks[3], (L, N_POOL_GROUPS, POOL_GROUP_DIM, POOL_GROUP_DIM), POOL_GROUP_DIM),
        'b_pool': small(ks[4], (L, N_POOL_GROUPS, POOL_GROUP_DIM)),
        'pool_scale': gain(ks[5], (L, D_POOL)),
        'g_q_a': gain(ks[6], (L, Q_LORA_RANK)),
        'w_q_b': nrm(ks[7], (L, Q_LORA_RANK, N_HEADS * QK_DIM), Q_LORA_RANK),
        'g_kv_a': gain(ks[8], (L, KV_LORA_RANK)),
        'w_kv_b': nrm(ks[9], (L, KV_LORA_RANK, N_HEADS * (QK_NOPE_DIM + V_HEAD_DIM)), KV_LORA_RANK),
        'g_out_pool': gain(ks[10], (L, D_POOL)),
        'g_out_attn': gain(ks[11], (L, D_ATTN)),
        'w_out': nrm(ks[12], (L, D_MIX, D), D_MIX),
        'g_ffn_norm': gain(ks[13], (L, D)),
        'w_router': nrm(ks[14], (L, D, E), D),
        'b_router': small(ks[15], (L, E)),
        'w_gate_up': nrm(ks[16], (L, E, D, 2 * F), D),
        'b_gate_up': small(ks[17], (L, E, 2 * F)),
        'w_down': nrm(ks[18], (L, E, F, D), F),
        'b_down': small(ks[19], (L, E, D)),
        'g_final': gain(ks[20], (D,)),
    }

def first_block(x, positions, g_attn_norm, w_in, w_pool, b_pool, pool_scale, g_q_a, w_q_b,
              g_kv_a, w_kv_b, g_out_pool, g_out_attn, w_out, g_ffn_norm, w_router, b_router,
              w_gate_up, b_gate_up, w_down, b_down, g_final):
    cos, sin = rope_tables(positions)
    o1 = D_POOL
    o2 = o1 + Q_LORA_RANK
    o3 = o2 + KV_LORA_RANK
    for l in range(DEPTH):
        h = rmsnorm(x, g_attn_norm[l])
        proj = h @ w_in[l]
        u, q_lat, kv_lat, k_r = proj[..., :o1], proj[..., o1:o2], proj[..., o2:o3], proj[..., o3:]
        y_pool = pool_mixer(u, w_pool[l], b_pool[l], pool_scale[l])
        y_attn = mla_attention(q_lat, kv_lat, k_r, cos, sin, g_q_a[l], w_q_b[l], g_kv_a[l], w_kv_b[l])
        mix = jnp.concatenate([rmsnorm(y_pool, g_out_pool[l]), rmsnorm(y_attn, g_out_attn[l])], axis=-1)
        x = x + mix @ w_out[l]
        h = rmsnorm(x, g_ffn_norm[l])
        x = x + moe(h, w_router[l], b_router[l], w_gate_up[l], b_gate_up[l], w_down[l], b_down[l])
    return rmsnorm(x, g_final)


H_A = 4
DK_A = 128
DV_A = 128
W_A = H_A * DV_A
CONV_W = 4
CHUNK = 64
H_B = 4
R_KV = 128
DV_B = 128
W_B = H_B * DV_B
H_IDX = 8
D_IDX = 64
TOPK_MAX = 256
N_BUCKETS = 32
MAX_EXACT = 16
MAX_DIST = 128
EPS = 1e-6
SPLITS = (3 * W_A, W_A, H_A, H_A, H_B * R_KV, R_KV, W_B, H_IDX * D_IDX, D_IDX, H_IDX)
SPLIT_OFFSETS = (3072 // 2, 2048, 2052, 2056, 2568, 2696, 3208, 3720, 3784)
D_IN = 3792


def rmsnorm_2(x, g):
    xf = x.astype(jnp.float32)
    xf = xf * lax.rsqrt(jnp.mean(xf * xf, axis=-1, keepdims=True) + EPS)
    return xf.astype(x.dtype) * g

def l2norm(x):
    return x * lax.rsqrt(jnp.sum(x * x, axis=-1, keepdims=True) + EPS)

def causal_conv(u, w):
    L = u.shape[1]
    up = jnp.pad(u, ((0, 0), (CONV_W - 1, 0), (0, 0)))
    out = up[:, 0:L] * w[0]
    for j in range(1, CONV_W):
        out = out + up[:, j:j + L] * w[j]
    return out

def t5_bucket(dist):
    n = jnp.maximum(dist, 0)
    nf = jnp.maximum(n, 1).astype(jnp.float32)
    large = MAX_EXACT + (jnp.log(nf / MAX_EXACT) / math.log(MAX_DIST / MAX_EXACT)
                         * (N_BUCKETS - MAX_EXACT)).astype(jnp.int32)
    large = jnp.minimum(large, N_BUCKETS - 1)
    return jnp.where(n < MAX_EXACT, n, large)

def gated_deltanet(qkv, z, b, a, conv_w, a_log, dt_bias, g_norm):
    Bsz, L, _ = qkv.shape
    n_chunks = L // CHUNK
    qkv = jax.nn.silu(causal_conv(qkv, conv_w))
    q, k, v = jnp.split(qkv, 3, axis=-1)

    def heads(t, d):
        t = t.reshape(Bsz, L, H_A, d).transpose(0, 2, 1, 3).astype(jnp.float32)
        return t.reshape(Bsz, H_A, n_chunks, CHUNK, d)

    q = l2norm(heads(q, DK_A)) * (DK_A ** -0.5)
    k = l2norm(heads(k, DK_A))
    v = heads(v, DV_A)
    beta = jax.nn.sigmoid(b.astype(jnp.float32)).transpose(0, 2, 1).reshape(Bsz, H_A, n_chunks, CHUNK)
    g = -jnp.exp(a_log.astype(jnp.float32)) * jax.nn.softplus(a.astype(jnp.float32) + dt_bias.astype(jnp.float32))
    g = g.transpose(0, 2, 1).reshape(Bsz, H_A, n_chunks, CHUNK)
    gc = jnp.cumsum(g, axis=-1)
    pos = jnp.arange(CHUNK)
    causal = pos[:, None] >= pos[None, :]
    strict = pos[:, None] > pos[None, :]
    decay = jnp.exp(jnp.where(causal, gc[..., :, None] - gc[..., None, :], -jnp.inf))
    kb = k * beta[..., None]
    vb = v * beta[..., None]
    lmat = jnp.where(strict, jnp.einsum('bhnik,bhnjk->bhnij', kb, k) * decay, 0.0)
    eye = jnp.eye(CHUNK, dtype=jnp.float32)
    tmat = lax.linalg.triangular_solve(lmat + eye, jnp.broadcast_to(eye, lmat.shape),
                                       left_side=True, lower=True, unit_diagonal=True)
    u = jnp.einsum('bhnij,bhnjd->bhnid', tmat, vb)
    w = jnp.einsum('bhnij,bhnjd->bhnid', tmat, kb * jnp.exp(gc)[..., None])
    attn = jnp.einsum('bhnik,bhnjk->bhnij', q, k) * decay
    qg = q * jnp.exp(gc)[..., None]
    kg = k * jnp.exp(gc[..., -1:] - gc)[..., None]
    glast = jnp.exp(gc[..., -1])
    xs = tuple(jnp.moveaxis(t, 2, 0) for t in (qg, kg, u, w, attn, glast))

    def step(S, inp):
        qg_c, kg_c, u_c, w_c, attn_c, gl_c = inp
        v_new = u_c - jnp.einsum('bhck,bhkv->bhcv', w_c, S)
        o = jnp.einsum('bhck,bhkv->bhcv', qg_c, S) + jnp.einsum('bhij,bhjv->bhiv', attn_c, v_new)
        S = S * gl_c[..., None, None] + jnp.einsum('bhck,bhcv->bhkv', kg_c, v_new)
        return S, o

    S0 = jnp.zeros((Bsz, H_A, DK_A, DV_A), jnp.float32)
    _, o = lax.scan(step, S0, xs)
    o = jnp.moveaxis(o, 0, 2).reshape(Bsz, H_A, L, DV_A).transpose(0, 2, 1, 3)
    o = rmsnorm_2(o, g_norm.astype(jnp.float32))
    o = o.reshape(Bsz, L, W_A) * jax.nn.silu(z.astype(jnp.float32))
    return o.astype(qkv.dtype)

def dsa_sparse_attention(q_b, ckv, iq, ik, iw, g_kv, w_uv, rel_bias, z):
    Bsz, L, _ = q_b.shape
    n_blocks = L // Q_BLOCK
    k_top = min(TOPK_MAX, L // 4)
    ckv = rmsnorm_2(ckv, g_kv)
    q_b = q_b.reshape(Bsz, L, H_B, R_KV)
    iq = iq.reshape(Bsz, L, H_IDX, D_IDX)
    iw = iw * (H_IDX ** -0.5 * D_IDX ** -0.5)
    key_pos = jnp.arange(L, dtype=jnp.int32)

    def to_blocks(t):
        return jnp.moveaxis(t.reshape((Bsz, n_blocks, Q_BLOCK) + t.shape[2:]), 1, 0)

    def block(args):
        qb, iqb, iwb, t0 = args
        t = t0 + jnp.arange(Q_BLOCK, dtype=jnp.int32)
        rel = jnp.einsum('bqhd,bsd->bqhs', iqb, ik)
        score = jnp.einsum('bqh,bqhs->bqs', iwb.astype(jnp.float32), jax.nn.relu(rel).astype(jnp.float32))
        score = jnp.where(key_pos[None, None, :] <= t[None, :, None], score, -jnp.inf)
        _, sel = lax.top_k(score, k_top)
        kv_sel = jax.vmap(lambda kv, i: kv[i])(ckv, sel)
        dist = t[None, :, None] - sel
        bias = jnp.moveaxis(rel_bias[t5_bucket(dist)], 3, 2)
        logits = (jnp.einsum('bqhr,bqkr->bqhk', qb, kv_sel).astype(jnp.float32) * (R_KV ** -0.5)
                  + bias.astype(jnp.float32))
        logits = jnp.where((dist >= 0)[:, :, None, :], logits, -jnp.inf)
        p = jax.nn.softmax(logits, axis=-1).astype(kv_sel.dtype)
        return jnp.einsum('bqhk,bqkr->bqhr', p, kv_sel)

    t0s = jnp.arange(n_blocks, dtype=jnp.int32) * Q_BLOCK
    o = lax.map(block, (to_blocks(q_b), to_blocks(iq), to_blocks(iw), t0s))
    o = jnp.moveaxis(o, 0, 1).reshape(Bsz, L, H_B, R_KV)
    o = jnp.einsum('blhr,hrd->blhd', o, w_uv).reshape(Bsz, L, W_B)
    return o * jax.nn.silu(z)

def second_inputs(seed: int = 0) -> dict:
    key = jax.random.key(seed)
    ks = jax.random.split(key, 16)
    nrm = jax.random.normal
    x = nrm(ks[0], (BATCH, SEQ, D_MODEL), jnp.float32)
    c = nrm(ks[1], (BATCH, D_MODEL), jnp.float32)
    w_ada = nrm(ks[2], (DEPTH, D_MODEL, 3 * D_MODEL), jnp.float32) * (0.5 * D_MODEL ** -0.5)
    b_ada = 0.01 * nrm(ks[3], (DEPTH, 3 * D_MODEL), jnp.float32)
    g_pre = 1.0 + 0.05 * nrm(ks[4], (DEPTH, D_MODEL), jnp.float32)
    w_in = nrm(ks[5], (DEPTH, D_MODEL, D_IN), jnp.float32) * (D_MODEL ** -0.5)
    conv_w = nrm(ks[6], (DEPTH, CONV_W, 3 * W_A), jnp.float32) * (CONV_W ** -0.5)
    a_log = jnp.log(jax.random.uniform(ks[7], (DEPTH, H_A), jnp.float32, 1.0, 16.0))
    dt = jnp.exp(jax.random.uniform(ks[8], (DEPTH, H_A), jnp.float32, math.log(1e-3), math.log(1e-1)))
    dt_bias = dt + jnp.log(-jnp.expm1(-dt))
    g_gdn = 1.0 + 0.05 * nrm(ks[9], (DEPTH, DV_A), jnp.float32)
    g_kv = 1.0 + 0.05 * nrm(ks[10], (DEPTH, R_KV), jnp.float32)
    w_uv = nrm(ks[11], (DEPTH, H_B, R_KV, DV_B), jnp.float32) * (R_KV ** -0.5)
    rel_bias = 0.5 * nrm(ks[12], (N_BUCKETS, H_B), jnp.float32)
    w_out = nrm(ks[13], (DEPTH, W_A + W_B, D_MODEL), jnp.float32) * ((W_A + W_B) ** -0.5)
    g_post = 1.0 + 0.05 * nrm(ks[14], (DEPTH, D_MODEL), jnp.float32)
    return {'x': x, 'c': c, 'w_ada': w_ada, 'b_ada': b_ada, 'g_pre': g_pre, 'w_in': w_in,
            'conv_w': conv_w, 'a_log': a_log, 'dt_bias': dt_bias, 'g_gdn': g_gdn, 'g_kv': g_kv,
            'w_uv': w_uv, 'rel_bias': rel_bias, 'w_out': w_out, 'g_post': g_post}

def second_block(x, c, w_ada, b_ada, g_pre, w_in, conv_w, a_log, dt_bias, g_gdn, g_kv, w_uv, rel_bias, w_out, g_post):
    for layer in range(DEPTH):
        mod = jax.nn.silu(c) @ w_ada[layer] + b_ada[layer]
        shift, scale, gate = jnp.split(mod, 3, axis=-1)
        h = rmsnorm_2(x, g_pre[layer]) * (1.0 + scale[:, None, :]) + shift[:, None, :]
        proj = h @ w_in[layer]
        (qkv_a, z_a, b_a, a_a, q_b, ckv, z_b, iq, ik, iw) = jnp.split(proj, list(SPLIT_OFFSETS), axis=-1)
        o_a = gated_deltanet(qkv_a, z_a, b_a, a_a, conv_w[layer], a_log[layer], dt_bias[layer], g_gdn[layer])
        o_b = dsa_sparse_attention(q_b, ckv, iq, ik, iw, g_kv[layer], w_uv[layer], rel_bias, z_b)
        mix = jnp.concatenate([o_a, o_b], axis=-1) @ w_out[layer]
        x = x + gate[:, None, :] * rmsnorm_2(mix, g_post[layer])
    return x


def setup_inputs(seed=0):
    out = dict(first_inputs(seed))
    for name, value in second_inputs(seed + 1).items():
        if name != "x":
            out[name + "_2"] = value
    return out


def reference(
    x, positions, g_attn_norm, w_in, w_pool, b_pool, pool_scale, g_q_a, w_q_b, g_kv_a, w_kv_b,
    g_out_pool, g_out_attn, w_out, g_ffn_norm, w_router, b_router, w_gate_up, b_gate_up, w_down,
    b_down, g_final, c_2, w_ada_2, b_ada_2, g_pre_2, w_in_2, conv_w_2, a_log_2, dt_bias_2,
    g_gdn_2, g_kv_2, w_uv_2, rel_bias_2, w_out_2, g_post_2,
):
    x = first_block(
        x, positions, g_attn_norm, w_in, w_pool, b_pool, pool_scale, g_q_a, w_q_b, g_kv_a,
        w_kv_b, g_out_pool, g_out_attn, w_out, g_ffn_norm, w_router, b_router, w_gate_up,
        b_gate_up, w_down, b_down, g_final,
    )
    return second_block(
        x, c_2, w_ada_2, b_ada_2, g_pre_2, w_in_2, conv_w_2, a_log_2, dt_bias_2, g_gdn_2,
        g_kv_2, w_uv_2, rel_bias_2, w_out_2, g_post_2,
    )


_drawn_inputs = setup_inputs


def setup_inputs(seed=0):
    import zlib

    import numpy as np

    out = dict(_drawn_inputs(seed))
    spreads = {}
    factors = {'b_gate_up': 8.0,
     'b_down': 8.0,
     'b_ada_2': 4.433,
     'g_gdn_2': 14.35,
     'g_kv_2': 8.0,
     'rel_bias_2': 2.917,
     'g_post_2': 3.882}
    for name, (base, spread) in spreads.items():
        noise = np.random.default_rng([zlib.crc32(name.encode()), seed]).standard_normal(out[name].shape)
        drawn = base * np.exp(spread * noise) if base else spread * noise
        out[name] = __import__('jax').numpy.asarray(drawn.astype(out[name].dtype))
    for name, factor in factors.items():
        out[name] = (out[name] * factor).astype(out[name].dtype)
    return out
```

```python
import math
from contextlib import ExitStack

import numpy as np
import concourse.bass as bass
from concourse import mybir

P = 128
F32, BF16, F16 = mybir.dt.float32, mybir.dt.bfloat16, mybir.dt.float16
I32, U32 = mybir.dt.int32, mybir.dt.uint32
ALU = mybir.AluOpType
ACT = mybir.ActivationFunctionType
AX = mybir.AxisListType.X

S, D = 512, 1024
T, KT = S // P, D // P
EPS = 1e-6
NEG = -1.0e30
D_POOL, GROUPS = 512, 4
H1, NOPE, ROPE, DV1 = 8, 64, 32, 64
QK = NOPE + ROPE
QLAT, KVLAT = 256, 128
D_IN1 = D_POOL + QLAT + KVLAT + ROPE
E, TOPK, DE = 32, 4, 1024
ALPHA, LIMIT = 1.702, 7.0
MAX_EXTRA = 16
BLOCKS = E + MAX_EXTRA
CHUNKS = 12
HA, HB, HI, DI = 4, 4, 8, 64
D_IN2 = 3792
CONV = 4
KEEP = 128
BUCKETS = 32

VEC = {}
_at = 0
for _name, _n in (("g_attn", 8), ("b_pool", 4), ("pool_scale", 4), ("g_q", 2), ("g_kv", 1),
                  ("g_out_pool", 4), ("g_out_attn", 4), ("c", 8), ("g_pre", 8), ("b_ada", 16),
                  ("g_gdn", 1), ("g_kv2", 1), ("conv", 48)):
    VEC[_name] = _at
    _at += _n
NVEC = _at

CON = {}
_at = 0
for _name, _n in (("ident", P), ("ones", P), ("upper", P), ("strict", P), ("negmask", P), ("iota", P),
                  ("token", T), ("freq", 1), ("phase", 1), ("sign", 1), ("base0", E), ("iota16", MAX_EXTRA),
                  ("poolinv", 4 * 16)):
    CON[_name] = _at
    _at += _n
NCON = _at


def constants():
    c = np.zeros((P, NCON), np.float32)
    p = np.arange(P)
    part, free = p[:, None], p[None, :]

    def put(name, value, n):
        c[:, CON[name]:CON[name] + n] = value

    put("ident", part == free, P)
    put("ones", 1.0, P)
    put("upper", part <= free, P)
    put("strict", part < free, P)
    put("negmask", np.where(free <= part, 0.0, NEG), P)
    put("iota", free, P)
    put("token", part + P * np.arange(T)[None, :], T)
    half = ROPE // 2
    freq = (np.float32(10000.0) ** (-np.arange(half, dtype=np.float32) / np.float32(half))).astype(np.float32)
    put("freq", freq[p % half][:, None], 1)
    put("sign", np.where(p % ROPE < half, -1.0, 1.0)[:, None], 1)
    put("base0", P * np.arange(E)[None, :], E)
    put("iota16", np.arange(MAX_EXTRA)[None, :], MAX_EXTRA)
    t = np.arange(16)
    put("poolinv", np.concatenate([1.0 / np.minimum(t + 1, w) for w in (2, 4, 8, 16)])[None, :], 64)
    levels = np.zeros((P, 8 * P), np.float32)
    levels[:, 7 * P:] = part + free == P - 1
    for n in range(7):
        b = 1 << n
        same = part // (2 * b) == free // (2 * b)
        put_at = same & (part % (2 * b) < b) & (free % (2 * b) >= b)
        levels[:, n * P:(n + 1) * P] = put_at
    dist = (S - 1) - np.arange(S + P)
    n = np.maximum(dist, 0)
    nf = np.maximum(n, 1).astype(np.float32)
    large = 16 + (np.log(nf / np.float32(16)) / np.float32(math.log(8.0)) * np.float32(16)).astype(np.int32)
    bucket = np.where(n < 16, n, np.minimum(large, BUCKETS - 1))
    onehot = (bucket[None, :] == np.arange(BUCKETS)[:, None]).astype(np.float32)
    return c, levels, onehot


class Place:

    def __init__(self, base, at, end):
        self.base, self.at, self.end = base, at, end

    def take(self, *shape, dt=F32, parts=P):
        n = int(np.prod(shape))
        words = n if dt not in (BF16, F16) else (n + 1) // 2
        assert self.at + words <= self.end, (self.at, words, self.end)
        ap = self.base[0:parts, self.at:self.at + words]
        self.at += words
        if dt != F32:
            ap = ap.bitcast(dt)
        if len(shape) == 2:
            ap = ap.rearrange("p (a b) -> p a b", a=shape[0])
        if len(shape) == 3:
            ap = ap.rearrange("p (a b c) -> p a b c", a=shape[0], b=shape[1])
        return ap


RING = CHUNKS * 2048
REST = 28632


def build(nc, a, out):
    with ExitStack() as ctx:
        sems, stages = {}, []

        def sig(name):
            if name not in sems:
                sems[name] = nc.alloc_semaphore(f"{name}_{len(stages)}")
            return sems[name]

        def retire(kept=""):
            done = [n for n in sems if not (kept and n.startswith(kept))]
            nc.clear_and_free_semaphores([sems.pop(n) for n in done])
            nc.all_engine_barrier()
            stages.append(len(done))

        ring = ctx.enter_context(nc.sbuf_tensor("ring", [P, RING], F32))
        rest = ctx.enter_context(nc.sbuf_tensor("rest", [P, REST], F32))
        bank = [ctx.enter_context(nc.psum_tensor(f"bank{n}", [P, 512], F32)) for n in range(8)]
        keep = Place(rest, 0, REST)
        m = {"ring": ring, "rest": rest, "bank": bank, "sig": sig}
        m["x"] = keep.take(T, D)
        m["con"] = keep.take(NCON)
        m["vecT"] = keep.take(P)
        m["mod_scale"] = keep.take(KT)
        m["mod_shift"] = keep.take(KT)
        m["gate_row"] = keep.take(D)
        m["ident_b"] = keep.take(P, dt=BF16)
        m["ones_b"] = keep.take(P, dt=BF16)
        m["strict_b"] = keep.take(P, dt=BF16)
        m["negmask_b"] = keep.take(P, dt=BF16)
        m["slot"] = keep.take(T, E + 2)
        m["gates"] = keep.take(T, TOPK)
        m["dest"] = keep.take(T, TOPK, dt=I32)
        m["extra"] = keep.take(4 * MAX_EXTRA)
        m["extra_i"] = keep.take(2 * MAX_EXTRA + 2, dt=I32)
        m["free"] = keep.at
        m["h2_dram"] = nc.dram_tensor("h2_rows", [S, D], F32, kind="Internal").ap()
        m["y_dram"] = nc.dram_tensor("expert_rows", [BLOCKS * P, D], F32, kind="Internal").ap()
        m["bias_dram"] = nc.dram_tensor("bias_by_distance", [HB, S + P], F32, kind="Internal").ap()
        first_block(nc, a, m)
        retire("chunk_loaded")
        experts(nc, a, m)
        retire()
        extra_experts(nc, a, m)
        retire()
        second_block(nc, a, m, out)


def con(m, name, n, parts=P):
    return m["con"][0:parts, CON[name]:CON[name] + n]


def col(m, name, n=0, parts=P):
    at = VEC[name] + n
    return m["vecT"][0:parts, at:at + 1]


class Chain:

    def __init__(self, eng, sem):
        self.eng, self.sem, self.n = eng, sem, 0

    def link(self, ins):
        self.n += 1
        ins.then_inc(self.sem, 1)
        self.eng.wait_ge(self.sem, self.n)


def newton(nc, chain, y, v, tmp):
    chain.link(nc.vector.scalar_tensor_tensor(out=tmp, in0=v, scalar=-0.5, in1=y, op0=ALU.mult, op1=ALU.mult))
    chain.link(nc.vector.tensor_tensor(tmp, tmp, y, ALU.mult))
    return nc.vector.scalar_tensor_tensor(out=y, in0=tmp, scalar=1.5, in1=y, op0=ALU.add, op1=ALU.mult)


def first_block(nc, a, m):
    sig, bank, ring, rest, x = m["sig"], m["bank"], m["ring"], m["rest"], m["x"]
    keep = Place(rest, m["free"], REST)
    ident, ones = con(m, "ident", P), con(m, "ones", P)
    ident_b, negmask_b, ones_b, strict_b = m["ident_b"], m["negmask_b"], m["ones_b"], m["strict_b"]
    link_v, link_a, link_p = sig("A_vector_own"), sig("A_scalar_own"), sig("A_pool_own")

    head = Place(ring, 0, 8 * 2048)
    xn = head.take(T, D)
    hT = head.take(KT, S)
    w_swap = head.take(2, 2 * P)
    w_q, w_qr = head.take(2, H1 * NOPE), head.take(2, H1 * ROPE)
    w_pool = head.take(GROUPS, P)
    qT = xn.rearrange("p a b -> p (a b)").rearrange("p (h s) -> p h s", h=H1)
    kT = hT
    tail = Place(ring, 8 * 2048, RING)
    w_in = tail.take(KT, D_IN1)
    krope_w = tail.take(KT, ROPE)
    w_out = ring[:, 8 * 2048:RING].rearrange("p (k n) -> p k n", k=KT)

    late = Place(rest, keep.at, REST)
    w_ada, acc = late.take(2, 3 * D), late.take(3 * D)
    probs, probsT = keep.take(2, S), keep.take(2, S)
    rope_c, rope_s = keep.take(S), keep.take(S)
    w_k, w_v = keep.take(H1 * NOPE), keep.take(H1 * DV1)
    v_sb = keep.take(T, S)
    cos, sin = keep.take(S), keep.take(S)
    lat = keep.take(3, S)
    sq = keep.take(2, S)
    assert late.at <= keep.at
    var, inv, tmp = keep.take(S), keep.take(S), keep.take(S)
    mixT = keep.take(KT, S)
    y_attn = keep.take(T, S)
    uT = keep.take(GROUPS, S)
    h2 = rest[:, keep.at - 2 * GROUPS * S:keep.at].rearrange("p (t d) -> p t d", t=T)
    h2T = mixT
    g_ffn = keep.take(D)
    w_router, b_router = keep.take(KT, E), keep.take(E)
    pa, pb = keep.take(S), keep.take(S)
    small = keep.take(136)
    b_ada_row = rest[:, keep.at - 136 - 2 * S:keep.at - 136]
    vec = y_attn.rearrange("p a b -> p (a b)")[:, 0:P]
    pos_i = mixT.rearrange("p a b -> p (a b)")[:, 0:S].bitcast(I32)
    ang = mixT.rearrange("p a b -> p (a b)")[:, S:2 * S]
    turn = mixT.rearrange("p a b -> p (a b)")[:, 2 * S:3 * S]
    ss, ssv, ssi, sst = (small[:, 4 * n:4 * n + 4] for n in range(4))
    rowmax, rowsum, rowinv = (small[:, 16 + 32 * n:48 + 32 * n] for n in range(3))
    silu_c = small[:, 112:120]
    silu_t = small[:, 120:128]
    room = Place(rest, m["free"], m["free"] + 6 * D)
    b_down = room.take(D)
    logits, picked, ranks, total = (room.take(T, E) for _ in range(4))
    hot, hot2, hot3 = (room.take(T * TOPK, E) for _ in range(3))
    best, place_k = room.take(T, 8), room.take(T * TOPK)
    place_i = room.take(T, 8, dt=U32)
    picked_b = room.take(T, E, dt=BF16)
    count, extra, upto, base1, one_e = (room.take(E) for _ in range(5))
    gsum, ginv = room.take(T), room.take(T)
    ej, bj = room.take(MAX_EXTRA), room.take(MAX_EXTRA)
    gateT = room.take(T, P, parts=E)
    SCALE = QK ** -0.5
    N_ATT = T * H1

    def keys(i):
        return (i // H1 + 1) * P

    with nc.Block() as block:

        @block.sync
        def _(sp):
            sp.dma_start(m["con"], a["constants"]).then_inc(sig("con_loaded"), 16)
            for t in range(T):
                sp.dma_start(x[:, t, :], a["x"][0, t * P:(t + 1) * P, :]).then_inc(sig(f"x_loaded{t}"), 16)
            rows = [("g_attn", a["g_attn_norm"].rearrange("l (r q) -> (l r) q", q=P)),
                    ("b_pool", a["b_pool"].rearrange("l g c -> (l g) c")),
                    ("pool_scale", a["pool_scale"].rearrange("l (r q) -> (l r) q", q=P)),
                    ("g_q", a["g_q_a"].rearrange("l (r q) -> (l r) q", q=P)),
                    ("g_kv", a["g_kv_a"]),
                    ("g_out_pool", a["g_out_pool"].rearrange("l (r q) -> (l r) q", q=P)),
                    ("g_out_attn", a["g_out_attn"].rearrange("l (r q) -> (l r) q", q=P)),
                    ("c", a["c_2"].rearrange("l (r q) -> (l r) q", q=P)),
                    ("g_pre", a["g_pre_2"].rearrange("l (r q) -> (l r) q", q=P)),
                    ("b_ada", a["b_ada_2"][:, 0:2 * D].rearrange("l (r q) -> (l r) q", q=P)),
                    ("g_gdn", a["g_gdn_2"]),
                    ("g_kv2", a["g_kv_2"]),
                    ("conv", a["conv_w_2"].rearrange("l j (r q) -> (l j r) q", q=P))]
            for name, src in rows:
                sp.dma_start(vec[VEC[name]:VEC[name] + src.shape[0], :], src).then_inc(sig("vec_loaded"), 16)
            for k in range(KT):
                sp.dma_start(w_in[:, k, :], a["w_in"][0, k * P:(k + 1) * P, :]).then_inc(sig("w_in_loaded"), 16)
            sp.dma_start(pos_i, a["positions"].partition_broadcast(P)).then_inc(sig("pos_loaded"), 16)
            for k in range(2):
                src = a["w_q_b"][0, k * P:(k + 1) * P, :].rearrange("p (h c) -> p h c", h=H1)
                sp.dma_start(w_q[:, k, :].rearrange("p (h c) -> p h c", h=H1), src[:, :, 0:NOPE]).then_inc(sig("w_q_loaded"), 16)
                sp.dma_start(w_qr[:, k, :].rearrange("p (h c) -> p h c", h=H1), src[:, :, NOPE:QK]).then_inc(sig("w_q_loaded"), 16)
            src = a["w_kv_b"][0].rearrange("p (h c) -> p h c", h=H1)
            sp.dma_start(w_k.rearrange("p (h c) -> p h c", h=H1), src[:, :, 0:NOPE]).then_inc(sig("w_kv_loaded"), 16)
            sp.dma_start(w_v.rearrange("p (h c) -> p h c", h=H1), src[:, :, NOPE:P]).then_inc(sig("w_kv_loaded"), 16)
            sp.dma_start(w_pool, a["w_pool"][0].rearrange("g c d -> c g d")).then_inc(sig("w_pool_loaded"), 16)
            sp.dma_start(m["gate_row"], a["g_post_2"].partition_broadcast(P)).then_inc(sig("g_post_loaded"), 16)
            sp.dma_start(g_ffn, a["g_ffn_norm"].partition_broadcast(P)).then_inc(sig("g_ffn_loaded"), 16)
            sp.dma_start(w_router, a["w_router"][0].rearrange("(k p) n -> p k n", p=P)).then_inc(sig("router_loaded"), 16)
            sp.dma_start(b_router, a["b_router"].partition_broadcast(P)).then_inc(sig("router_loaded"), 16)
            sp.wait_ge(sig("proj_done"), 9)
            for k in range(KT):
                sp.dma_start(w_out[:, k, :], a["w_out"][0, k * P:(k + 1) * P, :]).then_inc(sig("w_out_loaded"), 16)
            sp.wait_ge(sig("pool_mixed"), GROUPS)
            sp.dma_start(b_ada_row, a["b_ada_2"][:, 2 * D:3 * D].partition_broadcast(P)).then_inc(sig("b_ada2_loaded"), 16)
            sp.wait_ge(sig("weighed"), N_ATT)
            for k in range(2):
                sp.dma_start(w_ada[:, k, :], a["w_ada_2"][0, k * P:(k + 1) * P, :]).then_inc(sig(f"w_ada_loaded{k}"), 16)
            for c in range(8):
                load_chunk(sp, a, m, 0, c)
            for k in range(2, KT):
                sp.wait_ge(sig("ada_added"), k - 1)
                sp.dma_start(w_ada[:, k % 2, :], a["w_ada_2"][0, k * P:(k + 1) * P, :]).then_inc(sig(f"w_ada_loaded{k % 2}"), 16)
            sp.wait_ge(sig("ada_added"), KT)
            sp.dma_start(b_down[0:E, :], a["b_down"][0]).then_inc(sig("b_down_loaded"), 16)
            sp.wait_ge(sig("out_done"), 2 * T)
            for c in range(8, CHUNKS):
                load_chunk(sp, a, m, 0, c)
            for t in range(T):
                sp.wait_ge(sig("h2_ready"), t + 1)
                sp.dma_start(m["h2_dram"][t * P:(t + 1) * P, :], h2[:, t, :]).then_inc(sig("h2_stored"), 16)
            sp.wait_ge(sig("h2_stored"), 16 * T)

        @block.gpsimd
        def _(pool):
            chain = Chain(pool, link_p)
            pool.wait_ge(sig("w_in_loaded"), 16 * KT)
            o = D_IN1 - ROPE
            nc.gpsimd.tensor_copy(krope_w[:, :, 0:16], w_in[:, :, o + 16:o + 32])
            nc.gpsimd.tensor_copy(krope_w[:, :, 16:32], w_in[:, :, o:o + 16]).then_inc(sig("krope_w_ready"), 1)
            pool.wait_ge(sig("w_q_loaded"), 64)
            for k in range(2):
                src = w_qr[:, k, :].rearrange("p (h c) -> p h c", h=H1)
                dst = w_swap[:, k, :].rearrange("p (h c) -> p h c", h=H1)
                nc.gpsimd.tensor_copy(dst[:, :, 0:16], src[:, :, 16:32])
                ins = nc.gpsimd.tensor_copy(dst[:, :, 16:32], src[:, :, 0:16])
            ins.then_inc(sig("w_swap_ready"), 1)
            for g in range(GROUPS):
                pool.wait_ge(sig("uT_ready"), g + 1)
                cur = uT[:, g, :]
                if g:
                    pool.wait_ge(sig("pool_mixed"), g)
                for n in range(g + 1):
                    d, nxt = 1 << n, (pa, pb)[(g - n) % 2]
                    nc.gpsimd.tensor_copy(nxt[:, 0:d], cur[:, 0:d])
                    chain.link(nc.gpsimd.tensor_tensor(nxt[:, d:S], cur[:, d:S], cur[:, 0:S - d], ALU.add))
                    cur = nxt
                w = 2 << g
                inv16 = m["con"][:, CON["poolinv"] + 16 * g:CON["poolinv"] + 16 * g + 16]
                chain.link(nc.gpsimd.tensor_scalar(pa[:, 16:S], pa[:, 16:S], 1.0 / w, None, ALU.mult))
                chain.link(nc.gpsimd.tensor_tensor(pa[:, 0:16], pa[:, 0:16], inv16, ALU.mult))
                nc.gpsimd.tensor_tensor(pa, pa, uT[:, g, :], ALU.subtract).then_inc(sig("pool_diff"), 1)

        @block.scalar
        def _(act):
            chain = Chain(act, link_a)
            for t in range(T):
                act.wait_ge(sig(f"x_loaded{t}"), 16)
                nc.scalar.activation(xn[:, t, :], x[:, t, :], ACT.Square, accum_out=ss[:, t:t + 1]).then_inc(sig("x_squares"), 1)

            def rsqrt(k, y, v):
                act.wait_ge(sig("var_ready"), k + 1)
                chain.link(nc.scalar.activation(y, v, ACT.Ln))
                nc.scalar.activation(y, y, ACT.Exp, scale=-0.5).then_inc(sig("rsqrt_ready"), 1)

            rsqrt(0, ssi, ssv)
            act.wait_ge(sig("vecT_ready"), 1)
            nc.scalar.activation(silu_t, m["vecT"][:, VEC["c"]:VEC["c"] + 8], ACT.Exp, scale=-1.0).then_inc(sig("c_exp"), 1)
            for k in range(0, KT, 2):
                act.wait_ge(sig("hT_turned"), k + 1)
                nc.scalar.activation(hT[:, k, :], bank[k % 2][:], ACT.Copy, scale=col(m, "g_attn", k)).then_inc(sig("hT_ready0"), 1)
            act.wait_ge(sig("angles_ready"), 1)
            nc.scalar.activation(cos, ang, ACT.Sin).then_inc(sig("cos_ready"), 1)
            nc.scalar.activation(sin, turn, ACT.Sin).then_inc(sig("sin_ready"), 1)
            for n in range(3):
                act.wait_ge(sig("proj_done"), n + 1)
                nc.scalar.activation(lat[:, n, :], bank[2 + n % 2][:], ACT.Copy).then_inc(sig("lat_copied"), 1)
                if n == 2:
                    act.wait_ge(sig("lat_summed"), 1)
                nc.scalar.activation(sq[:, n % 2, :], bank[2 + n % 2][:], ACT.Square).then_inc(sig("lat_squared"), 1)
                if n == 0:
                    rsqrt(1, inv, var)
            rsqrt(2, inv, var)
            for g in range(GROUPS):
                act.wait_ge(sig("proj_done"), 6 + g)
                nc.scalar.activation(uT[:, g, :], bank[2 + g % 2][:], ACT.Copy).then_inc(sig("uT_ready"), 1)
            for n in range(4):
                act.wait_ge(sig("k_nope_done"), n + 1)
                nc.scalar.activation(kT[0:64, 2 * n, :], bank[4 + n % 2][0:64, :], ACT.Copy)
                nc.scalar.activation(kT[0:64, 2 * n + 1, :], bank[4 + n % 2][64:128, :], ACT.Copy).then_inc(sig("k_nope_ready"), 1)
            for n in range(4):
                act.wait_ge(sig("q_nope_done"), n + 1)
                nc.scalar.activation(qT[0:64, 2 * n, :], bank[4 + n % 2][0:64, :], ACT.Copy)
                nc.scalar.activation(qT[0:64, 2 * n + 1, :], bank[4 + n % 2][64:128, :], ACT.Copy).then_inc(sig("q_nope_ready"), 1)
            act.wait_ge(sig("k_rope_ready"), 1)
            for h in range(1, H1):
                ins = nc.scalar.activation(kT[64:96, h, :], kT[64:96, 0, :], ACT.Copy)
            ins.then_inc(sig("k_rope_spread"), 1)
            for t in range(T):
                act.wait_ge(sig("v_done"), t + 1)
                nc.scalar.activation(v_sb[:, t, :], bank[2 + t % 2][:], ACT.Copy).then_inc(sig("v_ready"), 1)
            for i in range(N_ATT):
                act.wait_ge(sig("rowmax_ready"), i + 1)
                if i >= 2:
                    act.wait_ge(sig("probs_turned"), i - 1)
                nc.scalar.activation(probs[:, i % 2, 0:keys(i)], bank[i % 2][:, 0:keys(i)], ACT.Exp,
                                     bias=rowmax[:, i:i + 1], scale=SCALE,
                                     accum_out=rowsum[:, i:i + 1]).then_inc(sig("probs_ready"), 1)
                if i == 2:
                    for g in range(GROUPS):
                        act.wait_ge(sig("pool_out"), g + 1)
                        if g >= 2:
                            act.wait_ge(sig("pool_summed"), g - 1)
                        nc.scalar.activation(sq[:, g % 2, :], mixT[:, g, :], ACT.Square).then_inc(sig("pool_squared"), 1)
                    rsqrt(3, inv, var)
            for t in range(T):
                act.wait_ge(sig("y_attn_ready"), t + 1)
                if t >= 2:
                    act.wait_ge(sig("y_squares"), t - 1)
                nc.scalar.activation(sq[:, t % 2, :], y_attn[:, t, :], ACT.Square, accum_out=ss[:, t:t + 1]).then_inc(sig("y_squares"), 1)
            rsqrt(4, ssi, ssv)
            for f in range(0, 4, 2):
                act.wait_ge(sig("mix_turned"), f + 1)
                nc.scalar.activation(mixT[:, 4 + f, :], bank[f % 2][:], ACT.Copy, scale=col(m, "g_out_attn", f)).then_inc(sig("mixT_ready0"), 1)
            for t in range(T):
                act.wait_ge(sig("x1_ready"), 2 * t + 2)
                nc.scalar.activation(h2[:, t, :], x[:, t, :], ACT.Square, accum_out=ss[:, t:t + 1]).then_inc(sig("x1_squares"), 1)
                rsqrt(5 + t, ssi[:, t:t + 1], ssv[:, t:t + 1])
            for k in range(0, KT, 2):
                act.wait_ge(sig("h2T_turned"), k + 1)
                nc.scalar.activation(h2T[:, k, :], bank[k % 2][:], ACT.Copy).then_inc(sig("h2T_ready0"), 1)
            act.wait_ge(sig("best_ready"), 1)
            nc.scalar.activation(m["gates"], m["gates"], ACT.Exp).then_inc(sig("gates_exp"), 1)
            for c in range(2):
                act.wait_ge(sig("gate_summed"), c + 1)
                nc.scalar.activation(mixT[:, c, :], bank[6 + c][:], ACT.Copy).then_inc(sig("gate_copied"), 1)

        @block.tensor
        def _(pe):
            pe.wait_ge(sig("con_loaded"), 16)
            pe.wait_ge(sig("vec_loaded"), 16 * 13)
            nc.tensor.transpose(bank[7][:, 0:NVEC], vec[0:NVEC, :], ident[0:NVEC, 0:NVEC]).then_inc(sig("vec_turned"), 1)
            for k in range(KT):
                if k >= 2:
                    pe.wait_ge(sig(f"hT_ready{k % 2}"), k // 2)
                for t in range(T):
                    if k == 0:
                        pe.wait_ge(sig("xn_ready"), t + 1)
                    ins = nc.tensor.transpose(bank[k % 2][:, t * P:(t + 1) * P], xn[:, t, k * P:(k + 1) * P], ident)
                ins.then_inc(sig("hT_turned"), 1)
            pe.wait_ge(sig("w_in_loaded"), 16 * KT)
            pe.wait_ge(sig("krope_w_ready"), 1)
            pe.wait_ge(sig("hT_ready0"), 4)
            pe.wait_ge(sig("hT_ready1"), 4)

            def project(o, w, c0, n):
                for k in range(KT):
                    ins = nc.tensor.matmul(o, w[:, k, c0:c0 + n], hT[:, k, :], start=(k == 0), stop=(k == KT - 1))
                ins.then_inc(sig("proj_done"), 1)

            def latent_sum(first, last, o):
                for n in range(first, last + 1):
                    pe.wait_ge(sig("lat_squared"), n + 1)
                    ins = nc.tensor.matmul(o, ones, sq[:, n % 2, :], start=(n == first), stop=(n == last))
                ins.then_inc(sig("lat_summed"), 1)

            project(bank[2][:], w_in, D_POOL + QLAT, KVLAT)
            project(bank[3][:], w_in, D_POOL, P)
            latent_sum(0, 0, bank[6][:])
            pe.wait_ge(sig("lat_copied"), 1)
            project(bank[2][:], w_in, D_POOL + P, P)
            project(bank[4][64:96, :], w_in, D_IN1 - ROPE, ROPE)
            project(bank[5][64:96, :], krope_w, 0, ROPE)
            pe.wait_ge(sig("var_ready"), 2)
            latent_sum(1, 2, bank[6][:])
            for g in range(GROUPS):
                if g < 2:
                    pe.wait_ge(sig("lat_squared"), 3 - g)
                else:
                    pe.wait_ge(sig("uT_ready"), g - 1)
                project(bank[2 + g % 2][:], w_in, g * P, P)
            pe.wait_ge(sig("kv_norm"), 1)
            pe.wait_ge(sig("k_rope_read"), 1)
            pe.wait_ge(sig("w_kv_loaded"), 32)
            for n in range(4):
                if n >= 2:
                    pe.wait_ge(sig("k_nope_ready"), n - 1)
                nc.tensor.matmul(bank[4 + n % 2][:], w_k[:, n * P:(n + 1) * P], lat[:, 0, :], start=True, stop=True).then_inc(sig("k_nope_done"), 1)
            pe.wait_ge(sig("q_norm"), 1)
            pe.wait_ge(sig("w_q_loaded"), 64)
            for n in range(4):
                if n < 2:
                    pe.wait_ge(sig("k_nope_ready"), n + 3)
                else:
                    pe.wait_ge(sig("q_nope_ready"), n - 1)
                for k in range(2):
                    ins = nc.tensor.matmul(bank[4 + n % 2][:], w_q[:, k, n * P:(n + 1) * P], lat[:, 1 + k, :], start=(k == 0), stop=(k == 1))
                ins.then_inc(sig("q_nope_done"), 1)
            for t in range(T):
                pe.wait_ge(sig("uT_ready"), 4) if t < 2 else pe.wait_ge(sig("v_ready"), t - 1)
                nc.tensor.matmul(bank[2 + t % 2][:], lat[:, 0, t * P:(t + 1) * P], w_v, start=True, stop=True).then_inc(sig("v_done"), 1)
            pe.wait_ge(sig("w_swap_ready"), 1)
            pe.wait_ge(sig("var_ready"), 3)
            for n in range(2):
                if n == 1:
                    pe.wait_ge(sig("q_rope_read"), 1)
                for k in range(2):
                    nc.tensor.matmul(bank[6][:], w_qr[:, k, n * P:(n + 1) * P], lat[:, 1 + k, :], start=(k == 0), stop=(k == 1))
                for k in range(2):
                    ins = nc.tensor.matmul(bank[7][:], w_swap[:, k, n * P:(n + 1) * P], lat[:, 1 + k, :], start=(k == 0), stop=(k == 1))
                ins.then_inc(sig("q_rope_done"), 1)
            pe.wait_ge(sig("q_rope_ready"), 2)
            pe.wait_ge(sig("q_nope_ready"), 4)
            pe.wait_ge(sig("k_rope_spread"), 1)
            pe.wait_ge(sig("v_ready"), 4)
            pe.wait_ge(sig("con_b_ready"), 1)

            def scores(i):
                q0, h = (i // H1) * P, i % H1
                if i >= 2:
                    pe.wait_ge(sig("probs_ready"), i - 1)
                nc.tensor.matmul(bank[i % 2][:, 0:keys(i)], qT[0:QK, h, q0:q0 + P], kT[0:QK, h, 0:keys(i)], start=True, stop=False, skip_group_check=True)
                nc.tensor.matmul(bank[i % 2][:, q0:q0 + P], ident_b, negmask_b, start=False, stop=True, skip_group_check=True).then_inc(sig("scores_ready"), 1)

            def turn_probs(i):
                pe.wait_ge(sig("probs_ready"), i + 1)
                if i >= 2:
                    pe.wait_ge(sig("probsT_ready"), i - 1)
                for k in range(i // H1 + 1):
                    ins = nc.tensor.transpose(bank[2 + i % 2][:, k * P:(k + 1) * P], probs[:, i % 2, k * P:(k + 1) * P], ident)
                ins.then_inc(sig("probs_turned"), 1)

            def weigh(i):
                t, h = i // H1, i % H1
                pe.wait_ge(sig("probsT_ready"), i + 1)
                if h == 0 and t >= 2:
                    pe.wait_ge(sig("y_attn_ready"), t - 1)
                for k in range(t + 1):
                    ins = nc.tensor.matmul(bank[4 + t % 2][:, h * DV1:(h + 1) * DV1], probsT[:, i % 2, k * P:(k + 1) * P],
                                           v_sb[:, k, h * DV1:(h + 1) * DV1], start=(k == 0), stop=(k == t), skip_group_check=True)
                ins.then_inc(sig("weighed"), 1)

            def pool_out(g):
                pe.wait_ge(sig("pool_diff"), g + 1)
                if g >= 1:
                    pe.wait_ge(sig("pool_out"), g)
                nc.tensor.matmul(bank[6][:], w_pool[:, g, :], pa, start=True, stop=True).then_inc(sig("pool_mixed"), 1)

            pe.wait_ge(sig("w_pool_loaded"), 16)
            for i in range(N_ATT + 2):
                if i < N_ATT:
                    scores(i)
                if i == 2:
                    for g in range(GROUPS):
                        pool_out(g)
                    for g in range(GROUPS):
                        pe.wait_ge(sig("pool_squared"), g + 1)
                        nc.tensor.matmul(bank[7][:], ones, sq[:, g % 2, :], start=(g == 0), stop=(g == GROUPS - 1)).then_inc(sig("pool_summed"), 1)
                if 1 <= i <= N_ATT:
                    turn_probs(i - 1)
                if i >= 2:
                    weigh(i - 2)
            for f in range(4):
                if f == 0:
                    pe.wait_ge(sig("yn_ready"), T)
                if f >= 2:
                    pe.wait_ge(sig(f"mixT_ready{f % 2}"), 1)
                for t in range(T):
                    ins = nc.tensor.transpose(bank[f % 2][:, t * P:(t + 1) * P], y_attn[:, t, f * P:(f + 1) * P], ident)
                ins.then_inc(sig("mix_turned"), 1)
            pe.wait_ge(sig("w_out_loaded"), 16 * KT)
            pe.wait_ge(sig("mixT_pool"), GROUPS)
            for t in range(T):
                for c in range(2):
                    b = bank[2 + (2 * t + c) % 4]
                    if 2 * t + c >= 4:
                        pe.wait_ge(sig("x1_ready"), 2 * t + c - 3)
                    for k in range(KT):
                        if t == 0 and c == 0 and k == 4:
                            pe.wait_ge(sig("mixT_ready0"), 2)
                            pe.wait_ge(sig("mixT_ready1"), 2)
                        ins = nc.tensor.matmul(b[:], mixT[:, k, t * P:(t + 1) * P], w_out[:, k, c * 512:(c + 1) * 512], start=(k == 0), stop=(k == KT - 1))
                    ins.then_inc(sig("out_done"), 1)
            for k in range(KT):
                if k >= 2:
                    pe.wait_ge(sig(f"h2T_ready{k % 2}"), k // 2)
                for t in range(T):
                    if k == 0:
                        pe.wait_ge(sig("h2_ready"), t + 1)
                    ins = nc.tensor.transpose(bank[k % 2][:, t * P:(t + 1) * P], h2[:, t, k * P:(k + 1) * P], ident)
                ins.then_inc(sig("h2T_turned"), 1)
            pe.wait_ge(sig("router_loaded"), 32)
            pe.wait_ge(sig("h2T_ready0"), 4)
            pe.wait_ge(sig("h2T_ready1"), 4)
            for t in range(T):
                for k in range(KT):
                    ins = nc.tensor.matmul(bank[2][:, t * E:(t + 1) * E], h2T[:, k, t * P:(t + 1) * P], w_router[:, k, :], start=(k == 0), stop=(k == KT - 1), skip_group_check=True)
            ins.then_inc(sig("logits_done"), 1)
            pe.wait_ge(sig("ada_added"), KT)
            for n in range(16):
                ins = nc.tensor.matmul(bank[3][:, n:n + 1], acc[:, n * P:(n + 1) * P], ones[:, 0:1], start=True, stop=True, skip_group_check=True)
            ins.then_inc(sig("mod_summed"), 1)
            for c in range(2):
                nc.tensor.matmul(bank[6 + c][:], ones, acc[:, 2 * D + c * 512:2 * D + (c + 1) * 512], start=True, stop=True).then_inc(sig("gate_summed"), 1)
            pe.wait_ge(sig("picked_ready"), 1)
            for t in range(T):
                for u in range(t + 1):
                    nc.tensor.matmul(bank[4][:, t * E:(t + 1) * E], strict_b if u == t else ones_b, picked_b[:, u, :], start=(u == 0), stop=(u == t), skip_group_check=True)
            for u in range(T):
                ins = nc.tensor.matmul(bank[4][:, T * E:(T + 1) * E], ones_b, picked_b[:, u, :], start=(u == 0), stop=(u == T - 1), skip_group_check=True)
            ins.then_inc(sig("ranked"), 1)
            pe.wait_ge(sig("gate_by_expert"), 1)
            for t in range(T):
                ins = nc.tensor.transpose(bank[5][0:E, t * P:(t + 1) * P], total[:, t, :], ident)
            ins.then_inc(sig("gateT_turned"), 1)
            pe.wait_ge(sig("gateT_ready"), 1)
            pe.wait_ge(sig("b_down_loaded"), 16)
            for t in range(T):
                for c in range(2):
                    n = 2 * t + c
                    if n >= 2:
                        pe.wait_ge(sig("bias_added"), n - 1)
                    nc.tensor.matmul(bank[n % 2][:], gateT[:, t, :], b_down[0:E, c * 512:(c + 1) * 512], start=True, stop=True).then_inc(sig("bias_done"), 1)

        @block.vector
        def _(dve):
            chain = Chain(dve, link_v)
            V = nc.vector

            def variance(k, v, s, n):
                V.tensor_scalar(v, s, 1.0 / n, EPS, ALU.mult, ALU.add).then_inc(sig("var_ready"), 1)

            def root(k, y, v, t):
                dve.wait_ge(sig("rsqrt_ready"), k + 1)
                chain.link(newton(nc, chain, y, v, t))

            dve.wait_ge(sig("con_loaded"), 16)
            V.tensor_copy(ident_b, ident)
            V.tensor_copy(ones_b, ones)
            V.tensor_copy(strict_b, con(m, "strict", P))
            V.tensor_copy(negmask_b, con(m, "negmask", P)).then_inc(sig("con_b_ready"), 1)
            dve.wait_ge(sig("vec_turned"), 1)
            V.tensor_copy(m["vecT"][:, 0:NVEC], bank[7][:, 0:NVEC]).then_inc(sig("vecT_ready"), 1)
            dve.wait_ge(sig("x_squares"), T)
            variance(0, ssv, ss, D)
            root(0, ssi, ssv, sst)
            for t in range(T):
                V.tensor_scalar(xn[:, t, :], x[:, t, :], ssi[:, t:t + 1], None, ALU.mult).then_inc(sig("xn_ready"), 1)
            dve.wait_ge(sig("vecT_ready"), 1)
            for k in range(1, KT, 2):
                dve.wait_ge(sig("hT_turned"), k + 1)
                V.tensor_scalar(hT[:, k, :], bank[k % 2][:], col(m, "g_attn", k), None, ALU.mult).then_inc(sig("hT_ready1"), 1)
            dve.wait_ge(sig("c_exp"), 1)
            chain.link(V.tensor_scalar(silu_t, silu_t, 1.0, None, ALU.add))
            chain.link(V.reciprocal(silu_c, silu_t))
            chain.link(V.tensor_tensor(silu_c, silu_c, m["vecT"][:, VEC["c"]:VEC["c"] + 8], ALU.mult))
            dve.wait_ge(sig("pos_loaded"), 16)
            chain.link(V.tensor_copy(tmp, pos_i))
            chain.link(V.tensor_scalar(tmp, tmp, con(m, "freq", 1), None, ALU.mult))
            two_pi = 2.0 * math.pi
            c1 = 6.28125
            c2 = float(np.float32(np.round((two_pi - c1) * 2.0 ** 20) / 2.0 ** 20))
            c3 = float(np.float32(two_pi - c1 - c2))
            big = 1.5 * 2.0 ** 23
            for dst, quarter in ((ang, 0.25), (turn, 0.0)):
                chain.link(V.tensor_scalar(var, tmp, 1.0 / two_pi, quarter, ALU.mult, ALU.add))
                chain.link(V.tensor_scalar(var, var, big, None, ALU.add))
                chain.link(V.tensor_scalar(var, var, big, None, ALU.subtract))
                chain.link(V.scalar_tensor_tensor(out=dst, in0=var, scalar=-c1, in1=tmp, op0=ALU.mult, op1=ALU.add))
                chain.link(V.scalar_tensor_tensor(out=dst, in0=var, scalar=-c2, in1=dst, op0=ALU.mult, op1=ALU.add))
                chain.link(V.scalar_tensor_tensor(out=dst, in0=var, scalar=-c3, in1=dst, op0=ALU.mult, op1=ALU.add))
                chain.link(V.tensor_scalar(dst, dst, quarter * two_pi, math.pi - 1e-6, ALU.add, ALU.min))
                chain.link(V.tensor_scalar(dst, dst, -(math.pi - 1e-6), None, ALU.max))
            dve.sem_inc(sig("angles_ready"), 1)
            dve.wait_ge(sig("lat_summed"), 1)
            variance(1, var, bank[6][:], KVLAT)
            root(1, inv, var, tmp)
            dve.wait_ge(sig("lat_copied"), 1)
            V.scalar_tensor_tensor(out=lat[:, 0, :], in0=lat[:, 0, :], scalar=col(m, "g_kv"), in1=inv, op0=ALU.mult, op1=ALU.mult).then_inc(sig("kv_norm"), 1)
            dve.wait_ge(sig("sin_ready"), 1)
            dve.wait_ge(sig("cos_ready"), 1)
            chain.link(V.tensor_scalar(sin, sin, con(m, "sign", 1), None, ALU.mult))
            dve.wait_ge(sig("proj_done"), 5)
            chain.link(V.tensor_tensor(rope_c[64:96, :], bank[4][64:96, :], cos[64:96, :], ALU.mult))
            V.tensor_tensor(rope_s[64:96, :], bank[5][64:96, :], sin[64:96, :], ALU.mult).then_inc(sig("k_rope_read"), 1)
            dve.wait_ge(sig("kv_norm"), 1)
            dve.wait_ge(sig("lat_summed"), 2)
            variance(2, var, bank[6][:], QLAT)
            root(2, inv, var, tmp)
            dve.wait_ge(sig("lat_copied"), 3)
            for k in range(2):
                ins = V.scalar_tensor_tensor(out=lat[:, 1 + k, :], in0=lat[:, 1 + k, :], scalar=col(m, "g_q", k), in1=inv, op0=ALU.mult, op1=ALU.mult)
            ins.then_inc(sig("q_norm"), 1)
            dve.wait_ge(sig("proj_done"), 9)
            dve.wait_ge(sig("k_rope_read"), 1)
            V.tensor_tensor(kT[64:96, 0, :], rope_c[64:96, :], rope_s[64:96, :], ALU.add).then_inc(sig("k_rope_ready"), 1)
            for n in range(2):
                dve.wait_ge(sig("q_rope_done"), n + 1)
                dve.wait_ge(sig("k_rope_ready"), 1) if n == 0 else dve.wait_ge(sig("q_rope_ready"), 1)
                chain.link(V.tensor_tensor(rope_c, bank[6][:], cos, ALU.mult))
                V.tensor_tensor(rope_s, bank[7][:], sin, ALU.mult).then_inc(sig("q_rope_read"), 1)
                dve.wait_ge(sig("q_rope_read"), n + 1)
                for h in range(4):
                    r = slice(32 * h, 32 * h + 32)
                    ins = V.tensor_tensor(qT[64:96, 4 * n + h, :], rope_c[r, :], rope_s[r, :], ALU.add)
                ins.then_inc(sig("q_rope_ready"), 1)
            for i in range(N_ATT + 2):
                if i < N_ATT:
                    dve.wait_ge(sig("scores_ready"), i + 1)
                    chain.link(V.tensor_reduce(rowmax[:, i:i + 1], bank[i % 2][:, 0:keys(i)], AX, ALU.max))
                    V.tensor_scalar(rowmax[:, i:i + 1], rowmax[:, i:i + 1], -SCALE, None, ALU.mult).then_inc(sig("rowmax_ready"), 1)
                if i == 2:
                    for g in range(GROUPS):
                        dve.wait_ge(sig("pool_mixed"), g + 1)
                        V.tensor_scalar(mixT[:, g, :], bank[6][:], col(m, "b_pool", g), col(m, "pool_scale", g), ALU.add, ALU.mult).then_inc(sig("pool_out"), 1)
                    dve.wait_ge(sig("pool_summed"), GROUPS)
                    variance(3, var, bank[7][:], D_POOL)
                    root(3, inv, var, tmp)
                    for g in range(GROUPS):
                        V.scalar_tensor_tensor(out=mixT[:, g, :], in0=mixT[:, g, :], scalar=col(m, "g_out_pool", g), in1=inv, op0=ALU.mult, op1=ALU.mult).then_inc(sig("mixT_pool"), 1)
                if 1 <= i <= N_ATT:
                    j = i - 1
                    dve.wait_ge(sig("probs_turned"), j + 1)
                    if j >= 2:
                        dve.wait_ge(sig("weighed"), j - 1)
                    V.tensor_copy(probsT[:, j % 2, 0:keys(j)], bank[2 + j % 2][:, 0:keys(j)]).then_inc(sig("probsT_ready"), 1)
                if i >= H1 + 1 and (i - 1) % H1 == 0:
                    t = (i - 1) // H1 - 1
                    dve.wait_ge(sig("weighed"), H1 * (t + 1))
                    chain.link(V.reciprocal(rowinv[:, H1 * t:H1 * (t + 1)], rowsum[:, H1 * t:H1 * (t + 1)]))
                    V.tensor_tensor(y_attn[:, t, :].rearrange("p (h d) -> p h d", h=H1), bank[4 + t % 2][:].rearrange("p (h d) -> p h d", h=H1),
                                    spread(rowinv[:, H1 * t:H1 * (t + 1)], DV1), ALU.mult).then_inc(sig("y_attn_ready"), 1)
            dve.wait_ge(sig("y_squares"), T)
            variance(4, ssv, ss, S)
            root(4, ssi, ssv, sst)
            for t in range(T):
                V.tensor_scalar(y_attn[:, t, :], y_attn[:, t, :], ssi[:, t:t + 1], None, ALU.mult).then_inc(sig("yn_ready"), 1)
            for f in range(1, 4, 2):
                dve.wait_ge(sig("mix_turned"), f + 1)
                V.tensor_scalar(mixT[:, 4 + f, :], bank[f % 2][:], col(m, "g_out_attn", f), None, ALU.mult).then_inc(sig("mixT_ready1"), 1)
            dve.wait_ge(sig("g_ffn_loaded"), 16)
            for t in range(T):
                for c in range(2):
                    n = 2 * t + c
                    dve.wait_ge(sig("out_done"), n + 1)
                    o = x[:, t, c * 512:(c + 1) * 512]
                    V.tensor_tensor(o, bank[2 + n % 4][:], o, ALU.add).then_inc(sig("x1_ready"), 1)
                for k in (2 * t, 2 * t + 1):
                    dve.wait_ge(sig(f"w_ada_loaded{k % 2}"), 16 * (k // 2 + 1))
                    if k == 0:
                        ins = V.tensor_scalar(acc, w_ada[:, 0, :], silu_c[:, 0:1], None, ALU.mult)
                    else:
                        dve.wait_ge(sig("ada_added"), k)
                        ins = V.scalar_tensor_tensor(out=acc, in0=w_ada[:, k % 2, :], scalar=silu_c[:, k:k + 1], in1=acc, op0=ALU.mult, op1=ALU.add)
                    ins.then_inc(sig("ada_added"), 1)
                dve.wait_ge(sig("x1_squares"), t + 1)
                variance(5 + t, ssv[:, t:t + 1], ss[:, t:t + 1], D)
                root(5 + t, ssi[:, t:t + 1], ssv[:, t:t + 1], sst[:, t:t + 1])
                V.scalar_tensor_tensor(out=h2[:, t, :], in0=x[:, t, :], scalar=ssi[:, t:t + 1], in1=g_ffn, op0=ALU.mult, op1=ALU.mult).then_inc(sig("h2_ready"), 1)
            for k in range(1, KT, 2):
                dve.wait_ge(sig("h2T_turned"), k + 1)
                V.tensor_copy(h2T[:, k, :], bank[k % 2][:]).then_inc(sig("h2T_ready1"), 1)
            dve.wait_ge(sig("logits_done"), 1)
            dve.wait_ge(sig("router_loaded"), 32)
            chain.link(V.tensor_tensor(logits, bank[2][:, 0:T * E].rearrange("p (t e) -> p t e", t=T), repeat(b_router, T), ALU.add))
            for t in range(T):
                chain.link(V.max(best[:, t, :], logits[:, t, :]))
                chain.link(V.max_index(place_i[:, t, :], best[:, t, :], logits[:, t, :]))
            V.tensor_tensor(m["gates"], best[:, :, 0:TOPK], spread(best[:, :, 0], TOPK), ALU.subtract).then_inc(sig("best_ready"), 1)
            chain.link(V.tensor_copy(place_k.rearrange("p (t k) -> p t k", t=T), place_i[:, :, 0:TOPK]))
            chain.link(V.tensor_tensor(hot, repeat(con(m, "iota", E), T * TOPK), spread(place_k, E), ALU.is_equal))
            by_expert = hot.rearrange("p (t k) e -> p t e k", t=T)
            chain.link(V.tensor_reduce(picked, by_expert, AX, ALU.add))
            V.tensor_copy(picked_b, picked).then_inc(sig("picked_ready"), 1)
            dve.wait_ge(sig("gates_exp"), 1)
            chain.link(V.tensor_reduce(gsum, m["gates"], AX, ALU.add))
            chain.link(V.reciprocal(ginv, gsum))
            chain.link(V.tensor_tensor(m["gates"], m["gates"], spread(ginv, TOPK), ALU.mult))
            chain.link(V.tensor_tensor(hot2, hot, spread(m["gates"].rearrange("p t k -> p (t k)"), E), ALU.mult))
            V.tensor_reduce(total, hot2.rearrange("p (t k) e -> p t e k", t=T), AX, ALU.add).then_inc(sig("gate_by_expert"), 1)
            dve.wait_ge(sig("ranked"), 1)
            chain.link(V.tensor_copy(ranks, bank[4][:, 0:T * E].rearrange("p (t e) -> p t e", t=T)))
            chain.link(V.tensor_copy(count, bank[4][:, T * E:(T + 1) * E]))
            chain.link(V.memset(m["slot"], -1.0))
            chain.link(V.scalar_tensor_tensor(out=logits, in0=ranks, scalar=1.0, in1=picked, op0=ALU.add, op1=ALU.mult))
            V.tensor_scalar(m["slot"][:, :, 0:E], logits, -1.0, None, ALU.add).then_inc(sig("slot_ready"), 1)
            dve.wait_ge(sig("slot_ready"), 1)
            chain.link(V.tensor_scalar(extra, count, float(P), None, ALU.is_gt))
            chain.link(V.scalar_tensor_tensor(out=extra, in0=count, scalar=2.0 * P, in1=extra, op0=ALU.is_gt, op1=ALU.add))
            chain.link(V.scalar_tensor_tensor(out=extra, in0=count, scalar=3.0 * P, in1=extra, op0=ALU.is_gt, op1=ALU.add))
            chain.link(V.memset(one_e, 1.0))
            chain.link(V.tensor_tensor_scan(upto, one_e, extra, 0.0, ALU.mult, ALU.add))
            chain.link(V.tensor_tensor(base1, upto, extra, ALU.subtract))
            chain.link(V.tensor_scalar(base1, base1, float(P), float(P * (E - 1)), ALU.mult, ALU.add))
            chain.link(V.tensor_tensor(base1, base1, con(m, "base0", E), ALU.subtract))
            chain.link(V.tensor_scalar(logits, ranks, float(P), None, ALU.is_ge))
            chain.link(V.tensor_tensor(logits, logits, repeat(base1, T), ALU.mult))
            chain.link(V.tensor_tensor(logits, logits, ranks, ALU.add))
            chain.link(V.tensor_tensor(logits, logits, repeat(con(m, "base0", E), T), ALU.add))
            for k in range(TOPK):
                hk = hot.rearrange("p (t k) e -> p t k e", t=T)[:, :, k, :]
                h2k = hot2.rearrange("p (t k) e -> p t k e", t=T)[:, :, k, :]
                dve.wait_ge(sig("gate_by_expert"), 1)
                chain.link(V.tensor_tensor(h2k, hk, logits, ALU.mult))
            chain.link(V.tensor_reduce(place_k, hot2, AX, ALU.add))
            chain.link(V.tensor_copy(m["dest"].rearrange("p t k -> p (t k)"), place_k))
            le = hot3[:, 0:MAX_EXTRA, :]
            chain.link(V.tensor_tensor(le, repeat(upto, MAX_EXTRA), spread(con(m, "iota16", MAX_EXTRA), E), ALU.is_le))
            chain.link(V.tensor_reduce(ej, le, AX, ALU.add))
            chain.link(V.tensor_scalar(ej, ej, float(E - 1), None, ALU.min))
            chain.link(V.tensor_copy(m["extra_i"][:, 0:MAX_EXTRA], ej))
            chain.link(V.tensor_tensor(le, le, repeat(extra, MAX_EXTRA), ALU.mult))
            chain.link(V.tensor_reduce(bj, le, AX, ALU.add))
            chain.link(V.tensor_tensor(bj, con(m, "iota16", MAX_EXTRA), bj, ALU.subtract))
            chain.link(V.tensor_scalar(m["extra"][:, 0:MAX_EXTRA], bj, 1.0, float(P), ALU.add, ALU.mult))
            chain.link(V.tensor_copy(m["extra_i"][:, MAX_EXTRA:MAX_EXTRA + 1], upto[:, E - 1:E]))
            dve.wait_ge(sig("gateT_turned"), 1)
            V.tensor_copy(gateT.rearrange("p t n -> p (t n)"), bank[5][0:E, :]).then_inc(sig("gateT_ready"), 1)
            for t in range(T):
                for c in range(2):
                    n = 2 * t + c
                    dve.wait_ge(sig("bias_done"), n + 1)
                    o = x[:, t, c * 512:(c + 1) * 512]
                    V.tensor_tensor(o, bank[n % 2][:], o, ALU.add).then_inc(sig("bias_added"), 1)
            dve.wait_ge(sig("mod_summed"), 1)
            chain.link(V.tensor_tensor(m["mod_shift"], bank[3][:, 0:8], m["vecT"][:, VEC["b_ada"]:VEC["b_ada"] + 8], ALU.add))
            chain.link(V.tensor_tensor(m["mod_scale"], bank[3][:, 8:16], m["vecT"][:, VEC["b_ada"] + 8:VEC["b_ada"] + 16], ALU.add))
            chain.link(V.scalar_tensor_tensor(out=m["mod_scale"], in0=m["mod_scale"], scalar=1.0, in1=m["vecT"][:, VEC["g_pre"]:VEC["g_pre"] + 8], op0=ALU.add, op1=ALU.mult))
            dve.wait_ge(sig("gate_copied"), 2)
            dve.wait_ge(sig("g_post_loaded"), 16)
            gate = mixT[:, 0:2, :].rearrange("p a b -> p (a b)")
            dve.wait_ge(sig("b_ada2_loaded"), 16)
            chain.link(V.tensor_tensor(gate, gate, b_ada_row, ALU.add))
            chain.link(V.tensor_tensor(m["gate_row"], gate, m["gate_row"], ALU.mult))


def spread(ap, n):
    return ap.unsqueeze(len(ap.shape)).broadcast_to(list(ap.shape) + [n])


def repeat(ap, n):
    return ap.unsqueeze(1).broadcast_to([ap.shape[0], n] + list(ap.shape[1:]))


def load_chunk(sp, a, m, e, c, signal="chunk_loaded"):
    dst = m["ring"][0:P, c * 2048:(c + 1) * 2048]
    if c < 8:
        half, k = c // 4, 2 * (c % 4)
        w = a["w_gate_up"][0, e].rearrange("(k p) (g n) -> p k g n", p=P, g=2)
        dst = dst.rearrange("p (k g n) -> p k g n", k=2, g=2)
        for q in range(2):
            sp.dma_start(dst[:, q], w[:, k + q, :, half * 512:(half + 1) * 512]).then_inc(m["sig"](f"{signal}{c}"), 16)
    else:
        k = 2 * (c - 8)
        w = a["w_down"][0, e].rearrange("(k p) n -> p k n", p=P)
        dst = dst.rearrange("p (k n) -> p k n", k=2)
        for q in range(2):
            sp.dma_start(dst[:, q], w[:, k + q, :]).then_inc(m["sig"](f"{signal}{c}"), 16)


def bias_tables(nc, m, keep):
    m["b_gu"] = keep.take(2 * DE, dt=BF16)
    m["pick_row"] = keep.take(E, P, dt=BF16)
    m["b_raw"] = keep.take(2 * DE)
    m["b_rem"] = keep.take(2 * DE)


def expert_places(m, keep):
    f = {}
    f["hot"] = keep.take(T, P, dt=F16)
    f["token"] = keep.take(T, dt=F16)
    f["index"] = keep.take(1, dt=I32)
    f["xg"] = keep.take(D)
    f["xT"] = keep.take(KT, P)
    f["gate"], f["sigm"], f["up"], f["act"] = (keep.take(2, 512) for _ in range(4))
    f["actT"] = keep.take(KT, P)
    f["y"] = keep.take(D)
    return f


def experts(nc, a, m):
    sig, bank, ring = m["sig"], m["bank"], m["ring"]
    keep = Place(m["rest"], m["free"], REST)
    bias_tables(nc, m, keep)
    f = expert_places(m, keep)
    m["f"] = f
    ident, iota = con(m, "ident", P), con(m, "iota", P)
    b_gu, pick_row, b_raw, b_rem = m["b_gu"], m["pick_row"], m["b_raw"], m["b_rem"]
    hot, xg, xT, gate, sigm, up, act_, actT, y = (f[n] for n in ("hot", "xg", "xT", "gate", "sigm", "up", "act", "actT", "y"))

    def chunk(c):
        return ring[:, c * 2048:(c + 1) * 2048]

    with nc.Block() as block:

        @block.sync
        def _(sp):
            for q in range(3):
                sp.dma_start(b_raw[32 * q:32 * q + 32, :], a["b_gate_up"][0]).then_inc(sig("b_raw_loaded"), 16)
            with sp.Fori(1, E) as e:
                for c in range(CHUNKS):
                    sp.wait_ge(sig("chunk_used"), CHUNKS * (e - 1) + c + 1)
                    load_chunk(sp, a, m, e, c)

        @block.gpsimd
        def _(pool):
            for q in range(3):
                r = slice(32 * q, 32 * q + 32)
                src = con(m, "ident", P)[r, 32 * q:32 * q + 32]
                nc.gpsimd.tensor_copy(pick_row[r, :, :], spread(src, P)).then_inc(sig("pick_ready"), 1)
                pool.wait_ge(sig("pick_ready"), q + 1)
            pool.wait_ge(sig("index_ready"), 1)
            gather_rows(pool, m, f).then_inc(sig("rows_loaded"), 16)
            with pool.Fori(0, E + 1) as e:
                pool.wait_ge(sig("index_ready"), e + 2)
                pool.wait_ge(sig("rows_turned"), e + 1)
                pool.sem_inc(sig("gather_begins"), 1)
                gather_rows(pool, m, f).then_inc(sig("rows_loaded"), 16)
            pool.wait_ge(sig("rows_loaded"), 16 * (E + 2))

        @block.scalar
        def _(act):
            act.sem_inc(sig("y_stored"), 16)
            act.sem_inc(sig("y_ready"), 1)

            def copy_rows(n):
                act.wait_ge(sig("rows_half0"), n)
                nc.scalar.activation(xT[:, 0:4, :].rearrange("p k n -> p (k n)"), bank[5][:], ACT.Copy).then_inc(sig("xT_half0"), 1)
                act.wait_ge(sig("rows_turned"), n)
                nc.scalar.activation(xT[:, 4:8, :].rearrange("p k n -> p (k n)"), bank[4][:], ACT.Copy).then_inc(sig("xT_ready"), 1)

            def copy_act(h, n):
                act.wait_ge(sig(f"act_turned{h}"), n)
                nc.scalar.activation(actT[:, 4 * h:4 * h + 4, :].rearrange("p k n -> p (k n)"), bank[4 + h][:], ACT.Copy).then_inc(sig(f"actT_ready{h}"), 1)

            def sigmoid(h, n):
                act.wait_ge(sig(f"gate_ready{h}"), n)
                nc.scalar.activation(sigm[:, h, :], gate[:, h, :], ACT.Sigmoid, scale=ALPHA).then_inc(sig(f"sigm_ready{h}"), 1)

            copy_rows(1)
            with act.Fori(0, E) as e:
                sigmoid(0, e + 1)
                copy_act(0, e + 1)
                sigmoid(1, e + 1)
                copy_rows(e + 2)
                copy_act(1, e + 1)
                act.wait_ge(sig("chunk_used"), CHUNKS * e + CHUNKS)
                act.wait_ge(sig("y_stored"), 16 * e + 16)
                nc.scalar.activation(y[:, 0:512], bank[6][:], ACT.Copy)
                nc.scalar.activation(y[:, 512:D], bank[7][:], ACT.Copy).then_inc(sig("y_ready"), 1)
                act.wait_ge(sig("y_ready"), e + 2)
                act.dma_start(m["y_dram"][bass.ts(e, P), :], y).then_inc(sig("y_stored"), 16)
            act.wait_ge(sig("y_stored"), 16 * (E + 1))

        @block.tensor
        def _(pe):
            def list_rows():
                for t in range(T):
                    ins = nc.tensor.matmul(bank[6][:, 0:1], hot[:, t, :], f["token"][:, t:t + 1], start=(t == 0), stop=(t == T - 1))
                ins.then_inc(sig("index_done"), 1)

            def turn_rows(n):
                pe.wait_ge(sig("rows_loaded"), 16 * n)
                for h in range(2):
                    for k in range(4):
                        ins = nc.tensor.transpose(bank[5 - h][:, k * P:(k + 1) * P], xg[:, (4 * h + k) * P:(4 * h + k + 1) * P], ident)
                    ins.then_inc(sig("rows_half0" if h == 0 else "rows_turned"), 1)

            def turn_act(h, n):
                pe.wait_ge(sig(f"act_ready{h}"), n)
                for k in range(4):
                    ins = nc.tensor.transpose(bank[4 + h][:, k * P:(k + 1) * P], act_[:, h, k * P:(k + 1) * P], ident)
                ins.then_inc(sig(f"act_turned{h}"), 1)

            def gate_up(h, e, c):
                w = chunk(4 * h + c).rearrange("p (k g n) -> p k g n", k=2, g=2)
                pe.wait_ge(sig(f"chunk_loaded{4 * h + c}"), 32 * (e + 1))
                for k in range(2):
                    for g in range(2):
                        ins = nc.tensor.matmul(bank[2 * h + g][:], xT[:, 2 * c + k, :], w[:, k, g, :], start=False, stop=(c == 3 and k == 1), skip_group_check=True)
                ins.then_inc(sig("chunk_used"), 1)

            def biases(h, e):
                for g in range(2):
                    o = g * DE + h * 512
                    nc.tensor.matmul(bank[2 * h + g][:], pick_row[0:96, bass.ds(e, 1), :].rearrange("p a n -> p (a n)"), b_gu[0:96, o:o + 512], start=True, stop=False, skip_group_check=True)

            def down(c, e):
                w = chunk(8 + c).rearrange("p (k n) -> p k n", k=2)
                pe.wait_ge(sig(f"chunk_loaded{8 + c}"), 32 * (e + 1))
                for k in range(2):
                    for n in range(2):
                        ins = nc.tensor.matmul(bank[6 + n][:], actT[:, 2 * c + k, :], w[:, k, n * 512:(n + 1) * 512],
                                               start=(c == 0 and k == 0), stop=(c == 3 and k == 1), skip_group_check=True)
                ins.then_inc(sig("chunk_used"), 1)

            pe.wait_ge(sig("hot_ready"), 1)
            list_rows()
            pe.wait_ge(sig("hot_ready"), 2)
            pe.wait_ge(sig("index_ready"), 1)
            list_rows()
            turn_rows(1)
            pe.wait_ge(sig("b_gu_ready"), 1)
            pe.wait_ge(sig("pick_ready"), 3)
            with pe.Fori(0, E) as e:
                pe.wait_ge(sig("xT_ready"), e + 1)
                pe.wait_ge(sig("gu_free0"), e + 1)
                biases(0, e)
                gate_up(0, e, 0)
                gate_up(0, e, 1)
                pe.wait_ge(sig("hot_ready"), e + 3)
                pe.wait_ge(sig("index_ready"), e + 2)
                pe.wait_ge(sig("y_ready"), e + 1)
                list_rows()
                gate_up(0, e, 2)
                gate_up(0, e, 3)
                pe.wait_ge(sig("gu_free1"), e + 1)
                biases(1, e)
                gate_up(1, e, 0)
                gate_up(1, e, 1)
                turn_act(0, e + 1)
                gate_up(1, e, 2)
                gate_up(1, e, 3)
                pe.wait_ge(sig("actT_ready0"), e + 1)
                turn_rows(e + 2)
                pe.wait_ge(sig("index_ready"), e + 3)
                down(0, e)
                pe.wait_ge(sig("xT_half0"), e + 2)
                turn_act(1, e + 1)
                down(1, e)
                pe.wait_ge(sig("actT_ready1"), e + 1)
                down(2, e)
                down(3, e)

        @block.vector
        def _(dve):
            chain = Chain(dve, sig("B_vector_own"))
            V = nc.vector
            dve.wait_ge(sig("b_raw_loaded"), 48)
            dve.sem_inc(sig("gu_free0"), 1)
            dve.sem_inc(sig("gu_free1"), 1)
            chain.link(V.tensor_copy(f["token"], con(m, "token", T)))

            def list_of(e):
                for t in range(T):
                    ins = V.tensor_scalar(hot[:, t, :], iota, m["slot"][:, t, bass.ds(e, 1)], None, ALU.is_equal)
                ins.then_inc(sig("hot_ready"), 1)

            def index(n):
                dve.wait_ge(sig("index_done"), n)
                V.tensor_copy(f["index"], bank[6][:, 0:1]).then_inc(sig("index_ready"), 1)

            def activate(h, n):
                dve.wait_ge(sig("chunk_used"), n)
                V.tensor_scalar(gate[:, h, :], bank[2 * h][:], LIMIT, None, ALU.min).then_inc(sig(f"gate_ready{h}"), 1)
                V.tensor_scalar(up[:, h, :], bank[2 * h + 1][:], LIMIT, -LIMIT, ALU.min, ALU.max).then_inc(sig(f"gu_free{h}"), 1)

            def finish(h, e):
                dve.wait_ge(sig(f"gu_free{h}"), e + 2)
                gated = sig(f"gated{h}")
                V.scalar_tensor_tensor(out=up[:, h, :], in0=up[:, h, :], scalar=1.0, in1=gate[:, h, :], op0=ALU.add, op1=ALU.mult).then_inc(gated, 1)
                dve.wait_ge(gated, e + 1)
                dve.wait_ge(sig(f"sigm_ready{h}"), e + 1)
                V.tensor_tensor(act_[:, h, :], up[:, h, :], sigm[:, h, :], ALU.mult).then_inc(sig(f"act_ready{h}"), 1)

            list_of(0)
            index(1)
            list_of(1)
            dve.wait_ge(sig("rows_loaded"), 16)
            index(2)
            chain.link(V.tensor_copy(b_gu[0:96, :], b_raw[0:96, :]))
            chain.link(V.tensor_tensor(b_rem[0:96, :], b_raw[0:96, :], b_gu[0:96, :], ALU.subtract))
            chain.link(V.tensor_copy(b_gu[32:64, :], b_rem[32:64, :]))
            chain.link(V.tensor_copy(b_gu[64:96, :], b_rem[64:96, :]))
            chain.link(V.tensor_tensor(b_rem[64:96, :], b_rem[64:96, :], b_gu[64:96, :], ALU.subtract))
            V.tensor_copy(b_gu[64:96, :], b_rem[64:96, :]).then_inc(sig("b_gu_ready"), 1)
            with dve.Fori(0, E) as e:
                dve.wait_ge(sig("index_ready"), e + 2)
                list_of(e + 2)
                dve.wait_ge(sig("rows_loaded"), 16 * e + 32)
                index(e + 3)
                activate(0, CHUNKS * e + 4)
                finish(0, e)
                activate(1, CHUNKS * e + 8)
                finish(1, e)


def gather_rows(pool, m, f):
    return pool.indirect_dma_start(out=f["xg"], out_offset=None, in_=m["h2_dram"],
                                   in_offset=bass.IndirectOffsetOnAxis(ap=f["index"].bitcast(U32), axis=0))


def extra_blocks(eng, m):
    return eng.value_load(m["extra_i"][0:1, MAX_EXTRA:MAX_EXTRA + 1], min_val=0, max_val=MAX_EXTRA)


def extra_experts(nc, a, m):
    sig, bank, ring, f = m["sig"], m["bank"], m["ring"], m["f"]
    ident, iota = con(m, "ident", P), con(m, "iota", P)
    hot, xg, xT, gate, sigm, up, act_, actT, y = (f[n] for n in ("hot", "xg", "xT", "gate", "sigm", "up", "act", "actT", "y"))

    def expert(eng, j):
        return eng.value_load(m["extra_i"][0:1, bass.ds(j, 1)], min_val=0, max_val=E - 1)

    with nc.Block() as block:

        @block.sync
        def _(sp):
            n = extra_blocks(sp, m)
            with sp.If(n > 0):
                for b in range(MAX_EXTRA):
                    sp.dma_start(m["y_dram"][(E + b) * P:(E + b + 1) * P, :], y).then_inc(sig("X_filled"), 16)
                sp.wait_ge(sig("X_filled"), 16 * MAX_EXTRA)
                sp.sem_inc(sig("X_fill_done"), 1)
                with sp.Fori(0, n) as j:
                    sp.wait_ge(sig("X_down_done"), j + 1)
                    e = expert(sp, j)
                    for c in range(CHUNKS):
                        load_chunk(sp, a, m, e, c, "X_chunk_loaded")

        @block.gpsimd
        def _(pool):
            n = extra_blocks(pool, m)
            with pool.If(n > 0):
                with pool.Fori(0, n) as j:
                    pool.wait_ge(sig("X_index_ready"), j + 1)
                    pool.sem_inc(sig("X_gather_begins"), 1)
                    gather_rows(pool, m, f).then_inc(sig("X_rows_loaded"), 16)

        @block.scalar
        def _(act):
            n = extra_blocks(act, m)
            act.sem_inc(sig("X_y_ready"), 1)
            with act.If(n > 0):
                with act.Fori(0, n) as j:
                    for h in range(2):
                        act.wait_ge(sig(f"X_rows_turned{h}"), j + 1)
                        nc.scalar.activation(xT[:, 4 * h:4 * h + 4, :].rearrange("p k n -> p (k n)"), bank[4 + h][:], ACT.Copy).then_inc(sig(f"X_xT_ready{h}"), 1)
                    for h in range(2):
                        act.wait_ge(sig(f"X_gate_ready{h}"), j + 1)
                        nc.scalar.activation(sigm[:, h, :], gate[:, h, :], ACT.Sigmoid, scale=ALPHA).then_inc(sig(f"X_sigm_ready{h}"), 1)
                    for h in range(2):
                        act.wait_ge(sig(f"X_act_turned{h}"), j + 1)
                        nc.scalar.activation(actT[:, 4 * h:4 * h + 4, :].rearrange("p k n -> p (k n)"), bank[4 + h][:], ACT.Copy).then_inc(sig(f"X_actT_ready{h}"), 1)
                    act.wait_ge(sig("X_fill_done"), 1)
                    act.wait_ge(sig("X_down_done"), j + 2)
                    nc.scalar.activation(y[:, 0:512], bank[6][:], ACT.Copy)
                    nc.scalar.activation(y[:, 512:D], bank[7][:], ACT.Copy).then_inc(sig("X_y_ready"), 1)
                    act.wait_ge(sig("X_y_ready"), j + 2)
                    act.dma_start(m["y_dram"][bass.ds((j + E) * P, P), :], y).then_inc(sig("X_y_stored"), 16)
                    act.wait_ge(sig("X_y_stored"), 16 * j + 16)

        @block.tensor
        def _(pe):
            n = extra_blocks(pe, m)
            pe.sem_inc(sig("X_down_done"), 1)
            with pe.If(n > 0):
                with pe.Fori(0, n) as j:
                    e = expert(pe, j)
                    pe.wait_ge(sig("X_hot_ready"), j + 1)
                    pe.wait_ge(sig("X_y_ready"), j + 1)
                    for t in range(T):
                        ins = nc.tensor.matmul(bank[6][:, 0:1], hot[:, t, :], f["token"][:, t:t + 1], start=(t == 0), stop=(t == T - 1))
                    ins.then_inc(sig("X_index_done"), 1)
                    pe.wait_ge(sig("X_rows_loaded"), 16 * j + 16)
                    for h in range(2):
                        for k in range(4):
                            ins = nc.tensor.transpose(bank[4 + h][:, k * P:(k + 1) * P], xg[:, (4 * h + k) * P:(4 * h + k + 1) * P], ident)
                        ins.then_inc(sig(f"X_rows_turned{h}"), 1)
                    for h in range(2):
                        pe.wait_ge(sig(f"X_xT_ready{h}"), j + 1)
                    for h in range(2):
                        for g in range(2):
                            o = g * DE + h * 512
                            nc.tensor.matmul(bank[2 * h + g][:], m["pick_row"][0:96, bass.ds(e, 1), :].rearrange("p a n -> p (a n)"), m["b_gu"][0:96, o:o + 512], start=True, stop=False, skip_group_check=True)
                        for c in range(4):
                            w = ring[:, (4 * h + c) * 2048:(4 * h + c + 1) * 2048].rearrange("p (k g n) -> p k g n", k=2, g=2)
                            pe.wait_ge(sig(f"X_chunk_loaded{4 * h + c}"), 32 * j + 32)
                            for k in range(2):
                                for g in range(2):
                                    ins = nc.tensor.matmul(bank[2 * h + g][:], xT[:, 2 * c + k, :], w[:, k, g, :], start=False, stop=(c == 3 and k == 1), skip_group_check=True)
                        ins.then_inc(sig(f"X_gate_up_done{h}"), 1)
                    for h in range(2):
                        pe.wait_ge(sig(f"X_act_ready{h}"), j + 1)
                        for k in range(4):
                            ins = nc.tensor.transpose(bank[4 + h][:, k * P:(k + 1) * P], act_[:, h, k * P:(k + 1) * P], ident)
                        ins.then_inc(sig(f"X_act_turned{h}"), 1)
                    pe.wait_ge(sig("X_index_ready"), j + 1)
                    for c in range(4):
                        if c % 2 == 0:
                            pe.wait_ge(sig(f"X_actT_ready{c // 2}"), j + 1)
                        w = ring[:, (8 + c) * 2048:(9 + c) * 2048].rearrange("p (k n) -> p k n", k=2)
                        pe.wait_ge(sig(f"X_chunk_loaded{8 + c}"), 32 * j + 32)
                        for k in range(2):
                            for q in range(2):
                                ins = nc.tensor.matmul(bank[6 + q][:], actT[:, 2 * c + k, :], w[:, k, q * 512:(q + 1) * 512],
                                                       start=(c == 0 and k == 0), stop=(c == 3 and k == 1), skip_group_check=True)
                    ins.then_inc(sig("X_down_done"), 1)

        @block.vector
        def _(dve):
            V = nc.vector
            n = extra_blocks(dve, m)
            with dve.If(n > 0):
                with dve.Fori(0, n) as j:
                    e = expert(dve, j)
                    for t in range(T):
                        ins = V.tensor_scalar(hot[:, t, :], iota, m["extra"][:, bass.ds(j, 1)], m["slot"][:, t, bass.ds(e, 1)], ALU.add, ALU.is_equal)
                    ins.then_inc(sig("X_hot_ready"), 1)
                    dve.wait_ge(sig("X_index_done"), j + 1)
                    V.tensor_copy(f["index"], bank[6][:, 0:1]).then_inc(sig("X_index_ready"), 1)
                    for h in range(2):
                        dve.wait_ge(sig(f"X_gate_up_done{h}"), j + 1)
                        V.tensor_scalar(gate[:, h, :], bank[2 * h][:], LIMIT, None, ALU.min).then_inc(sig(f"X_gate_ready{h}"), 1)
                        V.tensor_scalar(up[:, h, :], bank[2 * h + 1][:], LIMIT, -LIMIT, ALU.min, ALU.max).then_inc(sig(f"X_up_ready{h}"), 1)
                        dve.wait_ge(sig(f"X_up_ready{h}"), j + 1)
                        dve.wait_ge(sig(f"X_gate_ready{h}"), j + 1)
                        V.scalar_tensor_tensor(out=up[:, h, :], in0=up[:, h, :], scalar=1.0, in1=gate[:, h, :], op0=ALU.add, op1=ALU.mult).then_inc(sig(f"X_gated{h}"), 1)
                        dve.wait_ge(sig(f"X_gated{h}"), j + 1)
                        dve.wait_ge(sig(f"X_sigm_ready{h}"), j + 1)
                        V.tensor_tensor(act_[:, h, :], up[:, h, :], sigm[:, h, :], ALU.mult).then_inc(sig(f"X_act_ready{h}"), 1)


def second_block(nc, a, m, out):
    sig, bank, ring, rest, x = m["sig"], m["bank"], m["ring"], m["rest"], m["x"]
    ident, ones, upper = con(m, "ident", P), con(m, "ones", P), con(m, "upper", P)
    strict, negmask = con(m, "strict", P), con(m, "negmask", P)

    front = Place(ring, 0, 3 * 4096)
    slots = [front.take(KT, 512) for _ in range(3)]
    front = Place(ring, 0, 3 * 4096)
    LT, AT, kg, qgT, u_sb, wT = (front.take(T, HA, P) for _ in range(6))
    state = LT[:, 0].rearrange("p h n -> p (h n)").rearrange("p (h n) -> p h n", h=HA)
    v_new = LT[:, 1]
    mid = Place(ring, 3 * 4096, 4 * 4096)
    hT = mid.take(KT, S)
    mid = Place(ring, 3 * 4096, 4 * 4096)
    inverse, inverseT = mid.take(T, HA, P), mid.take(T, HA, P)
    mid = Place(ring, 3 * 4096, 4 * 4096)
    mixT = mid.take(KT, S)
    back = Place(ring, 4 * 4096, RING)
    qkvT = back.take(12, S)
    iqT = back.take(4, S)
    back = Place(ring, 4 * 4096 + 12 * S, RING)
    step_L, cross = back.take(2, HA, P), back.take(2, HA, P)
    diff, decay_row = step_L, cross
    back = Place(ring, 4 * 4096, RING)
    w_out = back.take(KT, D)

    keep = Place(rest, m["free"], REST)
    rows = keep.take(4, D)
    w_small = keep.take(KT, 208)
    tables = Place(rest, keep.at - KT * 208, keep.at)
    levels, w_uv = tables.take(8, P), tables.take(HB, P)
    z_a, z_b = keep.take(HA, S), keep.take(HB, S)
    xn = rest[:, keep.at - 4096:keep.at].rearrange("p (t d) -> p t d", t=T)
    over_rows = Place(rest, m["free"], m["free"] + 4 * D)
    q_bT, oT = over_rows.take(HB, S), over_rows.take(HA, S)
    ikT, ckvT, ckv = keep.take(S), keep.take(S), keep.take(T, P)
    score = [None] + [keep.take((t + 1) * P) for t in range(1, T)]
    relu = keep.take(2, S)
    g_final = rest[:, keep.at - D:keep.at]
    taps = keep.take(2, S + 4)
    square = keep.take(2, S)
    var, inv, tmp = keep.take(S), keep.take(S), keep.take(S)
    bias = keep.take(HB, S)
    probsT = keep.take(2, S)
    small = keep.take(T, 16)
    g_kv = keep.take(P)
    beta, g, gc, eg, egl, gl, bg, s1, s2, s3 = (keep.take(T, 4) for _ in range(10))
    a_log, dt_bias = keep.take(4), keep.take(4)
    w_index = keep.take(T, HI)
    ss, ssv, ssi, sst, ss2 = (keep.take(T) for _ in range(5))
    best = keep.take(8)
    rowmax, rowsum, rowinv = (keep.take(16) for _ in range(3))
    bucket_rows = rest[0:BUCKETS, m["free"] + 2048:m["free"] + 2048 + S + P]
    rel_bias = rest[0:BUCKETS, m["free"] + 3072:m["free"] + 3076]
    bias_row = rest[0:HB, m["free"] + 3200:m["free"] + 3200 + S + P]
    bias_sum, logits, probs = relu, taps[:, :, 0:S], square
    GROUPS2 = [(3208, 512), (0, 512), (512, 512), (1024, 512), (2056, 512), (1536, 512), (2696, 512)]
    SCALE_B = P ** -0.5
    N_B = T * HB

    def heads(b):
        return bank[b][:].rearrange("p (h n) -> p h n", h=HA)

    with nc.Block() as block:

        @block.sync
        def _(sp):
            sp.dma_start(w_small[:, :, 0:72], a["w_in_2"][0, :, 3720:3792].rearrange("(k p) n -> p k n", p=P)).then_inc(sig("w_small_loaded"), 16)
            sp.dma_start(w_small[:, :, 72:80], a["w_in_2"][0, :, 2048:2056].rearrange("(k p) n -> p k n", p=P)).then_inc(sig("w_small_loaded"), 16)
            sp.dma_start(w_small[:, :, 80:208], a["w_in_2"][0, :, 2568:2696].rearrange("(k p) n -> p k n", p=P)).then_inc(sig("w_small_loaded"), 16)
            sp.dma_start(g_final, a["g_final"].rearrange("(o n) -> o n", o=1).partition_broadcast(P)).then_inc(sig("g_final_loaded"), 16)
            sp.dma_start(g_kv, a["g_kv_2"].partition_broadcast(P)).then_inc(sig("g_kv_loaded"), 16)
            sp.dma_start(a_log, a["a_log_2"].partition_broadcast(P)).then_inc(sig("decay_loaded"), 16)
            sp.dma_start(dt_bias, a["dt_bias_2"].partition_broadcast(P)).then_inc(sig("decay_loaded"), 16)
            for n, (c0, w) in enumerate(GROUPS2):
                if n >= 3:
                    sp.wait_ge(sig("tile_done"), 4 * (n - 2) + (1 if n > 3 else 0))
                sp.dma_start(slots[n % 3], a["w_in_2"][0, :, c0:c0 + w].rearrange("(k p) n -> p k n", p=P)).then_inc(sig(f"slot_loaded{n % 3}"), 16)
                if n == 2:
                    sp.wait_ge(sig("combined"), 16)
                    sp.dma_start(bucket_rows, a["buckets"]).then_inc(sig("buckets_loaded"), 16)
                    sp.dma_start(rel_bias, a["rel_bias_2"]).then_inc(sig("buckets_loaded"), 16)
                    sp.wait_ge(sig("bias_row_ready"), 1)
                    sp.dma_start(m["bias_dram"], bias_row).then_inc(sig("bias_stored"), 16)
                    sp.wait_ge(sig("bias_stored"), 16)
                    for h in range(HB):
                        src = bass.AP(m["bias_dram"].tensor, h * (S + P), [[1, P], [1, S]])
                        sp.dma_start(bias[:, h, :], src).then_inc(sig("bias_loaded"), 16)
                if n == 3:
                    sp.wait_ge(sig("small_done"), 2)
                    sp.wait_ge(sig("tile_done"), 5)
                    sp.dma_start(levels, a["levels"].rearrange("p (n c) -> p n c", n=8)).then_inc(sig("levels_loaded"), 16)
                    sp.dma_start(w_uv, a["w_uv_2"][0].rearrange("h r d -> r h d")).then_inc(sig("w_uv_loaded"), 16)
            sp.wait_ge(sig("chunks_ready"), T)
            sp.wait_ge(sig("qg_ready"), T)
            sp.wait_ge(sig("kv_turned"), T)
            for k in range(KT):
                if k == 6:
                    sp.wait_ge(sig("inverseT_step"), 7 * T)
                sp.dma_start(w_out[:, k, :], a["w_out_2"][0, k * P:(k + 1) * P, :]).then_inc(sig("w_out_loaded"), 16)
            for t in range(T):
                sp.wait_ge(sig("x_out"), t + 1)
                sp.dma_start(out[0, t * P:(t + 1) * P, :], x[:, t, :]).then_inc(sig("out_stored"), 16)
            sp.wait_ge(sig("out_stored"), 16 * T)

        @block.gpsimd
        def _(pool):
            def gather_results(results):
                for n in range(T * TOPK):
                    if n >= 4:
                        pool.wait_ge(sig("combined"), n - 3)
                    t, k = n // TOPK, n % TOPK
                    pool.indirect_dma_start(out=rows[:, n % 4, :], out_offset=None, in_=results,
                                            in_offset=bass.IndirectOffsetOnAxis(ap=m["dest"][:, t, k:k + 1].bitcast(U32), axis=0)).then_inc(sig(f"row_loaded{n % 4}"), 16)

            with pool.If(extra_blocks(pool, m) > 0):
                gather_results(m["y_dram"])
            with pool.Else():
                gather_results(m["y_dram"][0:E * P, :])
            nc.gpsimd.memset(taps[:, 0, 0:3], 0.0)
            nc.gpsimd.memset(taps[:, 1, 0:3], 0.0).then_inc(sig("taps_zero"), 1)
            for t in range(T):
                pool.wait_ge(sig("decay_ready"), t + 1)
                if t >= 1:
                    pool.wait_ge(sig("chunks_ready"), t)
                d = diff[:, t % 2]
                nc.gpsimd.tensor_tensor(inv.rearrange("p (h n) -> p h n", h=HA), d, repeat(strict, HA), ALU.mult).then_inc(sig("strict_ready"), 1)
                nc.gpsimd.tensor_tensor(tmp.rearrange("p (h n) -> p h n", h=HA), d, repeat(upper, HA), ALU.mult).then_inc(sig("upper_ready"), 1)
            pool.wait_ge(sig("levels_loaded"), 16)
            for n in range(7):
                for t in range(T):
                    i = n * T + t
                    if i == 0:
                        pool.wait_ge(sig("chunks_ready"), T)
                        pool.wait_ge(sig("upper_ready"), T)
                        pool.wait_ge(sig("strict_ready"), T)
                    if i >= 2:
                        pool.wait_ge(sig("cross_done"), i - 1)
                    nc.gpsimd.tensor_tensor(step_L[:, i % 2], LT[:, t], repeat(levels[:, n, :], HA), ALU.mult).then_inc(sig("step_ready"), 1)
            for i in range(N_B):
                t, h = i // HB, i % HB
                n = (t + 1) * P
                if i >= 2:
                    pool.wait_ge(sig("logits_ready"), i - 1)
                else:
                    pool.wait_ge(sig("bias_turned"), HB)
                    pool.wait_ge(sig("chosen"), 3)
                mask = negmask if t == 0 else score[t]
                nc.gpsimd.tensor_tensor(bias_sum[:, i % 2, 0:n], bias[:, h, 3 * P - t * P:3 * P - t * P + n], mask, ALU.add).then_inc(sig("bias_sum_ready"), 1)

        @block.scalar
        def _(act):
            chain = Chain(act, sig("D_scalar_own"))
            A = nc.scalar

            def rsqrt(k, y, v):
                act.wait_ge(sig("var_ready"), k + 1)
                chain.link(A.activation(y, v, ACT.Ln))
                A.activation(y, y, ACT.Exp, scale=-0.5).then_inc(sig("rsqrt_ready"), 1)

            for t in range(T):
                act.wait_ge(sig("combined"), TOPK * (t + 1))
                chain.link(A.activation(xn[:, t, :], x[:, t, :], ACT.Square, accum_out=ss[:, t:t + 1]))
                A.sem_inc(sig("squares0"), 1)
                rsqrt(2 * t, ssi[:, t:t + 1], ssv[:, t:t + 1])
                act.wait_ge(sig("x_normed"), t + 1)
                chain.link(A.activation(xn[:, t, :], x[:, t, :], ACT.Square, accum_out=ss2[:, t:t + 1]))
                A.sem_inc(sig("squares1"), 1)
                rsqrt(2 * t + 1, ssi[:, t:t + 1], ssv[:, t:t + 1])
            for k in range(KT):
                act.wait_ge(sig("hT_turned"), k + 1)
                A.activation(hT[:, k, :], bank[k % 2][:], ACT.Identity, bias=m["mod_shift"][:, k:k + 1], scale=m["mod_scale"][:, k:k + 1]).then_inc(sig("hT_ready"), 1)
            act.wait_ge(sig("bias_row_done"), 1)
            A.activation(bias_row[:, 0:S], bank[7][0:HB, :], ACT.Copy)
            A.activation(bias_row[:, S:S + P], bank[6][0:HB, 0:P], ACT.Copy).then_inc(sig("bias_row_ready"), 1)
            for n in range(5):
                act.wait_ge(sig("tile_done"), n + 1)
                if n < 4:
                    A.activation(iqT[:, n, :], bank[n % 2][:], ACT.Copy).then_inc(sig("tile_read"), 1)
                else:
                    A.activation(ikT[0:64, :], bank[0][0:64, :], ACT.Copy)
                    A.activation(ikT[64:128, :], bank[0][0:64, :], ACT.Copy).then_inc(sig("tile_read"), 1)
            act.wait_ge(sig("small_done"), 2)
            A.activation(small[:, 0:3, :], bank[6][:, 0:432].rearrange("p (t n) -> p t n", t=3)[:, :, 0:16], ACT.Copy)
            chain.link(A.activation(small[:, 3, :], bank[7][:, 0:16], ACT.Copy))
            A.sem_inc(sig("small_ready"), 1)
            for t in range(T):
                src = bank[6 + t // 3][:, (t % 3) * 144 + 16:(t % 3) * 144 + 144]
                ins = A.activation(square[:, 0, t * P:(t + 1) * P], src, ACT.Square, accum_out=ss[:, t:t + 1])
            chain.link(ins)
            A.sem_inc(sig("ckv_squares"), 1)
            rsqrt(8, ssi, ssv)
            act.wait_ge(sig("ab_ready"), 1)
            A.activation(beta, small[:, :, 8:12], ACT.Exp, scale=-1.0).then_inc(sig("b_exp"), 1)
            act.wait_ge(sig("decay_loaded"), 32)
            A.activation(a_log, a_log, ACT.Exp).then_inc(sig("a_exp"), 1)
            A.activation(s2, s2, ACT.Exp, scale=-1.0).then_inc(sig("ab_exp"), 1)
            for i in range(3 * HI):
                t = 1 + i // HI
                n = (t + 1) * P
                if i == 2:
                    act.wait_ge(sig("ckv_turned"), 1)
                    A.activation(ckvT, bank[4][:], ACT.Copy).then_inc(sig("ckvT_ready"), 1)
                act.wait_ge(sig("index_done"), i + 1)
                if i >= 2:
                    act.wait_ge(sig("relu_read"), i - 1)
                if i == 0:
                    act.wait_ge(sig("x_normed"), T)
                A.activation(relu[:, i % 2, 0:n], bank[2 + i % 2][:, 0:n], ACT.Relu).then_inc(sig("relu_ready"), 1)
            act.wait_ge(sig("taps_zero"), 1)

            def tail_of(n):
                act.wait_ge(sig("conv_ready"), n + 1)
                act.wait_ge(sig("relu_read"), 3 * HI)
                A.activation(relu[:, n % 2, :], qkvT[:, n, :], ACT.Sigmoid).then_inc(sig("conv_sigm"), 1)
                if n < 8:
                    act.wait_ge(sig("silu_ready"), n + 1)
                    if n >= 2:
                        act.wait_ge(sig("qk_summed"), n - 1)
                    A.activation(square[:, n % 2, :], qkvT[:, n, :], ACT.Square).then_inc(sig("qk_squared"), 1)

            for n in range(12):
                act.wait_ge(sig("tile_done"), 6 + n)
                if n >= 2:
                    act.wait_ge(sig("conv_ready"), n - 1)
                A.activation(taps[:, n % 2, 3:S + 3], bank[(5 + n) % 2][:], ACT.Copy).then_inc(sig("tile_read"), 1)
                tail_of(n)
                if n >= 1 and n - 1 < 8:
                    rsqrt(9 + n - 1, inv, var)
            for n in range(12):
                i = 17 + n
                act.wait_ge(sig("tile_done"), i + 1)
                dst = (q_bT, z_a, z_b)[n // 4][:, n % 4, :]
                A.activation(dst, bank[i % 2][:], ACT.Copy).then_inc(sig("tile_read"), 1)
                if n >= 4:
                    j = n - 4
                    if j >= 2:
                        act.wait_ge(sig("z_ready"), j - 1)
                    act.wait_ge(sig("tile_read"), i + 1)
                    act.wait_ge(sig("qk_summed"), 8)
                    A.activation(square[:, j % 2, :], dst, ACT.Sigmoid).then_inc(sig("z_sigm"), 1)
            for h in range(HB):
                act.wait_ge(sig("bias_done"), h + 1)
                A.activation(bias[:, h, :], bank[4 + h % 2][:], ACT.Copy).then_inc(sig("bias_turned"), 1)
            for t in range(T):
                act.wait_ge(sig("diff_ready"), t + 1)
                if t >= 2:
                    act.wait_ge(sig("qg_ready"), t - 1)
                A.activation(decay_row[:, t % 2], bank[0 + 4 * (t % 2)][:].rearrange("p (h n) -> p h n", h=HA), ACT.Exp).then_inc(sig("decay_row_ready"), 1)
                A.activation(diff[:, t % 2], diff[:, t % 2], ACT.Exp).then_inc(sig("decay_ready"), 1)
                A.activation(egl[:, t, :], egl[:, t, :], ACT.Exp).then_inc(sig("egl_ready"), 1)
                if t == 0:
                    act.wait_ge(sig("gc_ready"), 1)
                    A.activation(eg, gc, ACT.Exp).then_inc(sig("eg_ready"), 1)
            for i in range(7 * T):
                act.wait_ge(sig("cross_done"), i + 1)
                if i >= 2:
                    act.wait_ge(sig("joined"), i - 1)
                else:
                    act.wait_ge(sig("qg_ready"), T)
                A.activation(cross[:, i % 2], bank[i % 2][:].rearrange("p (h n) -> p h n", h=HA), ACT.Copy).then_inc(sig("cross_ready"), 1)
            for t in range(T):
                act.wait_ge(sig("uw_done"), t + 1)
                A.activation(wT[:, t], bank[2 + t % 2][:].rearrange("p (h n) -> p h n", h=HA), ACT.Copy).then_inc(sig("wT_ready"), 1)
            for i in range(N_B):
                t = i // HB
                n = (t + 1) * P
                act.wait_ge(sig("rowmax_ready"), i + 1)
                if i >= 2:
                    act.wait_ge(sig("probs_turned"), i - 1)
                A.activation(probs[:, i % 2, 0:n], logits[:, i % 2, 0:n], ACT.Exp, bias=rowmax[:, i:i + 1], accum_out=rowsum[:, i:i + 1]).then_inc(sig("probs_exp"), 1)
                if i >= 1:
                    j = i - 1
                    nj = (j // HB + 1) * P
                    act.wait_ge(sig("probs_turned"), j + 1)
                    if j >= 2:
                        act.wait_ge(sig("weighed"), j - 1)
                    A.activation(probsT[:, j % 2, 0:nj], bank[4 + j % 2][:, 0:nj], ACT.Copy).then_inc(sig("probsT_ready"), 1)
            j = N_B - 1
            act.wait_ge(sig("probs_turned"), j + 1)
            act.wait_ge(sig("weighed"), j - 1)
            A.activation(probsT[:, j % 2, 0:S], bank[4 + j % 2][:, 0:S], ACT.Copy).then_inc(sig("probsT_ready"), 1)
            for t in range(T):
                act.wait_ge(sig("o_done"), t + 1)
                A.activation(oT[:, :, t * P:(t + 1) * P], bank[2][:].rearrange("p (h n) -> p h n", h=HA), ACT.Copy).then_inc(sig("oT_ready"), 1)
            act.wait_ge(sig("oT_ready"), T)
            for h in range(HA):
                if h >= 2:
                    act.wait_ge(sig("o_summed"), h - 1)
                A.activation(square[:, h % 2, :], oT[:, h, :], ACT.Square).then_inc(sig("o_squared"), 1)
                rsqrt(17 + h, inv, var)
            for t in range(T):
                for c in range(2):
                    act.wait_ge(sig("mix_done"), 2 * t + c + 1)
                    A.activation(square[:, c, :], bank[2 * (t % 2) + c][:], ACT.Square, accum_out=(ss, ss2)[c][:, t:t + 1]).then_inc(sig("mix_squared"), 1)
                    act.wait_ge(sig("mix_squared"), 2 * t + c + 1)
                rsqrt(21 + t, ssi[:, t:t + 1], ssv[:, t:t + 1])

        @block.tensor
        def _(pe):
            M = nc.tensor
            for k in range(KT):
                if k >= 2:
                    pe.wait_ge(sig("hT_ready"), k - 1)
                for t in range(T):
                    if k == 0:
                        pe.wait_ge(sig("xn_ready"), t + 1)
                    ins = M.transpose(bank[k % 2][:, t * P:(t + 1) * P], xn[:, t, k * P:(k + 1) * P], ident)
                ins.then_inc(sig("hT_turned"), 1)
            pe.wait_ge(sig("buckets_loaded"), 32)
            M.matmul(bank[7][0:HB, :], rel_bias, bucket_rows[:, 0:S], start=True, stop=True)
            M.matmul(bank[6][0:HB, 0:P], rel_bias, bucket_rows[:, S:S + P], start=True, stop=True).then_inc(sig("bias_row_done"), 1)
            pe.wait_ge(sig("hT_ready"), KT)

            def tile(i, w, c0, n):
                if i >= 2:
                    pe.wait_ge(sig("tile_read"), i - 1)
                for k in range(KT):
                    ins = M.matmul(bank[i % 2][0:n, :], w[:, k, c0:c0 + n], hT[:, k, :], start=(k == 0), stop=(k == KT - 1))
                ins.then_inc(sig("tile_done"), 1)

            def group(n, i):
                pe.wait_ge(sig(f"slot_loaded{n % 3}"), 16 * (n // 3 + 1))
                for c in range(4):
                    tile(i + c, slots[n % 3], c * P, P)
                    yield c

            for _ in group(0, 0):
                pass
            pe.wait_ge(sig("w_small_loaded"), 48)
            tile(4, w_small, 0, DI)
            pe.wait_ge(sig("bias_row_ready"), 1)
            for t in range(T):
                o = bank[6 + t // 3][:, (t % 3) * 144:(t % 3) * 144 + 144]
                for k in range(KT):
                    ins = M.matmul(o, hT[:, k, t * P:(t + 1) * P], w_small[:, k, DI:208], start=(k == 0), stop=(k == KT - 1), skip_group_check=True)
                if t >= 2:
                    ins.then_inc(sig("small_done"), 1)
            pe.wait_ge(sig("tile_read"), 5)
            for i in range(3 * HI):
                t, h = 1 + i // HI, i % HI
                r = slice(64 * (h % 2), 64 * (h % 2) + 64)
                if i >= 2:
                    pe.wait_ge(sig("relu_ready"), i - 1)
                if i == 2:
                    pe.wait_ge(sig("ckv_ready"), 1)
                    for q in range(T):
                        ins = M.transpose(bank[4][:, q * P:(q + 1) * P], ckv[:, q, :], ident)
                    ins.then_inc(sig("ckv_turned"), 1)
                M.matmul(bank[2 + i % 2][:, 0:(t + 1) * P], iqT[r, h // 2, t * P:(t + 1) * P], ikT[r, 0:(t + 1) * P], start=True, stop=True).then_inc(sig("index_done"), 1)

            pe.wait_ge(sig("small_ready"), 1)

            def qk_sum(n):
                pe.wait_ge(sig("qk_squared"), n + 1)
                if n >= 1:
                    pe.wait_ge(sig("var_ready"), 9 + n)
                M.matmul(bank[7][:], ones, square[:, n % 2, :], start=True, stop=True).then_inc(sig("qk_summed"), 1)

            for gr in range(3):
                for c in group(1 + gr, 5 + 4 * gr):
                    n = 4 * gr + c
                    if 1 <= n <= 8:
                        qk_sum(n - 1)
            for gr in range(3):
                for c in group(4 + gr, 17 + 4 * gr):
                    pass
            pe.wait_ge(sig("levels_loaded"), 16)
            pe.wait_ge(sig("bias_loaded"), 64)
            pe.wait_ge(sig("ckvT_ready"), 1)
            for h in range(HB):
                if h >= 2:
                    pe.wait_ge(sig("bias_turned"), h - 1)
                M.matmul(bank[4 + h % 2][:], levels[:, 7, :], bias[:, h, :], start=True, stop=True).then_inc(sig("bias_done"), 1)
            pe.wait_ge(sig("g_ready"), 1)
            for t in range(T):
                ins = M.matmul(bank[6][:, 4 * t:4 * t + 4], upper, g[:, t, :], start=True, stop=True, skip_group_check=True)
            ins.then_inc(sig("gc_done"), 1)
            pe.wait_ge(sig("tile_read"), 29)
            pe.wait_ge(sig("qk_normed"), 8)
            pe.wait_ge(sig("relu_ready"), 3 * HI)
            pe.wait_ge(sig("bias_turned"), HB)
            pe.wait_ge(sig("silu_ready"), 12)
            pe.wait_ge(sig("gc_ready"), 1)

            def chunk_products(t):
                b0, b1 = 4 * (t % 2), 4 * (t % 2) + 1
                c = slice(t * P, (t + 1) * P)
                if t >= 1:
                    pe.wait_ge(sig("chunks_ready"), t)
                    pe.wait_ge(sig("kv_chunk_ready"), t)
                if t >= 2:
                    pe.wait_ge(sig("decay_row_ready"), t - 1)
                for h in range(HA):
                    o = slice(h * P, (h + 1) * P)
                    M.matmul(bank[b0][:, o], g[:, t, h:h + 1].broadcast_to([P, P]), upper, start=True, stop=True, skip_group_check=True)
                    ins = M.matmul(bank[b1][:, o], beta[:, t, h:h + 1].broadcast_to([P, P]), ident, start=True, stop=True, skip_group_check=True)
                ins.then_inc(sig("rows_done"), 1)
                for h in range(HA):
                    o = slice(h * P, (h + 1) * P)
                    M.matmul(bank[2][:, o], qkvT[:, 4 + h, c], qkvT[:, 4 + h, c], start=True, stop=True, skip_group_check=True)
                    ins = M.matmul(bank[3][:, o], qkvT[:, 4 + h, c], qkvT[:, h, c], start=True, stop=True, skip_group_check=True)
                ins.then_inc(sig("kk_done"), 1)
                for h in range(HA):
                    o = slice(h * P, (h + 1) * P)
                    M.transpose(bank[6][:, o], qkvT[:, 4 + h, c], ident)
                    ins = M.transpose(bank[7][:, o], qkvT[:, 8 + h, c], ident)
                ins.then_inc(sig("kv_turned"), 1)

            for t in range(T):
                chunk_products(t)
            pe.wait_ge(sig("chunks_ready"), T)
            pe.wait_ge(sig("kv_chunk_ready"), T)
            pe.wait_ge(sig("decay_row_ready"), T)
            for n in range(7):
                for t in range(T):
                    i = n * T + t
                    if i >= 2:
                        pe.wait_ge(sig("cross_ready"), i - 1)
                    pe.wait_ge(sig("step_ready"), i + 1)
                    if n:
                        pe.wait_ge(sig("inverse_step"), i - T + 1)
                    for h in range(HA):
                        ins = M.matmul(bank[i % 2][:, h * P:(h + 1) * P], step_L[:, i % 2, h, :], ident if n == 0 else inverse[:, t, h, :], start=True, stop=True, skip_group_check=True)
                    ins.then_inc(sig("cross_done"), 1)
                    if i >= 1:
                        join(nc, pe, m, i - 1, cross, inverse, inverseT, ident)
            join(nc, pe, m, 7 * T - 1, cross, inverse, inverseT, ident)
            pe.wait_ge(sig("inverseT_step"), 7 * T)
            for t in range(T):
                if t >= 2:
                    pe.wait_ge(sig("u_ready"), t - 1)
                    pe.wait_ge(sig("wT_ready"), t - 1)
                for h in range(HA):
                    o = slice(h * P, (h + 1) * P)
                    M.matmul(bank[t % 2][:, o], inverseT[:, t, h, :], u_sb[:, t, h, :], start=True, stop=True, skip_group_check=True)
                    ins = M.matmul(bank[2 + t % 2][:, o], wT[:, t, h, :], inverseT[:, t, h, :], start=True, stop=True, skip_group_check=True)
                ins.then_inc(sig("uw_done"), 1)
            pe.wait_ge(sig("wT_ready"), T)
            pe.wait_ge(sig("ckvT_ready"), 1)

            def b_logits(i):
                t, h = i // HB, i % HB
                if i >= 2:
                    pe.wait_ge(sig("logits_ready"), i - 1)
                M.matmul(bank[2 + i % 2][:, 0:(t + 1) * P], q_bT[:, h, t * P:(t + 1) * P], ckvT[:, 0:(t + 1) * P], start=True, stop=True).then_inc(sig("b_logits_done"), 1)

            def b_turn(i):
                pe.wait_ge(sig("probs_ready"), i + 1)
                if i >= 2:
                    pe.wait_ge(sig("probsT_ready"), i - 1)
                for k in range(i // HB + 1):
                    ins = M.transpose(bank[4 + i % 2][:, k * P:(k + 1) * P], probs[:, i % 2, k * P:(k + 1) * P], ident)
                ins.then_inc(sig("probs_turned"), 1)

            def b_weigh(i):
                t, h = i // HB, i % HB
                pe.wait_ge(sig("probsT_ready"), i + 1)
                if h == 0 and t >= 2:
                    pe.wait_ge(sig("ob_ready"), t - 1)
                for k in range(t + 1):
                    ins = M.matmul(bank[6 + t % 2][:, h * P:(h + 1) * P], ckv[:, k, :], probsT[:, i % 2, k * P:(k + 1) * P], start=(k == 0), stop=(k == t), skip_group_check=True)
                ins.then_inc(sig("weighed"), 1)

            for i in range(N_B + 2):
                if i < N_B:
                    b_logits(i)
                if 1 <= i <= N_B:
                    b_turn(i - 1)
                if i >= 2:
                    b_weigh(i - 2)
            for t in range(T):
                if t:
                    pe.wait_ge(sig("state_ready"), t)
                    for h in range(HA):
                        ins = M.matmul(bank[0][:, h * P:(h + 1) * P], wT[:, t, h, :], state[:, h, :], start=True, stop=True, skip_group_check=True)
                    ins.then_inc(sig("ws_done"), 1)
                    pe.wait_ge(sig("oT_ready"), t)
                else:
                    pe.wait_ge(sig("logits_ready"), N_B)
                pe.wait_ge(sig("v_new_ready"), t + 1)
                for h in range(HA):
                    o = slice(h * P, (h + 1) * P)
                    if t:
                        M.matmul(bank[2][:, o], state[:, h, :], qgT[:, t, h, :], start=True, stop=False, skip_group_check=True)
                    ins = M.matmul(bank[2][:, o], v_new[:, h, :], AT[:, t, h, :], start=(t == 0), stop=True, skip_group_check=True)
                ins.then_inc(sig("o_done"), 1)
                if t < T - 1:
                    for h in range(HA):
                        ins = M.matmul(bank[1][:, h * P:(h + 1) * P], kg[:, t, h, :], v_new[:, h, :], start=True, stop=True, skip_group_check=True)
                    ins.then_inc(sig("gain_done"), 1)
            pe.wait_ge(sig("w_uv_loaded"), 16)
            pe.wait_ge(sig("ob_ready"), T)
            for h in range(HB):
                if h >= 2:
                    pe.wait_ge(sig("mixT_b"), h - 1)
                else:
                    pe.wait_ge(sig("oT_ready"), T)
                M.matmul(bank[4 + h % 2][:], w_uv[:, h, :], mixT[:, 4 + h, :], start=True, stop=True).then_inc(sig("uv_done"), 1)
            for h in range(HA):
                pe.wait_ge(sig("o_squared"), h + 1)
                if h >= 1:
                    pe.wait_ge(sig("var_ready"), 17 + h)
                M.matmul(bank[7][:], ones, square[:, h % 2, :], start=True, stop=True).then_inc(sig("o_summed"), 1)
            pe.wait_ge(sig("w_out_loaded"), 16 * KT)
            pe.wait_ge(sig("mixT_b"), HB)
            pe.wait_ge(sig("mixT_a"), HA)
            for t in range(T):
                if t >= 2:
                    pe.wait_ge(sig("x_out"), t - 1)
                for c in range(2):
                    for k in range(KT):
                        ins = M.matmul(bank[2 * (t % 2) + c][:], mixT[:, k, t * P:(t + 1) * P], w_out[:, k, c * 512:(c + 1) * 512], start=(k == 0), stop=(k == KT - 1))
                    ins.then_inc(sig("mix_done"), 1)

        @block.vector
        def _(dve):
            chain = Chain(dve, sig("D_vector_own"))
            V = nc.vector

            def variance(v, s, scale):
                V.tensor_scalar(v, s, scale, EPS, ALU.mult, ALU.add).then_inc(sig("var_ready"), 1)

            def root(k, y, v, t):
                dve.wait_ge(sig("rsqrt_ready"), k + 1)
                chain.link(newton(nc, chain, y, v, t))

            dve.wait_ge(sig("g_final_loaded"), 16)
            for t in range(T):
                for k in range(TOPK):
                    n = t * TOPK + k
                    dve.wait_ge(sig(f"row_loaded{n % 4}"), 16 * (n // 4 + 1))
                    if k:
                        dve.wait_ge(sig("combined"), n)
                    V.scalar_tensor_tensor(out=x[:, t, :], in0=rows[:, n % 4, :], scalar=m["gates"][:, t, k:k + 1], in1=x[:, t, :], op0=ALU.mult, op1=ALU.add).then_inc(sig("combined"), 1)
                c = slice(t, t + 1)
                dve.wait_ge(sig("squares0"), t + 1)
                variance(ssv[:, c], ss[:, c], 1.0 / D)
                root(2 * t, ssi[:, c], ssv[:, c], sst[:, c])
                V.scalar_tensor_tensor(out=x[:, t, :], in0=x[:, t, :], scalar=ssi[:, c], in1=g_final, op0=ALU.mult, op1=ALU.mult).then_inc(sig("x_normed"), 1)
                dve.wait_ge(sig("squares1"), t + 1)
                dve.wait_ge(sig("x_normed"), t + 1)
                variance(ssv[:, c], ss2[:, c], 1.0 / D)
                root(2 * t + 1, ssi[:, c], ssv[:, c], sst[:, c])
                V.tensor_scalar(xn[:, t, :], x[:, t, :], ssi[:, c], None, ALU.mult).then_inc(sig("xn_ready"), 1)
            dve.wait_ge(sig("ckv_squares"), 1)
            variance(ssv, ss, 1.0 / P)
            root(8, ssi, ssv, sst)
            dve.wait_ge(sig("g_kv_loaded"), 16)
            for t in range(T):
                src = bank[6 + t // 3][:, (t % 3) * 144 + 16:(t % 3) * 144 + 144]
                ins = V.scalar_tensor_tensor(out=ckv[:, t, :], in0=src, scalar=ssi[:, t:t + 1], in1=g_kv, op0=ALU.mult, op1=ALU.mult)
            ins.then_inc(sig("ckv_ready"), 1)
            dve.wait_ge(sig("small_ready"), 1)
            chain.link(V.tensor_scalar(w_index, small[:, :, 0:HI], HI ** -0.5 * DI ** -0.5, None, ALU.mult))
            dve.wait_ge(sig("decay_loaded"), 32)
            chain.link(V.tensor_tensor(s1, small[:, :, 12:16], repeat(dt_bias, T), ALU.add))
            chain.link(V.tensor_scalar(s3, s1, -1.0, None, ALU.mult))
            chain.link(V.tensor_tensor(s2, s1, s3, ALU.max))
            V.tensor_scalar(s1, s1, 0.0, None, ALU.max).then_inc(sig("ab_ready"), 1)
            dve.wait_ge(sig("b_exp"), 1)
            chain.link(V.tensor_scalar(beta, beta, 1.0, None, ALU.add))
            chain.link(V.reciprocal(beta, beta))
            dve.wait_ge(sig("ab_ready"), 1)
            dve.wait_ge(sig("ab_exp"), 1)
            dve.wait_ge(sig("a_exp"), 1)
            chain.link(V.tensor_scalar(s3, s2, 2.0, None, ALU.add))
            chain.link(V.reciprocal(s3, s3))
            chain.link(V.tensor_tensor(s2, s2, s3, ALU.mult))
            chain.link(V.tensor_tensor(s3, s2, s2, ALU.mult))
            chain.link(V.tensor_scalar(g, s3, 2.0 / 17.0, 2.0 / 15.0, ALU.mult, ALU.add))
            for n in (13, 11, 9, 7, 5, 3, 1):
                chain.link(V.tensor_tensor(g, g, s3, ALU.mult))
                chain.link(V.tensor_scalar(g, g, 2.0 / n, None, ALU.add))
            chain.link(V.tensor_tensor(g, g, s2, ALU.mult))
            chain.link(V.tensor_tensor(g, g, s1, ALU.add))
            chain.link(V.tensor_tensor(g, g, repeat(a_log, T), ALU.mult))
            V.tensor_scalar(g, g, -1.0, None, ALU.mult).then_inc(sig("g_ready"), 1)
            for i in range(3 * HI):
                t, h = 1 + i // HI, i % HI
                n = (t + 1) * P
                dve.wait_ge(sig("relu_ready"), i + 1)
                if h == 0:
                    V.tensor_scalar(score[t], relu[:, i % 2, 0:n], w_index[:, t, 0:1], None, ALU.mult).then_inc(sig("relu_read"), 1)
                else:
                    dve.wait_ge(sig("relu_read"), i)
                    V.scalar_tensor_tensor(out=score[t], in0=relu[:, i % 2, 0:n], scalar=w_index[:, t, h:h + 1], in1=score[t], op0=ALU.mult, op1=ALU.add).then_inc(sig("relu_read"), 1)
                if h == HI - 1:
                    dve.wait_ge(sig("relu_read"), i + 1)
                    chain.link(V.tensor_tensor(score[t][:, t * P:n], score[t][:, t * P:n], negmask, ALU.add))

            GONE = -3.0e38

            def choose(i):
                t, r = 1 + i // 16, i % 16
                chain.link(V.max(best, score[t]))
                chain.link(V.match_replace(score[t], best, score[t], GONE))
                if r == 15:
                    V.tensor_scalar(score[t], score[t], -2.0e38, NEG, ALU.is_gt, ALU.mult).then_inc(sig("chosen"), 1)

            rounds = iter(range(48))

            def l2(n):
                dve.wait_ge(sig("qk_summed"), n + 1)
                variance(var, bank[7][:], 1.0)

            def l2_end(n):
                root(9 + n, inv, var, tmp)
                dve.wait_ge(sig("qk_squared"), n + 1)
                V.scalar_tensor_tensor(out=qkvT[:, n, :], in0=qkvT[:, n, :], scalar=(P ** -0.5 if n < 4 else 1.0), in1=inv, op0=ALU.mult, op1=ALU.mult).then_inc(sig("qk_normed"), 1)

            for n in range(12):
                dve.wait_ge(sig("tile_read"), 6 + n)
                dve.wait_ge(sig("taps_zero"), 1)
                w = [col(m, "conv", 12 * j + n) for j in range(CONV)]
                chain.link(V.tensor_scalar(qkvT[:, n, :], taps[:, n % 2, 0:S], w[0], None, ALU.mult))
                for j in range(1, CONV):
                    ins = V.scalar_tensor_tensor(out=qkvT[:, n, :], in0=taps[:, n % 2, j:j + S], scalar=w[j], in1=qkvT[:, n, :], op0=ALU.mult, op1=ALU.add)
                    if j < CONV - 1:
                        chain.link(ins)
                ins.then_inc(sig("conv_ready"), 1)
                choose(next(rounds))
                dve.wait_ge(sig("conv_sigm"), n + 1)
                V.tensor_tensor(qkvT[:, n, :], qkvT[:, n, :], relu[:, n % 2, :], ALU.mult).then_inc(sig("silu_ready"), 1)
                if 1 <= n <= 8:
                    l2(n - 1)
                choose(next(rounds))
                if 1 <= n <= 8:
                    l2_end(n - 1)
            for n in range(8):
                dst = (z_a, z_b)[n // 4][:, n % 4, :]
                for _ in range(3):
                    choose(next(rounds))
                dve.wait_ge(sig("z_sigm"), n + 1)
                V.tensor_tensor(dst, dst, square[:, n % 2, :], ALU.mult).then_inc(sig("z_ready"), 1)
            dve.wait_ge(sig("gc_done"), 1)
            V.tensor_copy(gc, bank[6][:, 0:16].rearrange("p (t h) -> p t h", t=T)).then_inc(sig("gc_ready"), 1)
            dve.wait_ge(sig("gc_ready"), 1)
            for t in range(T):
                b0, b1 = 4 * (t % 2), 4 * (t % 2) + 1
                dve.wait_ge(sig("rows_done"), t + 1)
                if t >= 2:
                    dve.wait_ge(sig("strict_ready"), t - 1)
                    dve.wait_ge(sig("upper_ready"), t - 1)
                last = bank[b0][:].rearrange("p (h n) -> p h n", h=HA)[:, :, P - 1]
                V.tensor_tensor(egl[:, t, :], last, gc[:, t, :], ALU.subtract)
                for h in range(HA):
                    ins = V.tensor_scalar(diff[:, t % 2, h, :], bank[b0][:, h * P:(h + 1) * P], gc[:, t, h:h + 1], 0.0, ALU.subtract, ALU.min)
                ins.then_inc(sig("diff_ready"), 1)
                if t == 0:
                    dve.wait_ge(sig("eg_ready"), 1)
                    chain.link(V.tensor_tensor(bg, beta, eg, ALU.mult))
                dve.wait_ge(sig("kk_done"), t + 1)
                dve.wait_ge(sig("strict_ready"), t + 1)
                chain.link(V.tensor_tensor(LT[:, t], heads(2), inv.rearrange("p (h n) -> p h n", h=HA), ALU.mult))
                chain.link(V.tensor_tensor(LT[:, t], LT[:, t], heads(b1), ALU.mult))
                dve.wait_ge(sig("upper_ready"), t + 1)
                V.tensor_tensor(AT[:, t], heads(3), tmp.rearrange("p (h n) -> p h n", h=HA), ALU.mult).then_inc(sig("chunks_ready"), 1)
                dve.wait_ge(sig("decay_row_ready"), t + 1)
                V.tensor_copy(gl[:, t, :], decay_row[:, t % 2, :, P - 1])
                V.tensor_tensor(qgT[:, t], qkvT[:, 0:4, t * P:(t + 1) * P], decay_row[:, t % 2], ALU.mult).then_inc(sig("qg_ready"), 1)
                dve.wait_ge(sig("kv_turned"), t + 1)
                dve.wait_ge(sig("egl_ready"), t + 1)
                V.tensor_tensor(kg[:, t], heads(6), spread(egl[:, t, :], P), ALU.mult)
                V.tensor_tensor(u_sb[:, t], heads(7), spread(beta[:, t, :], P), ALU.mult)
                V.tensor_tensor(wT[:, t], heads(6), spread(bg[:, t, :], P), ALU.mult).then_inc(sig("kv_chunk_ready"), 1)
            for i in range(7 * T):
                n, t = i // T, i % T
                one = repeat(ident, HA)
                dve.wait_ge(sig("joined"), i + 1)
                prev = one if n == 0 else inverse[:, t]
                prevT = one if n == 0 else inverseT[:, t]
                if n:
                    dve.wait_ge(sig("inverse_step"), i - T + 1)
                    dve.wait_ge(sig("inverseT_step"), i - T + 1)
                if n < 6:
                    V.tensor_tensor(inverse[:, t], prev, heads(2 + i % 2), ALU.subtract).then_inc(sig("inverse_step"), 1)
                V.tensor_tensor(inverseT[:, t], prevT, heads(4 + i % 2), ALU.subtract).then_inc(sig("inverseT_step"), 1)
            for t in range(T):
                dve.wait_ge(sig("uw_done"), t + 1)
                V.tensor_copy(u_sb[:, t], heads(t % 2)).then_inc(sig("u_ready"), 1)
            for i in range(N_B + 3):
                if i < N_B:
                    t = i // HB
                    n = (t + 1) * P
                    dve.wait_ge(sig("b_logits_done"), i + 1)
                    dve.wait_ge(sig("bias_sum_ready"), i + 1)
                    if i >= 2:
                        dve.wait_ge(sig("probs_exp"), i - 1)
                    V.scalar_tensor_tensor(out=logits[:, i % 2, 0:n], in0=bank[2 + i % 2][:, 0:n], scalar=SCALE_B, in1=bias_sum[:, i % 2, 0:n], op0=ALU.mult, op1=ALU.add).then_inc(sig("logits_ready"), 1)
                    dve.wait_ge(sig("logits_ready"), i + 1)
                    chain.link(V.tensor_reduce(rowmax[:, i:i + 1], logits[:, i % 2, 0:n], AX, ALU.max))
                    V.tensor_scalar(rowmax[:, i:i + 1], rowmax[:, i:i + 1], -1.0, None, ALU.mult).then_inc(sig("rowmax_ready"), 1)
                if 1 <= i <= N_B:
                    j = i - 1
                    nj = (j // HB + 1) * P
                    dve.wait_ge(sig("probs_exp"), j + 1)
                    chain.link(V.reciprocal(rowinv[:, j:j + 1], rowsum[:, j:j + 1]))
                    V.tensor_scalar(probs[:, j % 2, 0:nj], probs[:, j % 2, 0:nj], rowinv[:, j:j + 1], None, ALU.mult).then_inc(sig("probs_ready"), 1)
                if i >= HB + 2 and (i - 2) % HB == 0:
                    t = (i - 2) // HB - 1
                    dve.wait_ge(sig("weighed"), HB * (t + 1))
                    V.tensor_copy(mixT[:, 4:8, t * P:(t + 1) * P], heads(6 + t % 2)).then_inc(sig("ob_ready"), 1)
            for t in range(T):
                dve.wait_ge(sig("u_ready"), T)
                if t == 0:
                    V.tensor_copy(v_new, u_sb[:, 0]).then_inc(sig("v_new_ready"), 1)
                else:
                    dve.wait_ge(sig("ws_done"), t)
                    V.tensor_tensor(v_new, u_sb[:, t], heads(0), ALU.subtract).then_inc(sig("v_new_ready"), 1)
                if t < T - 1:
                    dve.wait_ge(sig("gain_done"), t + 1)
                    if t == 0:
                        ins = V.tensor_copy(state, heads(1))
                    else:
                        dve.wait_ge(sig("state_ready"), t)
                        for h in range(HA):
                            ins = V.scalar_tensor_tensor(out=state[:, h, :], in0=state[:, h, :], scalar=gl[:, t, h:h + 1], in1=bank[1][:, h * P:(h + 1) * P], op0=ALU.mult, op1=ALU.add)
                    ins.then_inc(sig("state_ready"), 1)
            for h in range(HB):
                dve.wait_ge(sig("uv_done"), h + 1)
                V.tensor_tensor(mixT[:, 4 + h, :], bank[4 + h % 2][:], z_b[:, h, :], ALU.mult).then_inc(sig("mixT_b"), 1)
            for h in range(HA):
                dve.wait_ge(sig("o_summed"), h + 1)
                variance(var, bank[7][:], 1.0 / P)
                root(17 + h, inv, var, tmp)
                chain.link(V.scalar_tensor_tensor(out=mixT[:, h, :], in0=oT[:, h, :], scalar=col(m, "g_gdn"), in1=inv, op0=ALU.mult, op1=ALU.mult))
                V.tensor_tensor(mixT[:, h, :], mixT[:, h, :], z_a[:, h, :], ALU.mult).then_inc(sig("mixT_a"), 1)
            for t in range(T):
                c1 = slice(t, t + 1)
                dve.wait_ge(sig("mix_squared"), 2 * t + 2)
                chain.link(V.tensor_tensor(ss[:, c1], ss[:, c1], ss2[:, c1], ALU.add))
                variance(ssv[:, c1], ss[:, c1], 1.0 / D)
                root(21 + t, ssi[:, c1], ssv[:, c1], sst[:, c1])
                for c in range(2):
                    o = slice(c * 512, (c + 1) * 512)
                    part = (inv, tmp)[c]
                    if t:
                        dve.wait_ge(sig("x_out"), t)
                    chain.link(V.scalar_tensor_tensor(out=part, in0=bank[2 * (t % 2) + c][:], scalar=ssi[:, c1], in1=m["gate_row"][:, o], op0=ALU.mult, op1=ALU.mult))
                    ins = V.tensor_tensor(x[:, t, o], x[:, t, o], part, ALU.add)
                ins.then_inc(sig("x_out"), 1)


def join(nc, pe, m, i, cross, inverse, inverseT, ident):
    sig, bank = m["sig"], m["bank"]
    n, t = i // T, i % T
    pe.wait_ge(sig("cross_ready"), i + 1)
    if i >= 2:
        pe.wait_ge(sig("inverseT_step"), i - 1)
    for h in range(HA):
        o = slice(h * P, (h + 1) * P)
        turned = ident if n == 0 else inverseT[:, t, h, :]
        if n < 6:
            nc.tensor.matmul(bank[2 + i % 2][:, o], turned, cross[:, i % 2, h, :], start=True, stop=True, skip_group_check=True)
        ins = nc.tensor.matmul(bank[4 + i % 2][:, o], cross[:, i % 2, h, :], turned, start=True, stop=True, skip_group_check=True)
    ins.then_inc(sig("joined"), 1)


INPUTS = ["x", "positions", "g_attn_norm", "w_in", "w_pool", "b_pool", "pool_scale", "g_q_a", "w_q_b", "g_kv_a",
          "w_kv_b", "g_out_pool", "g_out_attn", "w_out", "g_ffn_norm", "w_router", "b_router", "w_gate_up",
          "b_gate_up", "w_down", "b_down", "g_final", "c_2", "w_ada_2", "b_ada_2", "g_pre_2", "w_in_2",
          "conv_w_2", "a_log_2", "dt_bias_2", "g_gdn_2", "g_kv_2", "w_uv_2", "rel_bias_2", "w_out_2", "g_post_2"]


def kernel(**inputs):
    import numpy as _np
    import concourse.bacc as _bacc
    from concourse import mybir as _mybir
    from concourse.bass_utils import run_bass_kernel_spmd as _run

    nc = _bacc.Bacc("TRN2", target_bir_lowering=False, num_devices=1)
    arrays, aps = {}, {}
    table, levels, onehot = constants()
    for name, value in [(n, inputs[n]) for n in INPUTS] + [("constants", table), ("levels", levels), ("buckets", onehot)]:
        v = _np.ascontiguousarray(value)
        arrays[f"in_{name}"] = v
        aps[name] = nc.dram_tensor(f"in_{name}", v.shape, _mybir.dt.from_np(v.dtype), kind="ExternalInput").ap()
    out = nc.dram_tensor("out_x", (1, S, D), F32, kind="ExternalOutput").ap()
    build(nc, aps, out)
    return _run(nc, [arrays], core_ids=[0]).results[0]["out_x"]
```

```python
import math
from contextlib import ExitStack

import numpy as np
import concourse.bass as bass
from concourse import mybir

P = 128
F32, BF16, F16 = mybir.dt.float32, mybir.dt.bfloat16, mybir.dt.float16
F32R = mybir.dt.float32r
I32, U32 = mybir.dt.int32, mybir.dt.uint32
ALU = mybir.AluOpType
ACT = mybir.ActivationFunctionType
AX = mybir.AxisListType.X

S, D = 512, 1024
T, KT = S // P, D // P
EPS = 1e-6
NEG = -1.0e30
D_POOL, GROUPS = 512, 4
H1, NOPE, ROPE, DV1 = 8, 64, 32, 64
QK = NOPE + ROPE
QLAT, KVLAT = 256, 128
D_IN1 = D_POOL + QLAT + KVLAT + ROPE
E, TOPK, DE = 32, 4, 1024
ALPHA, LIMIT = 1.702, 7.0
MAX_EXTRA = 16
BLOCKS = E + MAX_EXTRA
CHUNKS = 12
RAW, PARTS = 4, 6
EARLY = 4
POOL_CHUNKS = (9, 11)
HA, HB, HI, DI = 4, 4, 8, 64
D_IN2 = 3792
CONV = 4
KEEP = 128
BUCKETS = 32
GROUPS2 = (3208, 0, 512, 1024, 2056, 1536, 2696)

VEC = {}
_at = 0
for _name, _n in (("g_attn", 8), ("b_pool", 4), ("pool_scale", 4), ("g_q", 2), ("g_kv", 1),
                  ("g_out_pool", 4), ("g_out_attn", 4), ("c", 8), ("g_pre", 8), ("b_ada", 16),
                  ("g_gdn", 1), ("g_kv2", 1), ("conv", 48)):
    VEC[_name] = _at
    _at += _n
NVEC = _at

CON = {}
_at = 0
for _name, _n in (("ident", P), ("ones", P), ("upper", P), ("strict", P), ("negmask", P), ("iota", P),
                  ("token", T), ("freq", 1), ("phase", 1), ("sign", 1), ("base0", E), ("iota16", MAX_EXTRA),
                  ("poolinv", 4 * 16)):
    CON[_name] = _at
    _at += _n
NCON = _at


def constants():
    c = np.zeros((P, NCON), np.float32)
    p = np.arange(P)
    part, free = p[:, None], p[None, :]

    def put(name, value, n):
        c[:, CON[name]:CON[name] + n] = value

    put("ident", part == free, P)
    put("ones", 1.0, P)
    put("upper", part <= free, P)
    put("strict", part < free, P)
    put("negmask", np.where(free <= part, 0.0, NEG), P)
    put("iota", free, P)
    put("token", part + P * np.arange(T)[None, :], T)
    half = ROPE // 2
    freq = (np.float32(10000.0) ** (-np.arange(half, dtype=np.float32) / np.float32(half))).astype(np.float32)
    put("freq", freq[p % half][:, None], 1)
    put("sign", np.where(p % ROPE < half, -1.0, 1.0)[:, None], 1)
    put("base0", P * np.arange(E)[None, :], E)
    put("iota16", np.arange(MAX_EXTRA)[None, :], MAX_EXTRA)
    t = np.arange(16)
    put("poolinv", np.concatenate([1.0 / np.minimum(t + 1, w) for w in (2, 4, 8, 16)])[None, :], 64)
    levels = np.zeros((P, 8 * P), np.float32)
    levels[:, 7 * P:] = part + free == P - 1
    for n in range(7):
        b = 1 << n
        same = part // (2 * b) == free // (2 * b)
        put_at = same & (part % (2 * b) < b) & (free % (2 * b) >= b)
        levels[:, n * P:(n + 1) * P] = put_at
    dist = (S - 1) - np.arange(S + P)
    n = np.maximum(dist, 0)
    nf = np.maximum(n, 1).astype(np.float32)
    large = 16 + (np.log(nf / np.float32(16)) / np.float32(math.log(8.0)) * np.float32(16)).astype(np.int32)
    bucket = np.where(n < 16, n, np.minimum(large, BUCKETS - 1))
    onehot = (bucket[None, :] == np.arange(BUCKETS)[:, None]).astype(np.float32)
    return c, levels, onehot


class Place:

    def __init__(self, base, at, end):
        self.base, self.at, self.end = base, at, end

    def align(self):
        self.at += -self.at % 8
        return self.at

    def take(self, *shape, dt=F32, parts=P):
        n = int(np.prod(shape))
        words = n if dt not in (BF16, F16) else (n + 1) // 2
        assert self.at + words <= self.end, (self.at, words, self.end)
        ap = self.base[0:parts, self.at:self.at + words]
        self.at += words
        if dt != F32:
            ap = ap.bitcast(dt)
        if len(shape) == 2:
            ap = ap.rearrange("p (a b) -> p a b", a=shape[0])
        if len(shape) == 3:
            ap = ap.rearrange("p (a b c) -> p a b c", a=shape[0], b=shape[1])
        return ap


RING = CHUNKS * 2048
REST = 28632
PARTS_AT = REST - 2 * (PARTS - EARLY) * 2048


def build(nc, a, out):
    with ExitStack() as ctx:
        sems, stages = {}, []

        def sig(name):
            if name not in sems:
                sems[name] = nc.alloc_semaphore(f"{name}_{len(stages)}")
            return sems[name]

        def retire(kept=""):
            done = [n for n in sems if not (kept and n.startswith(kept))]
            nc.clear_and_free_semaphores([sems.pop(n) for n in done])
            nc.all_engine_barrier()
            stages.append(len(done))

        ring = ctx.enter_context(nc.sbuf_tensor("ring", [P, RING], F32))
        rest = ctx.enter_context(nc.sbuf_tensor("rest", [P, REST], F32))
        base = {"ring": nc.sbuf_base - 4 * (RING + REST), "rest": nc.sbuf_base - 4 * REST}

        def rounded(name, where, at, n):
            return nc.alloc_sbuf_tensor_at(name, [P, n], F32R, offset=base[where] + 4 * at)[:]

        assert RAW + 2 * EARLY == CHUNKS
        places = [("ring", at) for at in range(RAW * 2048, RING, 2048)]
        places += [("rest", at) for at in range(PARTS_AT, REST, 2048)]
        parts = [rounded(f"part{n}", where, at, 2048) for n, (where, at) in enumerate(places)]
        hi = parts[0:EARLY] + parts[2 * EARLY:EARLY + PARTS]
        lo = parts[EARLY:2 * EARLY] + parts[EARLY + PARTS:]
        bank = [ctx.enter_context(nc.psum_tensor(f"bank{n}", [P, 512], F32)) for n in range(8)]
        keep = Place(rest, 0, REST)
        m = {"hi": hi, "lo": lo, "ring": ring, "rest": rest, "rounded": rounded, "bank": bank, "sig": sig}
        m["x"] = keep.take(T, D)
        m["con"] = keep.take(NCON)
        m["vecT"] = keep.take(P)
        m["mod_scale"] = keep.take(KT)
        m["mod_shift"] = keep.take(KT)
        m["gate_row"] = keep.take(D)
        m["ident_b"] = keep.take(P, dt=BF16)
        m["ones_b"] = keep.take(P, dt=BF16)
        m["strict_b"] = keep.take(P, dt=BF16)
        m["negmask_b"] = keep.take(P, dt=BF16)
        m["slot"] = keep.take(T, E + 2)
        m["gates"] = keep.take(T, TOPK)
        m["dest"] = keep.take(T, TOPK, dt=I32)
        m["extra"] = keep.take(4 * MAX_EXTRA)
        m["extra_i"] = keep.take(2 * MAX_EXTRA + 2, dt=I32)
        m["first_free"] = keep.at
        m["gateT"] = keep.take(T, P, parts=E)
        m["b_down"] = keep.take(D, parts=E)
        m["free"] = keep.at
        m["h2_dram"] = nc.dram_tensor("h2_rows", [S, D], F32, kind="Internal").ap()
        m["y_dram"] = nc.dram_tensor("expert_rows", [BLOCKS * P, D], F32, kind="Internal").ap()
        m["bias_dram"] = nc.dram_tensor("bias_by_distance", [HB, S + P], F32, kind="Internal").ap()
        first_block(nc, a, m)
        retire("chunk_loaded")
        experts(nc, a, m)
        retire("slot_loaded")
        extra_experts(nc, a, m)
        retire("slot_loaded")
        second_block(nc, a, m, out)


def con(m, name, n, parts=P):
    return m["con"][0:parts, CON[name]:CON[name] + n]


def col(m, name, n=0, parts=P):
    at = VEC[name] + n
    return m["vecT"][0:parts, at:at + 1]


class Chain:

    def __init__(self, eng, sem):
        self.eng, self.sem, self.n = eng, sem, 0

    def link(self, ins):
        self.n += 1
        ins.then_inc(self.sem, 1)
        self.eng.wait_ge(self.sem, self.n)


def newton(nc, chain, y, v, tmp):
    chain.link(nc.vector.scalar_tensor_tensor(out=tmp, in0=v, scalar=-0.5, in1=y, op0=ALU.mult, op1=ALU.mult))
    chain.link(nc.vector.tensor_tensor(tmp, tmp, y, ALU.mult))
    return nc.vector.scalar_tensor_tensor(out=y, in0=tmp, scalar=1.5, in1=y, op0=ALU.add, op1=ALU.mult)


def first_block(nc, a, m):
    sig, bank, ring, rest, x = m["sig"], m["bank"], m["ring"], m["rest"], m["x"]
    keep = Place(rest, m["first_free"], REST)
    ident, ones = con(m, "ident", P), con(m, "ones", P)
    ident_b, negmask_b, ones_b, strict_b = m["ident_b"], m["negmask_b"], m["ones_b"], m["strict_b"]
    link_v, link_a, link_p = sig("A_vector_own"), sig("A_scalar_own"), sig("A_pool_own")

    head = Place(ring, 0, 8 * 2048)
    xn = head.take(T, D)
    hT = head.take(KT, S)
    w_swap = head.take(2, 2 * P)
    w_q, w_qr = head.take(2, H1 * NOPE), head.take(2, H1 * ROPE)
    w_pool = head.take(GROUPS, P)
    qT = xn.rearrange("p a b -> p (a b)").rearrange("p (h s) -> p h s", h=H1)
    kT = hT
    tail = Place(ring, 8 * 2048, RING)
    w_in = tail.take(KT, D_IN1)
    krope_w = tail.take(KT, ROPE)
    w_out = ring[:, 8 * 2048:RING].rearrange("p (k n) -> p k n", k=KT)

    late = Place(rest, keep.at, REST)
    w_ada, acc = late.take(2, 3 * D), late.take(3 * D)
    probs, probsT = keep.take(2, S), keep.take(2, S)
    rope_c, rope_s = keep.take(S), keep.take(S)
    w_k, w_v = keep.take(H1 * NOPE), keep.take(H1 * DV1)
    v_sb = keep.take(T, S)
    cos, sin = keep.take(S), keep.take(S)
    lat = keep.take(3, S)
    sq = keep.take(2, S)
    assert late.at <= keep.at
    gate_sum = Place(rest, keep.at, REST).take(2, S)
    var, inv, tmp = keep.take(S), keep.take(S), keep.take(S)
    mixT = keep.take(KT, S)
    y_attn = keep.take(T, S)
    uT = keep.take(GROUPS, S)
    h2 = rest[:, keep.at - 2 * GROUPS * S:keep.at].rearrange("p (t d) -> p t d", t=T)
    h2T = mixT
    g_ffn = keep.take(D)
    w_router, b_router = keep.take(KT, E), keep.take(E)
    pa, pb = keep.take(S), keep.take(S)
    small = keep.take(136)
    b_ada_row = rest[:, keep.at - 136 - 2 * S:keep.at - 136]
    vec = y_attn.rearrange("p a b -> p (a b)")[:, 0:P]
    pos_i = mixT.rearrange("p a b -> p (a b)")[:, 0:S].bitcast(I32)
    ang = mixT.rearrange("p a b -> p (a b)")[:, S:2 * S]
    turn = mixT.rearrange("p a b -> p (a b)")[:, 2 * S:3 * S]
    ss, ssv, ssi, sst = (small[:, 4 * n:4 * n + 4] for n in range(4))
    rowmax, rowsum, rowinv = (small[:, 16 + 32 * n:48 + 32 * n] for n in range(3))
    silu_c = small[:, 112:120]
    silu_t = small[:, 120:128]
    room = Place(rest, m["free"], m["first_free"] + 6 * D)
    gateT, b_down = m["gateT"], m["b_down"]
    logits, picked, ranks, total = (room.take(T, E) for _ in range(4))
    hot, hot2, hot3 = (room.take(T * TOPK, E) for _ in range(3))
    best, place_k = room.take(T, 8), room.take(T * TOPK)
    place_i = room.take(T, 8, dt=U32)
    picked_b = room.take(T, E, dt=BF16)
    count, extra, upto, base1, one_e = (room.take(E) for _ in range(5))
    gsum, ginv = room.take(T), room.take(T)
    ej, bj = room.take(MAX_EXTRA), room.take(MAX_EXTRA)
    SCALE = QK ** -0.5
    N_ATT = T * H1
    POOL_TURNS = [2 + 5 * g for g in range(GROUPS)]
    POOL_NORM_TURN = POOL_TURNS[-1] + 3

    def keys(i):
        return (i // H1 + 1) * P

    with nc.Block() as block:

        @block.sync
        def _(sp):
            sp.dma_start(m["con"], a["constants"]).then_inc(sig("con_loaded"), 16)
            for t in range(T):
                sp.dma_start(x[:, t, :], a["x"][0, t * P:(t + 1) * P, :]).then_inc(sig(f"x_loaded{t}"), 16)
            rows = [("g_attn", a["g_attn_norm"].rearrange("l (r q) -> (l r) q", q=P)),
                    ("b_pool", a["b_pool"].rearrange("l g c -> (l g) c")),
                    ("pool_scale", a["pool_scale"].rearrange("l (r q) -> (l r) q", q=P)),
                    ("g_q", a["g_q_a"].rearrange("l (r q) -> (l r) q", q=P)),
                    ("g_kv", a["g_kv_a"]),
                    ("g_out_pool", a["g_out_pool"].rearrange("l (r q) -> (l r) q", q=P)),
                    ("g_out_attn", a["g_out_attn"].rearrange("l (r q) -> (l r) q", q=P)),
                    ("c", a["c_2"].rearrange("l (r q) -> (l r) q", q=P)),
                    ("g_pre", a["g_pre_2"].rearrange("l (r q) -> (l r) q", q=P)),
                    ("b_ada", a["b_ada_2"][:, 0:2 * D].rearrange("l (r q) -> (l r) q", q=P)),
                    ("g_gdn", a["g_gdn_2"]),
                    ("g_kv2", a["g_kv_2"]),
                    ("conv", a["conv_w_2"].rearrange("l j (r q) -> (l j r) q", q=P))]
            for name, src in rows:
                sp.dma_start(vec[VEC[name]:VEC[name] + src.shape[0], :], src).then_inc(sig("vec_loaded"), 16)
            for k in range(KT):
                sp.dma_start(w_in[:, k, :], a["w_in"][0, k * P:(k + 1) * P, :]).then_inc(sig("w_in_loaded"), 16)
            sp.dma_start(pos_i, a["positions"].partition_broadcast(P)).then_inc(sig("pos_loaded"), 16)
            for k in range(2):
                src = a["w_q_b"][0, k * P:(k + 1) * P, :].rearrange("p (h c) -> p h c", h=H1)
                sp.dma_start(w_q[:, k, :].rearrange("p (h c) -> p h c", h=H1), src[:, :, 0:NOPE]).then_inc(sig("w_q_loaded"), 16)
                sp.dma_start(w_qr[:, k, :].rearrange("p (h c) -> p h c", h=H1), src[:, :, NOPE:QK]).then_inc(sig("w_q_loaded"), 16)
            src = a["w_kv_b"][0].rearrange("p (h c) -> p h c", h=H1)
            sp.dma_start(w_k.rearrange("p (h c) -> p h c", h=H1), src[:, :, 0:NOPE]).then_inc(sig("w_kv_loaded"), 16)
            sp.dma_start(w_v.rearrange("p (h c) -> p h c", h=H1), src[:, :, NOPE:P]).then_inc(sig("w_kv_loaded"), 16)
            sp.dma_start(w_pool, a["w_pool"][0].rearrange("g c d -> c g d")).then_inc(sig("w_pool_loaded"), 16)
            sp.dma_start(m["gate_row"], a["g_post_2"].partition_broadcast(P)).then_inc(sig("g_post_loaded"), 16)
            sp.dma_start(g_ffn, a["g_ffn_norm"].partition_broadcast(P)).then_inc(sig("g_ffn_loaded"), 16)
            sp.dma_start(w_router, a["w_router"][0].rearrange("(k p) n -> p k n", p=P)).then_inc(sig("router_loaded"), 16)
            sp.dma_start(b_router, a["b_router"].partition_broadcast(P)).then_inc(sig("router_loaded"), 16)
            sp.wait_ge(sig("proj_done"), 9)
            for k in range(KT):
                sp.dma_start(w_out[:, k, :], a["w_out"][0, k * P:(k + 1) * P, :]).then_inc(sig("w_out_loaded"), 16)
            sp.wait_ge(sig("pool_mixed"), GROUPS)
            sp.dma_start(b_ada_row, a["b_ada_2"][:, 2 * D:3 * D].partition_broadcast(P)).then_inc(sig("b_ada2_loaded"), 16)
            sp.wait_ge(sig("weighed"), N_ATT)
            for k in range(2):
                sp.dma_start(w_ada[:, k, :], a["w_ada_2"][0, k * P:(k + 1) * P, :]).then_inc(sig(f"w_ada_loaded{k}"), 16)
            for c in range(RAW):
                load_chunk(sp, a, m, 0, c, c)
            for k in range(2, KT):
                sp.wait_ge(sig("ada_added"), k - 1)
                sp.dma_start(w_ada[:, k % 2, :], a["w_ada_2"][0, k * P:(k + 1) * P, :]).then_inc(sig(f"w_ada_loaded{k % 2}"), 16)
            sp.wait_ge(sig("ada_added"), KT)
            sp.dma_start(b_down, a["b_down"][0]).then_inc(sig("b_down_loaded"), 16)
            for t in range(T):
                sp.wait_ge(sig("h2_ready"), t + 1)
                sp.dma_start(m["h2_dram"][t * P:(t + 1) * P, :], h2[:, t, :]).then_inc(sig("h2_stored"), 16)
            for c in range(EARLY):
                sp.wait_ge(sig("first_lo"), c + 1)
                load_chunk(sp, a, m, 0, RAW + c, c)
            sp.wait_ge(sig("h2_stored"), 16 * T)
            sp.wait_ge(sig("b_down_loaded"), 16)

        @block.gpsimd
        def _(pool):
            chain = Chain(pool, link_p)
            pool.wait_ge(sig("w_in_loaded"), 16 * KT)
            o = D_IN1 - ROPE
            nc.gpsimd.tensor_copy(krope_w[:, :, 0:16], w_in[:, :, o + 16:o + 32])
            nc.gpsimd.tensor_copy(krope_w[:, :, 16:32], w_in[:, :, o:o + 16]).then_inc(sig("krope_w_ready"), 1)
            pool.wait_ge(sig("w_q_loaded"), 64)
            for k in range(2):
                src = w_qr[:, k, :].rearrange("p (h c) -> p h c", h=H1)
                dst = w_swap[:, k, :].rearrange("p (h c) -> p h c", h=H1)
                nc.gpsimd.tensor_copy(dst[:, :, 0:16], src[:, :, 16:32])
                ins = nc.gpsimd.tensor_copy(dst[:, :, 16:32], src[:, :, 0:16])
            ins.then_inc(sig("w_swap_ready"), 1)
            for g in range(GROUPS):
                pool.wait_ge(sig("uT_ready"), g + 1)
                cur = uT[:, g, :]
                if g:
                    pool.wait_ge(sig("pool_mixed"), g)
                for n in range(g + 1):
                    d, nxt = 1 << n, (pa, pb)[(g - n) % 2]
                    nc.gpsimd.tensor_copy(nxt[:, 0:d], cur[:, 0:d])
                    chain.link(nc.gpsimd.tensor_tensor(nxt[:, d:S], cur[:, d:S], cur[:, 0:S - d], ALU.add))
                    cur = nxt
                w = 2 << g
                inv16 = m["con"][:, CON["poolinv"] + 16 * g:CON["poolinv"] + 16 * g + 16]
                chain.link(nc.gpsimd.tensor_scalar(pa[:, 16:S], pa[:, 16:S], 1.0 / w, None, ALU.mult))
                chain.link(nc.gpsimd.tensor_tensor(pa[:, 0:16], pa[:, 0:16], inv16, ALU.mult))
                nc.gpsimd.tensor_tensor(pa, pa, uT[:, g, :], ALU.subtract).then_inc(sig("pool_diff"), 1)

        @block.scalar
        def _(act):
            chain = Chain(act, link_a)
            for t in range(T):
                act.wait_ge(sig(f"x_loaded{t}"), 16)
                nc.scalar.activation(xn[:, t, :], x[:, t, :], ACT.Square, accum_out=ss[:, t:t + 1]).then_inc(sig("x_squares"), 1)

            def rsqrt(k, y, v):
                act.wait_ge(sig("var_ready"), k + 1)
                chain.link(nc.scalar.activation(y, v, ACT.Ln))
                nc.scalar.activation(y, y, ACT.Exp, scale=-0.5).then_inc(sig("rsqrt_ready"), 1)

            rsqrt(0, ssi, ssv)
            act.wait_ge(sig("vecT_ready"), 1)
            nc.scalar.activation(silu_t, m["vecT"][:, VEC["c"]:VEC["c"] + 8], ACT.Exp, scale=-1.0).then_inc(sig("c_exp"), 1)
            for k in range(0, KT, 2):
                act.wait_ge(sig("hT_turned"), k + 1)
                nc.scalar.activation(hT[:, k, :], bank[k % 2][:], ACT.Copy, scale=col(m, "g_attn", k)).then_inc(sig("hT_ready0"), 1)
            act.wait_ge(sig("angles_ready"), 1)
            nc.scalar.activation(cos, ang, ACT.Sin).then_inc(sig("cos_ready"), 1)
            nc.scalar.activation(sin, turn, ACT.Sin).then_inc(sig("sin_ready"), 1)
            for n in range(3):
                act.wait_ge(sig("proj_done"), n + 1)
                nc.scalar.activation(lat[:, n, :], bank[2 + n % 2][:], ACT.Copy).then_inc(sig("lat_copied"), 1)
                if n == 2:
                    act.wait_ge(sig("lat_summed"), 1)
                nc.scalar.activation(sq[:, n % 2, :], bank[2 + n % 2][:], ACT.Square).then_inc(sig("lat_squared"), 1)
                if n == 0:
                    rsqrt(1, inv, var)
            rsqrt(2, inv, var)
            for g in range(GROUPS):
                act.wait_ge(sig("proj_done"), 6 + g)
                nc.scalar.activation(uT[:, g, :], bank[2 + g % 2][:], ACT.Copy).then_inc(sig("uT_ready"), 1)
            for n in range(4):
                act.wait_ge(sig("k_nope_done"), n + 1)
                nc.scalar.activation(kT[0:64, 2 * n, :], bank[4 + n % 2][0:64, :], ACT.Copy)
                nc.scalar.activation(kT[0:64, 2 * n + 1, :], bank[4 + n % 2][64:128, :], ACT.Copy).then_inc(sig("k_nope_ready"), 1)
            for n in range(4):
                act.wait_ge(sig("q_nope_done"), n + 1)
                nc.scalar.activation(qT[0:64, 2 * n, :], bank[4 + n % 2][0:64, :], ACT.Copy)
                nc.scalar.activation(qT[0:64, 2 * n + 1, :], bank[4 + n % 2][64:128, :], ACT.Copy).then_inc(sig("q_nope_ready"), 1)
            act.wait_ge(sig("k_rope_ready"), 1)
            for h in range(1, H1):
                ins = nc.scalar.activation(kT[64:96, h, :], kT[64:96, 0, :], ACT.Copy)
            ins.then_inc(sig("k_rope_spread"), 1)
            for t in range(T):
                act.wait_ge(sig("v_done"), t + 1)
                nc.scalar.activation(v_sb[:, t, :], bank[2 + t % 2][:], ACT.Copy).then_inc(sig("v_ready"), 1)
            for i in range(N_ATT):
                act.wait_ge(sig("rowmax_ready"), i + 1)
                if i >= 2:
                    act.wait_ge(sig("probs_turned"), i - 1)
                nc.scalar.activation(probs[:, i % 2, 0:keys(i)], bank[i % 2][:, 0:keys(i)], ACT.Exp,
                                     bias=rowmax[:, i:i + 1], scale=SCALE,
                                     accum_out=rowsum[:, i:i + 1]).then_inc(sig("probs_ready"), 1)
                if i in POOL_TURNS:
                    g = POOL_TURNS.index(i)
                    act.wait_ge(sig("pool_out"), g + 1)
                    if g >= 2:
                        act.wait_ge(sig("pool_summed"), g - 1)
                    nc.scalar.activation(sq[:, g % 2, :], mixT[:, g, :], ACT.Square).then_inc(sig("pool_squared"), 1)
                if i == POOL_NORM_TURN:
                    rsqrt(3, inv, var)
            for t in range(T):
                act.wait_ge(sig("y_attn_ready"), t + 1)
                if t >= 2:
                    act.wait_ge(sig("y_squares"), t - 1)
                nc.scalar.activation(sq[:, t % 2, :], y_attn[:, t, :], ACT.Square, accum_out=ss[:, t:t + 1]).then_inc(sig("y_squares"), 1)
            rsqrt(4, ssi, ssv)
            for f in range(0, 4, 2):
                act.wait_ge(sig("mix_turned"), f + 1)
                nc.scalar.activation(mixT[:, 4 + f, :], bank[f % 2][:], ACT.Copy, scale=col(m, "g_out_attn", f)).then_inc(sig("mixT_ready0"), 1)
            for t in range(T):
                act.wait_ge(sig("x1_ready"), 2 * t + 2)
                nc.scalar.activation(h2[:, t, :], x[:, t, :], ACT.Square, accum_out=ss[:, t:t + 1]).then_inc(sig("x1_squares"), 1)
                rsqrt(5 + t, ssi[:, t:t + 1], ssv[:, t:t + 1])
            for k in range(0, KT, 2):
                act.wait_ge(sig("h2T_turned"), k + 1)
                nc.scalar.activation(h2T[:, k, :], bank[k % 2][:], ACT.Copy).then_inc(sig("h2T_ready0"), 1)
            for c in range(2):
                act.wait_ge(sig("gate_summed"), c + 1)
                nc.scalar.activation(gate_sum[:, c, :], bank[6 + c][:], ACT.Copy).then_inc(sig("gate_copied"), 1)
            for c in range(EARLY):
                act.wait_ge(sig(f"chunk_loaded{c}"), 32)
                nc.scalar.activation(m["hi"][c], ring[:, c * 2048:(c + 1) * 2048], ACT.Copy).then_inc(sig("first_hi"), 1)
            act.wait_ge(sig("best_ready"), 1)
            nc.scalar.activation(m["gates"], m["gates"], ACT.Exp).then_inc(sig("gates_exp"), 1)

        @block.tensor
        def _(pe):
            pe.wait_ge(sig("con_loaded"), 16)
            pe.wait_ge(sig("vec_loaded"), 16 * 13)
            nc.tensor.transpose(bank[7][:, 0:NVEC], vec[0:NVEC, :], ident[0:NVEC, 0:NVEC]).then_inc(sig("vec_turned"), 1)
            for k in range(KT):
                if k >= 2:
                    pe.wait_ge(sig(f"hT_ready{k % 2}"), k // 2)
                for t in range(T):
                    if k == 0:
                        pe.wait_ge(sig("xn_ready"), t + 1)
                    ins = nc.tensor.transpose(bank[k % 2][:, t * P:(t + 1) * P], xn[:, t, k * P:(k + 1) * P], ident)
                ins.then_inc(sig("hT_turned"), 1)
            pe.wait_ge(sig("w_in_loaded"), 16 * KT)
            pe.wait_ge(sig("krope_w_ready"), 1)
            pe.wait_ge(sig("hT_ready0"), 4)
            pe.wait_ge(sig("hT_ready1"), 4)

            def project(o, w, c0, n):
                for k in range(KT):
                    ins = nc.tensor.matmul(o, w[:, k, c0:c0 + n], hT[:, k, :], start=(k == 0), stop=(k == KT - 1))
                ins.then_inc(sig("proj_done"), 1)

            def latent_sum(first, last, o):
                for n in range(first, last + 1):
                    pe.wait_ge(sig("lat_squared"), n + 1)
                    ins = nc.tensor.matmul(o, ones, sq[:, n % 2, :], start=(n == first), stop=(n == last))
                ins.then_inc(sig("lat_summed"), 1)

            project(bank[2][:], w_in, D_POOL + QLAT, KVLAT)
            project(bank[3][:], w_in, D_POOL, P)
            latent_sum(0, 0, bank[6][:])
            pe.wait_ge(sig("lat_copied"), 1)
            project(bank[2][:], w_in, D_POOL + P, P)
            project(bank[4][64:96, :], w_in, D_IN1 - ROPE, ROPE)
            project(bank[5][64:96, :], krope_w, 0, ROPE)
            pe.wait_ge(sig("var_ready"), 2)
            latent_sum(1, 2, bank[6][:])
            for g in range(GROUPS):
                if g < 2:
                    pe.wait_ge(sig("lat_squared"), 3 - g)
                else:
                    pe.wait_ge(sig("uT_ready"), g - 1)
                project(bank[2 + g % 2][:], w_in, g * P, P)
            pe.wait_ge(sig("kv_norm"), 1)
            pe.wait_ge(sig("k_rope_read"), 1)
            pe.wait_ge(sig("w_kv_loaded"), 32)
            for n in range(4):
                if n >= 2:
                    pe.wait_ge(sig("k_nope_ready"), n - 1)
                nc.tensor.matmul(bank[4 + n % 2][:], w_k[:, n * P:(n + 1) * P], lat[:, 0, :], start=True, stop=True).then_inc(sig("k_nope_done"), 1)
            pe.wait_ge(sig("q_norm"), 1)
            pe.wait_ge(sig("w_q_loaded"), 64)
            for n in range(4):
                if n < 2:
                    pe.wait_ge(sig("k_nope_ready"), n + 3)
                else:
                    pe.wait_ge(sig("q_nope_ready"), n - 1)
                for k in range(2):
                    ins = nc.tensor.matmul(bank[4 + n % 2][:], w_q[:, k, n * P:(n + 1) * P], lat[:, 1 + k, :], start=(k == 0), stop=(k == 1))
                ins.then_inc(sig("q_nope_done"), 1)
            for t in range(T):
                pe.wait_ge(sig("uT_ready"), 4) if t < 2 else pe.wait_ge(sig("v_ready"), t - 1)
                nc.tensor.matmul(bank[2 + t % 2][:], lat[:, 0, t * P:(t + 1) * P], w_v, start=True, stop=True).then_inc(sig("v_done"), 1)
            pe.wait_ge(sig("w_swap_ready"), 1)
            pe.wait_ge(sig("var_ready"), 3)
            for n in range(2):
                if n == 1:
                    pe.wait_ge(sig("q_rope_read"), 1)
                for k in range(2):
                    nc.tensor.matmul(bank[6][:], w_qr[:, k, n * P:(n + 1) * P], lat[:, 1 + k, :], start=(k == 0), stop=(k == 1))
                for k in range(2):
                    ins = nc.tensor.matmul(bank[7][:], w_swap[:, k, n * P:(n + 1) * P], lat[:, 1 + k, :], start=(k == 0), stop=(k == 1))
                ins.then_inc(sig("q_rope_done"), 1)
            pe.wait_ge(sig("q_rope_ready"), 2)
            pe.wait_ge(sig("q_nope_ready"), 4)
            pe.wait_ge(sig("k_rope_spread"), 1)
            pe.wait_ge(sig("v_ready"), 4)
            pe.wait_ge(sig("con_b_ready"), 1)

            def scores(i):
                q0, h = (i // H1) * P, i % H1
                if i >= 2:
                    pe.wait_ge(sig("probs_ready"), i - 1)
                nc.tensor.matmul(bank[i % 2][:, 0:keys(i)], qT[0:QK, h, q0:q0 + P], kT[0:QK, h, 0:keys(i)], start=True, stop=False, skip_group_check=True)
                nc.tensor.matmul(bank[i % 2][:, q0:q0 + P], ident_b, negmask_b, start=False, stop=True, skip_group_check=True).then_inc(sig("scores_ready"), 1)

            def turn_probs(i):
                pe.wait_ge(sig("probs_ready"), i + 1)
                if i >= 2:
                    pe.wait_ge(sig("probsT_ready"), i - 1)
                for k in range(i // H1 + 1):
                    ins = nc.tensor.transpose(bank[2 + i % 2][:, k * P:(k + 1) * P], probs[:, i % 2, k * P:(k + 1) * P], ident)
                ins.then_inc(sig("probs_turned"), 1)

            def weigh(i):
                t, h = i // H1, i % H1
                pe.wait_ge(sig("probsT_ready"), i + 1)
                if h == 0 and t >= 2:
                    pe.wait_ge(sig("y_attn_ready"), t - 1)
                for k in range(t + 1):
                    ins = nc.tensor.matmul(bank[4 + t % 2][:, h * DV1:(h + 1) * DV1], probsT[:, i % 2, k * P:(k + 1) * P],
                                           v_sb[:, k, h * DV1:(h + 1) * DV1], start=(k == 0), stop=(k == t), skip_group_check=True)
                ins.then_inc(sig("weighed"), 1)

            def pool_out(g):
                pe.wait_ge(sig("pool_diff"), g + 1)
                if g >= 1:
                    pe.wait_ge(sig("pool_out"), g)
                nc.tensor.matmul(bank[6][:], w_pool[:, g, :], pa, start=True, stop=True).then_inc(sig("pool_mixed"), 1)

            pe.wait_ge(sig("w_pool_loaded"), 16)
            for i in range(N_ATT + 2):
                if i < N_ATT:
                    scores(i)
                if i in POOL_TURNS:
                    pool_out(POOL_TURNS.index(i))
                if i - 2 in POOL_TURNS:
                    g = POOL_TURNS.index(i - 2)
                    pe.wait_ge(sig("pool_squared"), g + 1)
                    nc.tensor.matmul(bank[7][:], ones, sq[:, g % 2, :], start=(g == 0), stop=(g == GROUPS - 1), skip_group_check=True).then_inc(sig("pool_summed"), 1)
                if 1 <= i <= N_ATT:
                    turn_probs(i - 1)
                if i >= 2:
                    weigh(i - 2)
            for f in range(4):
                if f == 0:
                    pe.wait_ge(sig("yn_ready"), T)
                if f >= 2:
                    pe.wait_ge(sig(f"mixT_ready{f % 2}"), 1)
                for t in range(T):
                    ins = nc.tensor.transpose(bank[f % 2][:, t * P:(t + 1) * P], y_attn[:, t, f * P:(f + 1) * P], ident)
                ins.then_inc(sig("mix_turned"), 1)
            pe.wait_ge(sig("w_out_loaded"), 16 * KT)
            pe.wait_ge(sig("mixT_pool"), GROUPS)
            for t in range(T):
                for c in range(2):
                    b = bank[2 + (2 * t + c) % 4]
                    if 2 * t + c >= 4:
                        pe.wait_ge(sig("x1_ready"), 2 * t + c - 3)
                    for k in range(KT):
                        if t == 0 and c == 0 and k == 4:
                            pe.wait_ge(sig("mixT_ready0"), 2)
                            pe.wait_ge(sig("mixT_ready1"), 2)
                        ins = nc.tensor.matmul(b[:], mixT[:, k, t * P:(t + 1) * P], w_out[:, k, c * 512:(c + 1) * 512], start=(k == 0), stop=(k == KT - 1))
                    ins.then_inc(sig("out_done"), 1)
            pe.wait_ge(sig("ada_added"), KT)
            pe.wait_ge(sig("x1_ready"), 2 * T)
            for n in range(16):
                ins = nc.tensor.matmul(bank[3][:, n:n + 1], acc[:, n * P:(n + 1) * P], ones[:, 0:1], start=True, stop=True, skip_group_check=True)
            ins.then_inc(sig("mod_summed"), 1)
            for c in range(2):
                nc.tensor.matmul(bank[6 + c][:], ones, acc[:, 2 * D + c * 512:2 * D + (c + 1) * 512], start=True, stop=True).then_inc(sig("gate_summed"), 1)
            for k in range(KT):
                if k >= 2:
                    pe.wait_ge(sig(f"h2T_ready{k % 2}"), k // 2)
                for t in range(T):
                    if k == 0:
                        pe.wait_ge(sig("h2_ready"), t + 1)
                    ins = nc.tensor.transpose(bank[k % 2][:, t * P:(t + 1) * P], h2[:, t, k * P:(k + 1) * P], ident)
                ins.then_inc(sig("h2T_turned"), 1)
            pe.wait_ge(sig("router_loaded"), 32)
            pe.wait_ge(sig("h2T_ready0"), 4)
            pe.wait_ge(sig("h2T_ready1"), 4)
            for t in range(T):
                for k in range(KT):
                    ins = nc.tensor.matmul(bank[2][:, t * E:(t + 1) * E], h2T[:, k, t * P:(t + 1) * P], w_router[:, k, :], start=(k == 0), stop=(k == KT - 1), skip_group_check=True)
            ins.then_inc(sig("logits_done"), 1)
            pe.wait_ge(sig("picked_ready"), 1)
            for t in range(T):
                for u in range(t + 1):
                    nc.tensor.matmul(bank[4][:, t * E:(t + 1) * E], strict_b if u == t else ones_b, picked_b[:, u, :], start=(u == 0), stop=(u == t), skip_group_check=True)
            for u in range(T):
                ins = nc.tensor.matmul(bank[4][:, T * E:(T + 1) * E], ones_b, picked_b[:, u, :], start=(u == 0), stop=(u == T - 1), skip_group_check=True)
            ins.then_inc(sig("ranked"), 1)
            pe.wait_ge(sig("gate_by_expert"), 1)
            for t in range(T):
                ins = nc.tensor.transpose(bank[5][0:E, t * P:(t + 1) * P], total[:, t, :], ident)
            ins.then_inc(sig("gateT_turned"), 1)

        @block.vector
        def _(dve):
            chain = Chain(dve, link_v)
            V = nc.vector

            def variance(k, v, s, n):
                V.tensor_scalar(v, s, 1.0 / n, EPS, ALU.mult, ALU.add).then_inc(sig("var_ready"), 1)

            def root(k, y, v, t):
                dve.wait_ge(sig("rsqrt_ready"), k + 1)
                chain.link(newton(nc, chain, y, v, t))

            dve.wait_ge(sig("con_loaded"), 16)
            V.tensor_copy(ident_b, ident)
            V.tensor_copy(ones_b, ones)
            V.tensor_copy(strict_b, con(m, "strict", P))
            V.tensor_copy(negmask_b, con(m, "negmask", P)).then_inc(sig("con_b_ready"), 1)
            dve.wait_ge(sig("vec_turned"), 1)
            V.tensor_copy(m["vecT"][:, 0:NVEC], bank[7][:, 0:NVEC]).then_inc(sig("vecT_ready"), 1)
            dve.wait_ge(sig("x_squares"), T)
            variance(0, ssv, ss, D)
            root(0, ssi, ssv, sst)
            for t in range(T):
                V.tensor_scalar(xn[:, t, :], x[:, t, :], ssi[:, t:t + 1], None, ALU.mult).then_inc(sig("xn_ready"), 1)
            dve.wait_ge(sig("vecT_ready"), 1)
            for k in range(1, KT, 2):
                dve.wait_ge(sig("hT_turned"), k + 1)
                V.tensor_scalar(hT[:, k, :], bank[k % 2][:], col(m, "g_attn", k), None, ALU.mult).then_inc(sig("hT_ready1"), 1)
            dve.wait_ge(sig("c_exp"), 1)
            chain.link(V.tensor_scalar(silu_t, silu_t, 1.0, None, ALU.add))
            chain.link(V.reciprocal(silu_c, silu_t))
            chain.link(V.tensor_tensor(silu_c, silu_c, m["vecT"][:, VEC["c"]:VEC["c"] + 8], ALU.mult))
            dve.wait_ge(sig("pos_loaded"), 16)
            chain.link(V.tensor_copy(tmp, pos_i))
            chain.link(V.tensor_scalar(tmp, tmp, con(m, "freq", 1), None, ALU.mult))
            two_pi = 2.0 * math.pi
            c1 = 6.28125
            c2 = float(np.float32(np.round((two_pi - c1) * 2.0 ** 20) / 2.0 ** 20))
            c3 = float(np.float32(two_pi - c1 - c2))
            big = 1.5 * 2.0 ** 23
            for dst, quarter in ((ang, 0.25), (turn, 0.0)):
                chain.link(V.tensor_scalar(var, tmp, 1.0 / two_pi, quarter, ALU.mult, ALU.add))
                chain.link(V.tensor_scalar(var, var, big, None, ALU.add))
                chain.link(V.tensor_scalar(var, var, big, None, ALU.subtract))
                chain.link(V.scalar_tensor_tensor(out=dst, in0=var, scalar=-c1, in1=tmp, op0=ALU.mult, op1=ALU.add))
                chain.link(V.scalar_tensor_tensor(out=dst, in0=var, scalar=-c2, in1=dst, op0=ALU.mult, op1=ALU.add))
                chain.link(V.scalar_tensor_tensor(out=dst, in0=var, scalar=-c3, in1=dst, op0=ALU.mult, op1=ALU.add))
                chain.link(V.tensor_scalar(dst, dst, quarter * two_pi, math.pi - 1e-6, ALU.add, ALU.min))
                chain.link(V.tensor_scalar(dst, dst, -(math.pi - 1e-6), None, ALU.max))
            dve.sem_inc(sig("angles_ready"), 1)
            dve.wait_ge(sig("lat_summed"), 1)
            variance(1, var, bank[6][:], KVLAT)
            root(1, inv, var, tmp)
            dve.wait_ge(sig("lat_copied"), 1)
            V.scalar_tensor_tensor(out=lat[:, 0, :], in0=lat[:, 0, :], scalar=col(m, "g_kv"), in1=inv, op0=ALU.mult, op1=ALU.mult).then_inc(sig("kv_norm"), 1)
            dve.wait_ge(sig("sin_ready"), 1)
            dve.wait_ge(sig("cos_ready"), 1)
            chain.link(V.tensor_scalar(sin, sin, con(m, "sign", 1), None, ALU.mult))
            dve.wait_ge(sig("proj_done"), 5)
            chain.link(V.tensor_tensor(rope_c[64:96, :], bank[4][64:96, :], cos[64:96, :], ALU.mult))
            V.tensor_tensor(rope_s[64:96, :], bank[5][64:96, :], sin[64:96, :], ALU.mult).then_inc(sig("k_rope_read"), 1)
            dve.wait_ge(sig("kv_norm"), 1)
            dve.wait_ge(sig("lat_summed"), 2)
            variance(2, var, bank[6][:], QLAT)
            root(2, inv, var, tmp)
            dve.wait_ge(sig("lat_copied"), 3)
            for k in range(2):
                ins = V.scalar_tensor_tensor(out=lat[:, 1 + k, :], in0=lat[:, 1 + k, :], scalar=col(m, "g_q", k), in1=inv, op0=ALU.mult, op1=ALU.mult)
            ins.then_inc(sig("q_norm"), 1)
            dve.wait_ge(sig("proj_done"), 9)
            dve.wait_ge(sig("k_rope_read"), 1)
            V.tensor_tensor(kT[64:96, 0, :], rope_c[64:96, :], rope_s[64:96, :], ALU.add).then_inc(sig("k_rope_ready"), 1)
            for n in range(2):
                dve.wait_ge(sig("q_rope_done"), n + 1)
                dve.wait_ge(sig("k_rope_ready"), 1) if n == 0 else dve.wait_ge(sig("q_rope_ready"), 1)
                chain.link(V.tensor_tensor(rope_c, bank[6][:], cos, ALU.mult))
                V.tensor_tensor(rope_s, bank[7][:], sin, ALU.mult).then_inc(sig("q_rope_read"), 1)
                dve.wait_ge(sig("q_rope_read"), n + 1)
                for h in range(4):
                    r = slice(32 * h, 32 * h + 32)
                    ins = V.tensor_tensor(qT[64:96, 4 * n + h, :], rope_c[r, :], rope_s[r, :], ALU.add)
                ins.then_inc(sig("q_rope_ready"), 1)
            for i in range(N_ATT + 2):
                if i < N_ATT:
                    dve.wait_ge(sig("scores_ready"), i + 1)
                    chain.link(V.tensor_reduce(rowmax[:, i:i + 1], bank[i % 2][:, 0:keys(i)], AX, ALU.max))
                    V.tensor_scalar(rowmax[:, i:i + 1], rowmax[:, i:i + 1], -SCALE, None, ALU.mult).then_inc(sig("rowmax_ready"), 1)
                if i in POOL_TURNS:
                    g = POOL_TURNS.index(i)
                    dve.wait_ge(sig("pool_mixed"), g + 1)
                    V.tensor_scalar(mixT[:, g, :], bank[6][:], col(m, "b_pool", g), col(m, "pool_scale", g), ALU.add, ALU.mult).then_inc(sig("pool_out"), 1)
                if i == POOL_NORM_TURN:
                    dve.wait_ge(sig("pool_summed"), GROUPS)
                    variance(3, var, bank[7][:], D_POOL)
                if i == POOL_NORM_TURN + 2:
                    root(3, inv, var, tmp)
                    for g in range(GROUPS):
                        V.scalar_tensor_tensor(out=mixT[:, g, :], in0=mixT[:, g, :], scalar=col(m, "g_out_pool", g), in1=inv, op0=ALU.mult, op1=ALU.mult).then_inc(sig("mixT_pool"), 1)
                if 1 <= i <= N_ATT:
                    j = i - 1
                    dve.wait_ge(sig("probs_turned"), j + 1)
                    if j >= 2:
                        dve.wait_ge(sig("weighed"), j - 1)
                    V.tensor_copy(probsT[:, j % 2, 0:keys(j)], bank[2 + j % 2][:, 0:keys(j)]).then_inc(sig("probsT_ready"), 1)
                if i >= H1 + 1 and (i - 1) % H1 == 0:
                    t = (i - 1) // H1 - 1
                    dve.wait_ge(sig("weighed"), H1 * (t + 1))
                    chain.link(V.reciprocal(rowinv[:, H1 * t:H1 * (t + 1)], rowsum[:, H1 * t:H1 * (t + 1)]))
                    V.tensor_tensor(y_attn[:, t, :].rearrange("p (h d) -> p h d", h=H1), bank[4 + t % 2][:].rearrange("p (h d) -> p h d", h=H1),
                                    spread(rowinv[:, H1 * t:H1 * (t + 1)], DV1), ALU.mult).then_inc(sig("y_attn_ready"), 1)
            dve.wait_ge(sig("y_squares"), T)
            variance(4, ssv, ss, S)
            root(4, ssi, ssv, sst)
            for t in range(T):
                V.tensor_scalar(y_attn[:, t, :], y_attn[:, t, :], ssi[:, t:t + 1], None, ALU.mult).then_inc(sig("yn_ready"), 1)
            for f in range(1, 4, 2):
                dve.wait_ge(sig("mix_turned"), f + 1)
                V.tensor_scalar(mixT[:, 4 + f, :], bank[f % 2][:], col(m, "g_out_attn", f), None, ALU.mult).then_inc(sig("mixT_ready1"), 1)
            dve.wait_ge(sig("g_ffn_loaded"), 16)
            for t in range(T):
                for c in range(2):
                    n = 2 * t + c
                    dve.wait_ge(sig("out_done"), n + 1)
                    o = x[:, t, c * 512:(c + 1) * 512]
                    V.tensor_tensor(o, bank[2 + n % 4][:], o, ALU.add).then_inc(sig("x1_ready"), 1)
                for k in (2 * t, 2 * t + 1):
                    dve.wait_ge(sig(f"w_ada_loaded{k % 2}"), 16 * (k // 2 + 1))
                    if k == 0:
                        ins = V.tensor_scalar(acc, w_ada[:, 0, :], silu_c[:, 0:1], None, ALU.mult)
                    else:
                        dve.wait_ge(sig("ada_added"), k)
                        ins = V.scalar_tensor_tensor(out=acc, in0=w_ada[:, k % 2, :], scalar=silu_c[:, k:k + 1], in1=acc, op0=ALU.mult, op1=ALU.add)
                    ins.then_inc(sig("ada_added"), 1)
                dve.wait_ge(sig("x1_squares"), t + 1)
                variance(5 + t, ssv[:, t:t + 1], ss[:, t:t + 1], D)
                root(5 + t, ssi[:, t:t + 1], ssv[:, t:t + 1], sst[:, t:t + 1])
                V.scalar_tensor_tensor(out=h2[:, t, :], in0=x[:, t, :], scalar=ssi[:, t:t + 1], in1=g_ffn, op0=ALU.mult, op1=ALU.mult).then_inc(sig("h2_ready"), 1)
            for k in range(1, KT, 2):
                dve.wait_ge(sig("h2T_turned"), k + 1)
                V.tensor_copy(h2T[:, k, :], bank[k % 2][:]).then_inc(sig("h2T_ready1"), 1)
            dve.wait_ge(sig("mod_summed"), 1)
            chain.link(V.tensor_tensor(m["mod_shift"], bank[3][:, 0:8], m["vecT"][:, VEC["b_ada"]:VEC["b_ada"] + 8], ALU.add))
            chain.link(V.tensor_tensor(m["mod_scale"], bank[3][:, 8:16], m["vecT"][:, VEC["b_ada"] + 8:VEC["b_ada"] + 16], ALU.add))
            chain.link(V.scalar_tensor_tensor(out=m["mod_scale"], in0=m["mod_scale"], scalar=1.0, in1=m["vecT"][:, VEC["g_pre"]:VEC["g_pre"] + 8], op0=ALU.add, op1=ALU.mult))
            dve.wait_ge(sig("gate_copied"), 2)
            dve.wait_ge(sig("g_post_loaded"), 16)
            gate = gate_sum.rearrange("p a b -> p (a b)")
            dve.wait_ge(sig("b_ada2_loaded"), 16)
            chain.link(V.tensor_tensor(gate, gate, b_ada_row, ALU.add))
            chain.link(V.tensor_tensor(m["gate_row"], gate, m["gate_row"], ALU.mult))
            for c in range(EARLY):
                dve.wait_ge(sig("first_hi"), c + 1)
                V.tensor_tensor(m["lo"][c], ring[:, c * 2048:(c + 1) * 2048], m["hi"][c].bitcast(F32), ALU.subtract).then_inc(sig("first_lo"), 1)
            dve.wait_ge(sig("logits_done"), 1)
            dve.wait_ge(sig("router_loaded"), 32)
            chain.link(V.tensor_tensor(logits, bank[2][:, 0:T * E].rearrange("p (t e) -> p t e", t=T), repeat(b_router, T), ALU.add))
            for t in range(T):
                chain.link(V.max(best[:, t, :], logits[:, t, :]))
                chain.link(V.max_index(place_i[:, t, :], best[:, t, :], logits[:, t, :]))
            V.tensor_tensor(m["gates"], best[:, :, 0:TOPK], spread(best[:, :, 0], TOPK), ALU.subtract).then_inc(sig("best_ready"), 1)
            chain.link(V.tensor_copy(place_k.rearrange("p (t k) -> p t k", t=T), place_i[:, :, 0:TOPK]))
            chain.link(V.tensor_tensor(hot, repeat(con(m, "iota", E), T * TOPK), spread(place_k, E), ALU.is_equal))
            by_expert = hot.rearrange("p (t k) e -> p t e k", t=T)
            chain.link(V.tensor_reduce(picked, by_expert, AX, ALU.add))
            V.tensor_copy(picked_b, picked).then_inc(sig("picked_ready"), 1)
            dve.wait_ge(sig("gates_exp"), 1)
            chain.link(V.tensor_reduce(gsum, m["gates"], AX, ALU.add))
            chain.link(V.reciprocal(ginv, gsum))
            chain.link(V.tensor_tensor(m["gates"], m["gates"], spread(ginv, TOPK), ALU.mult))
            chain.link(V.tensor_tensor(hot2, hot, spread(m["gates"].rearrange("p t k -> p (t k)"), E), ALU.mult))
            V.tensor_reduce(total, hot2.rearrange("p (t k) e -> p t e k", t=T), AX, ALU.add).then_inc(sig("gate_by_expert"), 1)
            dve.wait_ge(sig("ranked"), 1)
            chain.link(V.tensor_copy(ranks, bank[4][:, 0:T * E].rearrange("p (t e) -> p t e", t=T)))
            chain.link(V.tensor_copy(count, bank[4][:, T * E:(T + 1) * E]))
            chain.link(V.memset(m["slot"], -1.0))
            chain.link(V.scalar_tensor_tensor(out=logits, in0=ranks, scalar=1.0, in1=picked, op0=ALU.add, op1=ALU.mult))
            V.tensor_scalar(m["slot"][:, :, 0:E], logits, -1.0, None, ALU.add).then_inc(sig("slot_ready"), 1)
            dve.wait_ge(sig("slot_ready"), 1)
            chain.link(V.tensor_scalar(extra, count, float(P), None, ALU.is_gt))
            chain.link(V.scalar_tensor_tensor(out=extra, in0=count, scalar=2.0 * P, in1=extra, op0=ALU.is_gt, op1=ALU.add))
            chain.link(V.scalar_tensor_tensor(out=extra, in0=count, scalar=3.0 * P, in1=extra, op0=ALU.is_gt, op1=ALU.add))
            chain.link(V.memset(one_e, 1.0))
            chain.link(V.tensor_tensor_scan(upto, one_e, extra, 0.0, ALU.mult, ALU.add))
            chain.link(V.tensor_tensor(base1, upto, extra, ALU.subtract))
            chain.link(V.tensor_scalar(base1, base1, float(P), float(P * (E - 1)), ALU.mult, ALU.add))
            chain.link(V.tensor_tensor(base1, base1, con(m, "base0", E), ALU.subtract))
            chain.link(V.tensor_scalar(logits, ranks, float(P), None, ALU.is_ge))
            chain.link(V.tensor_tensor(logits, logits, repeat(base1, T), ALU.mult))
            chain.link(V.tensor_tensor(logits, logits, ranks, ALU.add))
            chain.link(V.tensor_tensor(logits, logits, repeat(con(m, "base0", E), T), ALU.add))
            for k in range(TOPK):
                hk = hot.rearrange("p (t k) e -> p t k e", t=T)[:, :, k, :]
                h2k = hot2.rearrange("p (t k) e -> p t k e", t=T)[:, :, k, :]
                dve.wait_ge(sig("gate_by_expert"), 1)
                chain.link(V.tensor_tensor(h2k, hk, logits, ALU.mult))
            chain.link(V.tensor_reduce(place_k, hot2, AX, ALU.add))
            chain.link(V.tensor_copy(m["dest"].rearrange("p t k -> p (t k)"), place_k))
            le = hot3[:, 0:MAX_EXTRA, :]
            chain.link(V.tensor_tensor(le, repeat(upto, MAX_EXTRA), spread(con(m, "iota16", MAX_EXTRA), E), ALU.is_le))
            chain.link(V.tensor_reduce(ej, le, AX, ALU.add))
            chain.link(V.tensor_scalar(ej, ej, float(E - 1), None, ALU.min))
            chain.link(V.tensor_copy(m["extra_i"][:, 0:MAX_EXTRA], ej))
            chain.link(V.tensor_tensor(le, le, repeat(extra, MAX_EXTRA), ALU.mult))
            chain.link(V.tensor_reduce(bj, le, AX, ALU.add))
            chain.link(V.tensor_tensor(bj, con(m, "iota16", MAX_EXTRA), bj, ALU.subtract))
            chain.link(V.tensor_scalar(m["extra"][:, 0:MAX_EXTRA], bj, 1.0, float(P), ALU.add, ALU.mult))
            chain.link(V.tensor_copy(m["extra_i"][:, MAX_EXTRA:MAX_EXTRA + 1], upto[:, E - 1:E]))
            dve.wait_ge(sig("gateT_turned"), 1)
            V.tensor_copy(gateT.rearrange("p t n -> p (t n)"), bank[5][0:E, :])


def spread(ap, n):
    return ap.unsqueeze(len(ap.shape)).broadcast_to(list(ap.shape) + [n])


def repeat(ap, n):
    return ap.unsqueeze(1).broadcast_to([ap.shape[0], n] + list(ap.shape[1:]))


def load_chunk(sp, a, m, e, c, slot, signal="chunk_loaded"):
    dst = m["ring"][0:P, slot * 2048:(slot + 1) * 2048]
    if c < 8:
        half, k = c // 4, 2 * (c % 4)
        w = a["w_gate_up"][0, e].rearrange("(k p) (g n) -> p k g n", p=P, g=2)
        dst = dst.rearrange("p (k g n) -> p k g n", k=2, g=2)
        for q in range(2):
            sp.dma_start(dst[:, q], w[:, k + q, :, half * 512:(half + 1) * 512]).then_inc(m["sig"](f"{signal}{c}"), 16)
    else:
        k = 2 * (c - 8)
        w = a["w_down"][0, e].rearrange("(k p) n -> p k n", p=P)
        dst = dst.rearrange("p (k n) -> p k n", k=2)
        for q in range(2):
            sp.dma_start(dst[:, q], w[:, k + q, :]).then_inc(m["sig"](f"{signal}{c}"), 16)


def bias_tables(nc, m, keep):
    m["b_gu"] = keep.take(2 * DE, dt=BF16)
    m["pick"] = keep.take(E, dt=BF16)


def expert_places(m, keep):
    f = {}
    f["hot"] = keep.take(T, P, dt=F16)
    f["token"] = keep.take(T, dt=F16)
    f["index"] = keep.take(1, dt=I32)
    f["xg"] = keep.take(D)
    def pair(name):
        at = keep.align()
        f[name] = keep.take(KT, P)
        keep.take(KT, P)
        for n, part in enumerate(("_hi", "_lo")):
            f[name + part] = m["rounded"](name + part, "rest", at + n * D, D).rearrange("p (k n) -> p k n", k=KT)

    pair("xT")
    over = Place(m["rest"], keep.at, REST)
    m["b_raw"], m["b_rem"] = over.take(2 * DE), over.take(2 * DE)
    f["gate"], f["sigm"], f["up"], f["act"] = (keep.take(2, 512) for _ in range(4))
    pair("actT")
    f["y"] = keep.take(D)
    return f


def experts(nc, a, m):
    sig, bank, ring = m["sig"], m["bank"], m["ring"]
    keep = Place(m["rest"], m["free"], REST)
    bias_tables(nc, m, keep)
    f = expert_places(m, keep)
    m["f"] = f
    ident, iota = con(m, "ident", P), con(m, "iota", P)
    b_gu, pick, b_raw, b_rem = m["b_gu"], m["pick"], m["b_raw"], m["b_rem"]
    hot, xg, xT_hi, xT_lo, gate, sigm, up, act_, actT_hi, actT_lo, y = (
        f[n] for n in ("hot", "xg", "xT_hi", "xT_lo", "gate", "sigm", "up", "act", "actT_hi", "actT_lo", "y"))
    spare = keep.take(1)
    assert keep.at <= PARTS_AT
    hi, lo = m["hi"], m["lo"]
    BY_POOL = [sum(q <= c for q in POOL_CHUNKS) for c in range(CHUNKS)]
    BY_VECTOR = [c + 1 - BY_POOL[c] for c in range(CHUNKS)]

    def raw(c):
        return ring[:, (c % RAW) * 2048:(c % RAW + 1) * 2048]

    def wait_lo(eng, e, c):
        if c in POOL_CHUNKS:
            eng.wait_ge(sig("pool_lo_ready"), len(POOL_CHUNKS) * e + BY_POOL[c])
        else:
            eng.wait_ge(sig("lo_ready"), BY_VECTOR[-1] * e + BY_VECTOR[c])

    def make_lo(eng, e, c):
        eng.wait_ge(sig("hi_ready"), CHUNKS * e + c + 1)
        pool = c in POOL_CHUNKS
        (nc.gpsimd if pool else nc.vector).tensor_tensor(lo[c % PARTS], raw(c), hi[c % PARTS].bitcast(F32), ALU.subtract).then_inc(sig("pool_lo_ready" if pool else "lo_ready"), 1)

    def flat(ap, h):
        return ap[:, 4 * h:4 * h + 4, :].rearrange("p k n -> p (k n)")

    with nc.Block() as block:

        @block.sync
        def _(sp):
            for q in range(3):
                sp.dma_start(b_raw[32 * q:32 * q + 32, :], a["b_gate_up"][0]).then_inc(sig("b_raw_loaded"), 16)
            sp.sem_inc(sig("y_stored"), 16)

            def store_rows(e):
                sp.wait_ge(sig("y_ready"), e + 2)
                sp.dma_start(m["y_dram"][bass.ts(e, P), :], y).then_inc(sig("y_stored"), 16)

            for c in range(RAW + EARLY, CHUNKS):
                wait_lo(sp, 0, c - RAW)
                load_chunk(sp, a, m, 0, c, c % RAW)
            with sp.Fori(1, E) as e:
                for c in range(CHUNKS):
                    if c < RAW:
                        wait_lo(sp, e - 1, c + CHUNKS - RAW)
                    else:
                        wait_lo(sp, e, c - RAW)
                    load_chunk(sp, a, m, e, c, c % RAW)
                    if c == CHUNKS - 2:
                        store_rows(e - 1)
            for n in range(2):
                for c in (8 + 2 * n, 9 + 2 * n):
                    wait_lo(sp, E - 1, c)
                load_columns(sp, a, m, n).then_inc(sig(f"slot_loaded{n}"), 16)
            store_rows(E - 1)
            sp.wait_ge(sig("y_stored"), 16 * (E + 1))

        @block.gpsimd
        def _(pool):
            for q in range(3):
                r = slice(32 * q, 32 * q + 32)
                src = con(m, "ident", P)[r, 32 * q:32 * q + 32]
                nc.gpsimd.tensor_copy(pick[r, :], src).then_inc(sig("pick_ready"), 1)
                pool.wait_ge(sig("pick_ready"), q + 1)
            pool.wait_ge(sig("index_ready"), 1)
            gather_rows(pool, m, f).then_inc(sig("rows_loaded"), 16)
            with pool.Fori(0, E) as e:
                pool.wait_ge(sig("index_ready"), e + 2)
                pool.wait_ge(sig("rows_turned"), e + 1)
                pool.sem_inc(sig("gather_begins"), 1)
                gather_rows(pool, m, f).then_inc(sig("rows_loaded"), 16)
                for c in POOL_CHUNKS:
                    make_lo(pool, e, c)
            pool.wait_ge(sig("index_ready"), E + 2)
            pool.wait_ge(sig("rows_turned"), E + 1)
            gather_rows(pool, m, f).then_inc(sig("rows_loaded"), 16)
            pool.wait_ge(sig("rows_loaded"), 16 * (E + 2))

        @block.scalar
        def _(act):
            act.sem_inc(sig("y_ready"), 1)
            act.sem_inc(sig("hi_ready"), EARLY)

            def make_hi(e, c):
                act.wait_ge(sig(f"chunk_loaded{c}"), 32 * e + 32)
                act.wait_ge(sig("chunk_used"), CHUNKS * e + c + 1)
                nc.scalar.activation(hi[c % PARTS], raw(c), ACT.Copy).then_inc(sig("hi_ready"), 1)

            def copy_rows(n):
                for h in range(2):
                    act.wait_ge(sig("rows_turned" if h else "rows_half0"), n)
                    nc.scalar.activation(flat(xT_hi, h), bank[5 - h][:], ACT.Copy).then_inc(sig(f"xT_hi{h}"), 1)

            def copy_act(h, n):
                act.wait_ge(sig(f"act_turned{h}"), n)
                nc.scalar.activation(flat(actT_hi, h), bank[4 + h][:], ACT.Copy).then_inc(sig(f"actT_hi{h}"), 1)

            def sigmoid(h, n):
                act.wait_ge(sig(f"gate_ready{h}"), n)
                nc.scalar.activation(sigm[:, h, :], gate[:, h, :], ACT.Sigmoid, scale=ALPHA).then_inc(sig(f"sigm_ready{h}"), 1)

            def turn(e, last=False):
                nc.scalar.activation(spare[0:1, 0:1], con(m, "ident", 1)[0:1], ACT.Sigmoid)
                for c in (6, 7, 8):
                    make_hi(e, c)
                sigmoid(0, e + 1)
                make_hi(e, 9)
                make_hi(e, 10)
                copy_act(0, e + 1)
                make_hi(e, 11)
                sigmoid(1, e + 1)
                copy_rows(e + 2)
                if not last:
                    make_hi(e + 1, 0)
                if not last:
                    make_hi(e + 1, 1)
                copy_act(1, e + 1)
                if not last:
                    for c in (2, 3, 4):
                        make_hi(e + 1, c)
                act.wait_ge(sig("chunk_used"), CHUNKS * e + CHUNKS + PARTS)
                act.wait_ge(sig("y_stored"), 16 * e + 16)
                nc.scalar.activation(y[:, 0:512], bank[6][:], ACT.Copy)
                nc.scalar.activation(y[:, 512:D], bank[7][:], ACT.Copy).then_inc(sig("y_ready"), 1)
                if not last:
                    make_hi(e + 1, 5)

            for c in range(EARLY, PARTS):
                make_hi(0, c)
            act.wait_ge(sig("b_raw_loaded"), 48)
            nc.scalar.activation(b_gu[0:96, :], b_raw[0:96, :], ACT.Copy).then_inc(sig("b_part0"), 1)
            copy_rows(1)
            act.wait_ge(sig("b_rem0"), 1)
            act.wait_ge(sig("b_part0"), 1)
            nc.scalar.activation(b_gu[32:64, :], b_rem[32:64, :], ACT.Copy)
            nc.scalar.activation(b_gu[64:96, :], b_rem[64:96, :], ACT.Copy).then_inc(sig("b_part1"), 1)
            act.wait_ge(sig("b_rem1"), 1)
            act.wait_ge(sig("b_part1"), 1)
            nc.scalar.activation(b_gu[64:96, :], b_rem[64:96, :], ACT.Copy).then_inc(sig("b_gu_ready"), 1)
            with act.Fori(0, E - 1) as e:
                turn(e)
            turn(E - 1, last=True)

        @block.tensor
        def _(pe):
            pe.sem_inc(sig("chunk_used"), PARTS)

            def list_rows():
                for t in range(T):
                    ins = nc.tensor.matmul(bank[6][:, 0:1], hot[:, t, :], f["token"][:, t:t + 1], start=(t == 0), stop=(t == T - 1))
                ins.then_inc(sig("index_done"), 1)

            def turn_rows(n):
                pe.wait_ge(sig("rows_loaded"), 16 * n)
                for h in range(2):
                    for k in range(4):
                        ins = nc.tensor.transpose(bank[5 - h][:, k * P:(k + 1) * P], xg[:, (4 * h + k) * P:(4 * h + k + 1) * P], ident)
                    ins.then_inc(sig("rows_half0" if h == 0 else "rows_turned"), 1)

            def turn_act(h, n):
                pe.wait_ge(sig(f"act_ready{h}"), n)
                for k in range(4):
                    ins = nc.tensor.transpose(bank[4 + h][:, k * P:(k + 1) * P], act_[:, h, k * P:(k + 1) * P], ident)
                ins.then_inc(sig(f"act_turned{h}"), 1)

            def products(e, c, first, last, rows_hi, rows_lo, outs):
                view = "p (k g n) -> p k g n"
                w_hi, w_lo = (w[c % PARTS].rearrange(view, k=2, g=2) for w in (hi, lo))
                wait_lo(pe, e, c)
                for k in range(2):
                    n = 2 * (c % 4) + k
                    for g in range(2):
                        nc.tensor.matmul(outs[g], rows_hi[:, n, :], w_hi[:, k, g, :], start=(first and k == 0), stop=False, skip_group_check=True)
                        nc.tensor.matmul(outs[g], rows_hi[:, n, :], w_lo[:, k, g, :], start=False, stop=False, skip_group_check=True)
                    for g in range(2):
                        ins = nc.tensor.matmul(outs[g], rows_lo[:, n, :], w_hi[:, k, g, :], start=False, stop=(last and k == 1), skip_group_check=True)
                ins.then_inc(sig("chunk_used"), 1)

            def gate_up(h, e, c):
                products(e, 4 * h + c, c == 0, c == 3, xT_hi, xT_lo, (bank[2 * h][:], bank[2 * h + 1][:]))

            def biases(h, e):
                for g in range(2):
                    o = g * DE + h * 512
                    nc.tensor.matmul(bank[2 * h + g][:], pick[0:96, bass.ds(e, 1)].broadcast_to([96, P]), b_gu[0:96, o:o + 512], start=False, stop=False, skip_group_check=True)

            def down(c, e):
                products(e, 8 + c, c == 0, c == 3, actT_hi, actT_lo, (bank[6][:], bank[7][:]))

            pe.wait_ge(sig("hot_ready"), 1)
            list_rows()
            pe.wait_ge(sig("hot_ready"), 2)
            pe.wait_ge(sig("index_ready"), 1)
            list_rows()
            turn_rows(1)
            pe.wait_ge(sig("pick_ready"), 3)
            with pe.Fori(0, E) as e:
                pe.wait_ge(sig("xT_lo0"), e + 1)
                pe.wait_ge(sig("xT_lo1"), e + 1)
                pe.wait_ge(sig("gu_free0"), e + 1)
                gate_up(0, e, 0)
                gate_up(0, e, 1)
                gate_up(0, e, 2)
                pe.wait_ge(sig("b_gu_ready"), 1)
                biases(0, e)
                gate_up(0, e, 3)
                pe.wait_ge(sig("hot_ready"), e + 3)
                pe.wait_ge(sig("index_ready"), e + 2)
                pe.wait_ge(sig("y_ready"), e + 1)
                list_rows()
                pe.wait_ge(sig("gu_free1"), e + 1)
                gate_up(1, e, 0)
                gate_up(1, e, 1)
                turn_act(0, e + 1)
                gate_up(1, e, 2)
                biases(1, e)
                gate_up(1, e, 3)
                pe.wait_ge(sig("actT_lo0"), e + 1)
                turn_rows(e + 2)
                pe.wait_ge(sig("index_ready"), e + 3)
                down(0, e)
                pe.wait_ge(sig("xT_lo0"), e + 2)
                turn_act(1, e + 1)
                down(1, e)
                pe.wait_ge(sig("actT_lo1"), e + 1)
                down(2, e)
                down(3, e)

        @block.vector
        def _(dve):
            chain = Chain(dve, sig("B_vector_own"))
            V = nc.vector
            dve.sem_inc(sig("lo_ready"), EARLY)
            dve.sem_inc(sig("gu_free0"), 1)
            dve.sem_inc(sig("gu_free1"), 1)
            chain.link(V.tensor_copy(f["token"], con(m, "token", T)))

            def list_of(e):
                for t in range(T):
                    ins = V.tensor_scalar(hot[:, t, :], iota, m["slot"][:, t, bass.ds(e, 1)], None, ALU.is_equal)
                ins.then_inc(sig("hot_ready"), 1)

            def index(n):
                dve.wait_ge(sig("index_done"), n)
                V.tensor_copy(f["index"], bank[6][:, 0:1]).then_inc(sig("index_ready"), 1)

            def activate(h, n):
                dve.wait_ge(sig("chunk_used"), n)
                V.tensor_scalar(gate[:, h, :], bank[2 * h][:], LIMIT, None, ALU.min).then_inc(sig(f"gate_ready{h}"), 1)
                V.tensor_scalar(up[:, h, :], bank[2 * h + 1][:], LIMIT, -LIMIT, ALU.min, ALU.max).then_inc(sig(f"gu_free{h}"), 1)

            def finish(h, e):
                dve.wait_ge(sig(f"gu_free{h}"), e + 2)
                gated = sig(f"gated{h}")
                V.scalar_tensor_tensor(out=up[:, h, :], in0=up[:, h, :], scalar=1.0, in1=gate[:, h, :], op0=ALU.add, op1=ALU.mult).then_inc(gated, 1)
                dve.wait_ge(gated, e + 1)
                dve.wait_ge(sig(f"sigm_ready{h}"), e + 1)
                V.tensor_tensor(act_[:, h, :], up[:, h, :], sigm[:, h, :], ALU.mult).then_inc(sig(f"act_ready{h}"), 1)

            def rows_lo(n):
                for h in range(2):
                    dve.wait_ge(sig(f"xT_hi{h}"), n)
                    V.tensor_tensor(flat(xT_lo, h), bank[5 - h][:], flat(xT_hi, h).bitcast(F32), ALU.subtract).then_inc(sig(f"xT_lo{h}"), 1)

            def act_lo(h, n):
                dve.wait_ge(sig(f"actT_hi{h}"), n)
                V.tensor_tensor(flat(actT_lo, h), bank[4 + h][:], flat(actT_hi, h).bitcast(F32), ALU.subtract).then_inc(sig(f"actT_lo{h}"), 1)

            def turn(e, last=False):
                dve.wait_ge(sig("index_ready"), e + 2)
                list_of(e + 2)
                for c in (6, 7):
                    make_lo(dve, e, c)
                activate(0, CHUNKS * e + 4 + PARTS)
                finish(0, e)
                make_lo(dve, e, 8)
                dve.wait_ge(sig("rows_loaded"), 16 * e + 32)
                index(e + 3)
                make_lo(dve, e, 10)
                act_lo(0, e + 1)
                activate(1, CHUNKS * e + 8 + PARTS)
                finish(1, e)
                rows_lo(e + 2)
                if not last:
                    make_lo(dve, e + 1, 0)
                act_lo(1, e + 1)
                if not last:
                    for c in (1, 2, 3, 4, 5):
                        make_lo(dve, e + 1, c)

            list_of(0)
            index(1)
            list_of(1)
            for c in range(EARLY, PARTS):
                make_lo(dve, 0, c)
            dve.wait_ge(sig("b_part0"), 1)
            V.tensor_tensor(b_rem[0:96, :], b_raw[0:96, :], b_gu[0:96, :], ALU.subtract).then_inc(sig("b_rem0"), 1)
            dve.wait_ge(sig("rows_loaded"), 16)
            index(2)
            rows_lo(1)
            dve.wait_ge(sig("b_part1"), 1)
            V.tensor_tensor(b_rem[64:96, :], b_rem[64:96, :], b_gu[64:96, :], ALU.subtract).then_inc(sig("b_rem1"), 1)
            dve.wait_ge(sig("b_gu_ready"), 1)
            with dve.Fori(0, E - 1) as e:
                turn(e)
            turn(E - 1, last=True)


def gather_rows(pool, m, f):
    return pool.indirect_dma_start(out=f["xg"], out_offset=None, in_=m["h2_dram"],
                                   in_offset=bass.IndirectOffsetOnAxis(ap=f["index"].bitcast(U32), axis=0))


def load_columns(sp, a, m, n):
    dst = m["ring"][:, (n % 3) * 4096:(n % 3 + 1) * 4096].rearrange("p (k n) -> p k n", k=KT)
    return sp.dma_start(dst, a["w_in_2"][0, :, GROUPS2[n]:GROUPS2[n] + 512].rearrange("(k p) n -> p k n", p=P))


def extra_blocks(eng, m):
    return eng.value_load(m["extra_i"][0:1, MAX_EXTRA:MAX_EXTRA + 1], min_val=0, max_val=MAX_EXTRA)


def extra_experts(nc, a, m):
    sig, bank, ring, f = m["sig"], m["bank"], m["ring"], m["f"]
    ident, iota = con(m, "ident", P), con(m, "iota", P)
    hot, xg, xT, gate, sigm, up, act_, actT, y = (f[n] for n in ("hot", "xg", "xT", "gate", "sigm", "up", "act", "actT", "y"))

    def expert(eng, j):
        return eng.value_load(m["extra_i"][0:1, bass.ds(j, 1)], min_val=0, max_val=E - 1)

    with nc.Block() as block:

        @block.sync
        def _(sp):
            n = extra_blocks(sp, m)
            with sp.If(n > 0):
                for q in range(2):
                    sp.wait_ge(sig(f"slot_loaded{q}"), 16)
                for b in range(MAX_EXTRA):
                    sp.dma_start(m["y_dram"][(E + b) * P:(E + b + 1) * P, :], y).then_inc(sig("X_filled"), 16)
                sp.wait_ge(sig("X_filled"), 16 * MAX_EXTRA)
                sp.sem_inc(sig("X_fill_done"), 1)
                with sp.Fori(0, n) as j:
                    sp.wait_ge(sig("X_down_done"), j + 1)
                    e = expert(sp, j)
                    for c in range(CHUNKS):
                        load_chunk(sp, a, m, e, c, c, "X_chunk_loaded")
                sp.wait_ge(sig("X_down_done"), n + 1)
                for q in range(2):
                    load_columns(sp, a, m, q).then_inc(sig("X_slots_loaded"), 16)
                sp.wait_ge(sig("X_slots_loaded"), 32)

        @block.gpsimd
        def _(pool):
            n = extra_blocks(pool, m)
            with pool.If(n > 0):
                with pool.Fori(0, n) as j:
                    pool.wait_ge(sig("X_index_ready"), j + 1)
                    pool.sem_inc(sig("X_gather_begins"), 1)
                    gather_rows(pool, m, f).then_inc(sig("X_rows_loaded"), 16)

        @block.scalar
        def _(act):
            n = extra_blocks(act, m)
            act.sem_inc(sig("X_y_ready"), 1)
            with act.If(n > 0):
                with act.Fori(0, n) as j:
                    for h in range(2):
                        act.wait_ge(sig(f"X_rows_turned{h}"), j + 1)
                        nc.scalar.activation(xT[:, 4 * h:4 * h + 4, :].rearrange("p k n -> p (k n)"), bank[4 + h][:], ACT.Copy).then_inc(sig(f"X_xT_ready{h}"), 1)
                    for h in range(2):
                        act.wait_ge(sig(f"X_gate_ready{h}"), j + 1)
                        nc.scalar.activation(sigm[:, h, :], gate[:, h, :], ACT.Sigmoid, scale=ALPHA).then_inc(sig(f"X_sigm_ready{h}"), 1)
                    for h in range(2):
                        act.wait_ge(sig(f"X_act_turned{h}"), j + 1)
                        nc.scalar.activation(actT[:, 4 * h:4 * h + 4, :].rearrange("p k n -> p (k n)"), bank[4 + h][:], ACT.Copy).then_inc(sig(f"X_actT_ready{h}"), 1)
                    act.wait_ge(sig("X_fill_done"), 1)
                    act.wait_ge(sig("X_down_done"), j + 2)
                    nc.scalar.activation(y[:, 0:512], bank[6][:], ACT.Copy)
                    nc.scalar.activation(y[:, 512:D], bank[7][:], ACT.Copy).then_inc(sig("X_y_ready"), 1)
                    act.wait_ge(sig("X_y_ready"), j + 2)
                    act.dma_start(m["y_dram"][bass.ds((j + E) * P, P), :], y).then_inc(sig("X_y_stored"), 16)
                    act.wait_ge(sig("X_y_stored"), 16 * j + 16)

        @block.tensor
        def _(pe):
            n = extra_blocks(pe, m)
            pe.sem_inc(sig("X_down_done"), 1)
            with pe.If(n > 0):
                with pe.Fori(0, n) as j:
                    e = expert(pe, j)
                    pe.wait_ge(sig("X_hot_ready"), j + 1)
                    pe.wait_ge(sig("X_y_ready"), j + 1)
                    for t in range(T):
                        ins = nc.tensor.matmul(bank[6][:, 0:1], hot[:, t, :], f["token"][:, t:t + 1], start=(t == 0), stop=(t == T - 1))
                    ins.then_inc(sig("X_index_done"), 1)
                    pe.wait_ge(sig("X_rows_loaded"), 16 * j + 16)
                    for h in range(2):
                        for k in range(4):
                            ins = nc.tensor.transpose(bank[4 + h][:, k * P:(k + 1) * P], xg[:, (4 * h + k) * P:(4 * h + k + 1) * P], ident)
                        ins.then_inc(sig(f"X_rows_turned{h}"), 1)
                    for h in range(2):
                        pe.wait_ge(sig(f"X_xT_ready{h}"), j + 1)
                    for h in range(2):
                        for g in range(2):
                            o = g * DE + h * 512
                            nc.tensor.matmul(bank[2 * h + g][:], m["pick"][0:96, bass.ds(e, 1)].broadcast_to([96, P]), m["b_gu"][0:96, o:o + 512], start=True, stop=False, skip_group_check=True)
                        for c in range(4):
                            w = ring[:, (4 * h + c) * 2048:(4 * h + c + 1) * 2048].rearrange("p (k g n) -> p k g n", k=2, g=2)
                            pe.wait_ge(sig(f"X_chunk_loaded{4 * h + c}"), 32 * j + 32)
                            for k in range(2):
                                for g in range(2):
                                    ins = nc.tensor.matmul(bank[2 * h + g][:], xT[:, 2 * c + k, :], w[:, k, g, :], start=False, stop=(c == 3 and k == 1), skip_group_check=True)
                        ins.then_inc(sig(f"X_gate_up_done{h}"), 1)
                    for h in range(2):
                        pe.wait_ge(sig(f"X_act_ready{h}"), j + 1)
                        for k in range(4):
                            ins = nc.tensor.transpose(bank[4 + h][:, k * P:(k + 1) * P], act_[:, h, k * P:(k + 1) * P], ident)
                        ins.then_inc(sig(f"X_act_turned{h}"), 1)
                    pe.wait_ge(sig("X_index_ready"), j + 1)
                    for c in range(4):
                        if c % 2 == 0:
                            pe.wait_ge(sig(f"X_actT_ready{c // 2}"), j + 1)
                        w = ring[:, (8 + c) * 2048:(9 + c) * 2048].rearrange("p (k n) -> p k n", k=2)
                        pe.wait_ge(sig(f"X_chunk_loaded{8 + c}"), 32 * j + 32)
                        for k in range(2):
                            for q in range(2):
                                ins = nc.tensor.matmul(bank[6 + q][:], actT[:, 2 * c + k, :], w[:, k, q * 512:(q + 1) * 512],
                                                       start=(c == 0 and k == 0), stop=(c == 3 and k == 1), skip_group_check=True)
                    ins.then_inc(sig("X_down_done"), 1)

        @block.vector
        def _(dve):
            V = nc.vector
            n = extra_blocks(dve, m)
            with dve.If(n > 0):
                with dve.Fori(0, n) as j:
                    e = expert(dve, j)
                    for t in range(T):
                        ins = V.tensor_scalar(hot[:, t, :], iota, m["extra"][:, bass.ds(j, 1)], m["slot"][:, t, bass.ds(e, 1)], ALU.add, ALU.is_equal)
                    ins.then_inc(sig("X_hot_ready"), 1)
                    dve.wait_ge(sig("X_index_done"), j + 1)
                    V.tensor_copy(f["index"], bank[6][:, 0:1]).then_inc(sig("X_index_ready"), 1)
                    for h in range(2):
                        dve.wait_ge(sig(f"X_gate_up_done{h}"), j + 1)
                        V.tensor_scalar(gate[:, h, :], bank[2 * h][:], LIMIT, None, ALU.min).then_inc(sig(f"X_gate_ready{h}"), 1)
                        V.tensor_scalar(up[:, h, :], bank[2 * h + 1][:], LIMIT, -LIMIT, ALU.min, ALU.max).then_inc(sig(f"X_up_ready{h}"), 1)
                        dve.wait_ge(sig(f"X_up_ready{h}"), j + 1)
                        dve.wait_ge(sig(f"X_gate_ready{h}"), j + 1)
                        V.scalar_tensor_tensor(out=up[:, h, :], in0=up[:, h, :], scalar=1.0, in1=gate[:, h, :], op0=ALU.add, op1=ALU.mult).then_inc(sig(f"X_gated{h}"), 1)
                        dve.wait_ge(sig(f"X_gated{h}"), j + 1)
                        dve.wait_ge(sig(f"X_sigm_ready{h}"), j + 1)
                        V.tensor_tensor(act_[:, h, :], up[:, h, :], sigm[:, h, :], ALU.mult).then_inc(sig(f"X_act_ready{h}"), 1)


def second_block(nc, a, m, out):
    sig, bank, ring, rest, x = m["sig"], m["bank"], m["ring"], m["rest"], m["x"]
    ident, ones, upper = con(m, "ident", P), con(m, "ones", P), con(m, "upper", P)
    strict, negmask = con(m, "strict", P), con(m, "negmask", P)

    front = Place(ring, 0, 3 * 4096)
    slots = [front.take(KT, 512) for _ in range(3)]
    front = Place(ring, 0, 3 * 4096)
    LT, AT, kg, qgT, u_sb, wT = (front.take(T, HA, P) for _ in range(6))
    state = LT[:, 0].rearrange("p h n -> p (h n)").rearrange("p (h n) -> p h n", h=HA)
    v_new = LT[:, 1]
    o_square, o_var, o_inv, o_tmp = kg, qgT, u_sb, wT
    mid = Place(ring, 3 * 4096, 4 * 4096)
    hT = mid.take(KT, S)
    mid = Place(ring, 3 * 4096, 4 * 4096)
    inverse, inverseT = mid.take(T, HA, P), mid.take(T, HA, P)
    mid = Place(ring, 3 * 4096, 4 * 4096)
    mixT = mid.take(KT, S)
    back = Place(ring, 4 * 4096, RING)
    qkvT = back.take(12, S)
    iqT = back.take(4, S)
    back = Place(ring, 4 * 4096 + 12 * S, RING)
    step_L, cross = back.take(2, HA, P), back.take(2, HA, P)
    diff, decay_row = step_L, cross
    back = Place(ring, 4 * 4096, RING)
    w_out = back.take(KT, D)

    keep = Place(rest, m["first_free"], REST)
    rows = [ring[:, 3 * 4096 + n * D:3 * 4096 + (n + 1) * D] for n in range(12)] + [keep.take(D) for _ in range(4)]
    w_small = keep.take(KT, 208)
    tables = Place(rest, keep.at - KT * 208, keep.at)
    levels, w_uv = tables.take(8, P), tables.take(HB, P)
    z_a, z_b = keep.take(HA, S), keep.take(HB, S)
    xn = rest[:, keep.at - 4096:keep.at].rearrange("p (t d) -> p t d", t=T)
    over_rows = Place(rest, m["first_free"], m["first_free"] + 4 * D)
    q_bT, oT = over_rows.take(HB, S), over_rows.take(HA, S)
    ikT, ckvT, ckv = keep.take(S), keep.take(S), keep.take(T, P)
    score = [None] + [keep.take((t + 1) * P) for t in range(1, T)]
    relu = keep.take(2, S)
    g_final = rest[:, keep.at - D:keep.at]
    taps = keep.take(2, S + 4)
    square = keep.take(2, S)
    var, inv, tmp = keep.take(S), keep.take(S), keep.take(S)
    bias = keep.take(HB, S)
    probsT = keep.take(2, S)
    small = keep.take(T, 16)
    g_kv = keep.take(P)
    beta, g, gc, eg, egl, gl, bg, s1, s2, s3 = (keep.take(T, 4) for _ in range(10))
    a_log, dt_bias = keep.take(4), keep.take(4)
    w_index = keep.take(T, HI)
    ss, ssv, ssi, sst, ss2 = (keep.take(T) for _ in range(5))
    best = keep.take(8)
    half = keep.take(1)
    rowmax, rowsum, rowinv = (keep.take(16) for _ in range(3))
    bucket_rows = rest[0:BUCKETS, m["first_free"] + 2048:m["first_free"] + 2048 + S + P]
    rel_bias = rest[0:BUCKETS, m["first_free"] + 3072:m["first_free"] + 3076]
    bias_row = rest[0:HB, m["first_free"] + 3200:m["first_free"] + 3200 + S + P]
    bias_sum, logits, probs = relu, taps[:, :, 0:S], square
    SCALE_B = P ** -0.5
    N_B = T * HB

    def heads(b):
        return bank[b][:].rearrange("p (h n) -> p h n", h=HA)

    def flat(ap, h):
        return ap[:, h].rearrange("p h n -> p (h n)")

    def delta_chunk(i, step):
        t, at = divmod(i - 4, 3)
        return t if at == step and 0 <= t < T else None

    with nc.Block() as block:

        @block.sync
        def _(sp):
            sp.dma_start(g_final, a["g_final"].rearrange("(o n) -> o n", o=1).partition_broadcast(P)).then_inc(sig("g_final_loaded"), 16)
            sp.wait_ge(sig("combined"), 3 * TOPK)
            sp.dma_start(w_small[:, :, 0:72], a["w_in_2"][0, :, 3720:3792].rearrange("(k p) n -> p k n", p=P)).then_inc(sig("w_small_loaded"), 16)
            sp.dma_start(w_small[:, :, 72:80], a["w_in_2"][0, :, 2048:2056].rearrange("(k p) n -> p k n", p=P)).then_inc(sig("w_small_loaded"), 16)
            sp.dma_start(w_small[:, :, 80:208], a["w_in_2"][0, :, 2568:2696].rearrange("(k p) n -> p k n", p=P)).then_inc(sig("w_small_loaded"), 16)
            sp.dma_start(g_kv, a["g_kv_2"].partition_broadcast(P)).then_inc(sig("g_kv_loaded"), 16)
            sp.dma_start(a_log, a["a_log_2"].partition_broadcast(P)).then_inc(sig("decay_loaded"), 16)
            sp.dma_start(dt_bias, a["dt_bias_2"].partition_broadcast(P)).then_inc(sig("decay_loaded"), 16)
            for n in range(2, len(GROUPS2)):
                if n >= 3:
                    sp.wait_ge(sig("tile_done"), 4 * (n - 2) + (1 if n > 3 else 0))
                load_columns(sp, a, m, n).then_inc(sig(f"slot_loaded{n % 3}"), 16)
                if n == 2:
                    sp.wait_ge(sig("combined"), 16)
                    sp.dma_start(bucket_rows, a["buckets"]).then_inc(sig("buckets_loaded"), 16)
                    sp.dma_start(rel_bias, a["rel_bias_2"]).then_inc(sig("buckets_loaded"), 16)
                    sp.wait_ge(sig("bias_row_ready"), 1)
                    sp.dma_start(m["bias_dram"], bias_row).then_inc(sig("bias_stored"), 16)
                    sp.wait_ge(sig("bias_stored"), 16)
                    for h in range(HB):
                        src = bass.AP(m["bias_dram"].tensor, h * (S + P), [[1, P], [1, S]])
                        sp.dma_start(bias[:, h, :], src).then_inc(sig("bias_loaded"), 16)
                if n == 3:
                    sp.wait_ge(sig("small_done"), 2)
                    sp.wait_ge(sig("tile_done"), 5)
                    sp.dma_start(levels, a["levels"].rearrange("p (n c) -> p n c", n=8)).then_inc(sig("levels_loaded"), 16)
                    sp.dma_start(w_uv, a["w_uv_2"][0].rearrange("h r d -> r h d")).then_inc(sig("w_uv_loaded"), 16)
            sp.wait_ge(sig("chunks_ready"), T)
            sp.wait_ge(sig("qg_ready"), T)
            sp.wait_ge(sig("kv_turned"), T)
            for k in range(KT):
                if k == 6:
                    sp.wait_ge(sig("inverseT_step"), 7 * T)
                sp.dma_start(w_out[:, k, :], a["w_out_2"][0, k * P:(k + 1) * P, :]).then_inc(sig("w_out_loaded"), 16)
            for t in range(T):
                sp.wait_ge(sig("x_out"), t + 1)
                sp.dma_start(out[0, t * P:(t + 1) * P, :], x[:, t, :]).then_inc(sig("out_stored"), 16)
            sp.wait_ge(sig("out_stored"), 16 * T)

        @block.gpsimd
        def _(pool):
            chain = Chain(pool, sig("D_pool_own"))

            def gather_results(results):
                for n in range(T * TOPK):
                    t, k = n // TOPK, n % TOPK
                    if n == 12:
                        pool.wait_ge(sig("expert_bias_done"), 2 * T)
                    pool.indirect_dma_start(out=rows[n], out_offset=None, in_=results,
                                            in_offset=bass.IndirectOffsetOnAxis(ap=m["dest"][:, t, k:k + 1].bitcast(U32), axis=0)).then_inc(sig(f"rows_loaded{t}"), 16)

            with pool.If(extra_blocks(pool, m) > 0):
                gather_results(m["y_dram"])
            with pool.Else():
                gather_results(m["y_dram"][0:E * P, :])
            pool.wait_ge(sig("half_ready"), 1)

            def root_of(v, y):
                return nc.gpsimd.tensor_tensor(y, v, half.broadcast_to([P, v.shape[1]]), ALU.pow)

            for i in range(2):
                for t in range(T):
                    c = slice(t, t + 1)
                    pool.wait_ge(sig(f"squares{i}"), t + 1)
                    chain.link(nc.gpsimd.tensor_scalar(ssv[:, c], (ss, ss2)[i][:, c], 1.0 / D, EPS, ALU.mult, ALU.add))
                    root_of(ssv[:, c], (ssi, sst)[i][:, c]).then_inc(sig(f"root{i}"), 1)
            pool.wait_ge(sig("var_ready"), 1)
            root_of(ssv, ssi).then_inc(sig("ckv_root"), 1)
            nc.gpsimd.memset(taps[:, 0, 0:3], 0.0)
            nc.gpsimd.memset(taps[:, 1, 0:3], 0.0).then_inc(sig("taps_zero"), 1)
            for t in range(T):
                pool.wait_ge(sig("decay_ready"), t + 1)
                if t >= 1:
                    pool.wait_ge(sig("chunks_ready"), t)
                d = diff[:, t % 2]
                nc.gpsimd.tensor_tensor(inv.rearrange("p (h n) -> p h n", h=HA), d, repeat(strict, HA), ALU.mult).then_inc(sig("strict_ready"), 1)
                nc.gpsimd.tensor_tensor(tmp.rearrange("p (h n) -> p h n", h=HA), d, repeat(upper, HA), ALU.mult).then_inc(sig("upper_ready"), 1)
            pool.wait_ge(sig("levels_loaded"), 16)
            for n in range(7):
                for t in range(T):
                    i = n * T + t
                    if i == 0:
                        pool.wait_ge(sig("chunks_ready"), T)
                        pool.wait_ge(sig("upper_ready"), T)
                        pool.wait_ge(sig("strict_ready"), T)
                    if i >= 2:
                        pool.wait_ge(sig("cross_done"), i - 1)
                    nc.gpsimd.tensor_tensor(step_L[:, i % 2], LT[:, t], repeat(levels[:, n, :], HA), ALU.mult).then_inc(sig("step_ready"), 1)
            for i in range(N_B):
                t, h = i // HB, i % HB
                n = (t + 1) * P
                if i >= 2:
                    pool.wait_ge(sig("logits_ready"), i - 1)
                else:
                    pool.wait_ge(sig("bias_turned"), HB)
                    pool.wait_ge(sig("chosen"), 3)
                mask = negmask if t == 0 else score[t]
                nc.gpsimd.tensor_tensor(bias_sum[:, i % 2, 0:n], bias[:, h, 3 * P - t * P:3 * P - t * P + n], mask, ALU.add).then_inc(sig("bias_sum_ready"), 1)
            for t in range(T):
                pool.wait_ge(sig("post_var"), t + 1)
                root_of(ssv[:, t:t + 1], ssi[:, t:t + 1]).then_inc(sig("post_root"), 1)

        @block.scalar
        def _(act):
            chain = Chain(act, sig("D_scalar_own"))
            A = nc.scalar

            def rsqrt(k, y, v):
                act.wait_ge(sig("var_ready"), k + 1)
                chain.link(A.activation(y, v, ACT.Ln))
                A.activation(y, y, ACT.Exp, scale=-0.5).then_inc(sig("rsqrt_ready"), 1)

            for t in range(T):
                act.wait_ge(sig("combined"), TOPK * (t + 1))
                chain.link(A.activation(xn[:, t, :], x[:, t, :], ACT.Square, accum_out=ss[:, t:t + 1]))
                A.sem_inc(sig("squares0"), 1)
            for t in range(T):
                act.wait_ge(sig("x_normed"), t + 1)
                chain.link(A.activation(xn[:, t, :], x[:, t, :], ACT.Square, accum_out=ss2[:, t:t + 1]))
                A.sem_inc(sig("squares1"), 1)
            for k in range(KT):
                act.wait_ge(sig("hT_turned"), k + 1)
                A.activation(hT[:, k, :], bank[k % 2][:], ACT.Identity, bias=m["mod_shift"][:, k:k + 1], scale=m["mod_scale"][:, k:k + 1]).then_inc(sig("hT_ready"), 1)
            act.wait_ge(sig("bias_row_done"), 1)
            A.activation(bias_row[:, 0:S], bank[7][0:HB, :], ACT.Copy)
            A.activation(bias_row[:, S:S + P], bank[6][0:HB, 0:P], ACT.Copy).then_inc(sig("bias_row_ready"), 1)
            for n in range(5):
                act.wait_ge(sig("tile_done"), n + 1)
                if n < 4:
                    A.activation(iqT[:, n, :], bank[n % 2][:], ACT.Copy).then_inc(sig("tile_read"), 1)
                else:
                    A.activation(ikT[0:64, :], bank[0][0:64, :], ACT.Copy)
                    A.activation(ikT[64:128, :], bank[0][0:64, :], ACT.Copy).then_inc(sig("tile_read"), 1)
            act.wait_ge(sig("small_done"), 2)
            A.activation(small[:, 0:3, :], bank[6][:, 0:432].rearrange("p (t n) -> p t n", t=3)[:, :, 0:16], ACT.Copy)
            chain.link(A.activation(small[:, 3, :], bank[7][:, 0:16], ACT.Copy))
            A.sem_inc(sig("small_ready"), 1)
            for t in range(T):
                src = bank[6 + t // 3][:, (t % 3) * 144 + 16:(t % 3) * 144 + 144]
                ins = A.activation(square[:, 0, t * P:(t + 1) * P], src, ACT.Square, accum_out=ss[:, t:t + 1])
            chain.link(ins)
            A.sem_inc(sig("ckv_squares"), 1)
            for i in range(3 * HI):
                t = 1 + i // HI
                n = (t + 1) * P
                if i == 10:
                    act.wait_ge(sig("ckv_turned"), 1)
                    A.activation(ckvT, bank[4][:], ACT.Copy).then_inc(sig("ckvT_ready"), 1)
                act.wait_ge(sig("index_done"), i + 1)
                if i >= 2:
                    act.wait_ge(sig("relu_read"), i - 1)
                if i == 0:
                    act.wait_ge(sig("x_normed"), T)
                A.activation(relu[:, i % 2, 0:n], bank[2 + i % 2][:, 0:n], ACT.Relu).then_inc(sig("relu_ready"), 1)
            act.wait_ge(sig("ab_ready"), 1)
            A.activation(beta, small[:, :, 8:12], ACT.Exp, scale=-1.0).then_inc(sig("b_exp"), 1)
            act.wait_ge(sig("decay_loaded"), 32)
            A.activation(a_log, a_log, ACT.Exp).then_inc(sig("a_exp"), 1)
            A.activation(s2, s2, ACT.Exp, scale=-1.0).then_inc(sig("ab_exp"), 1)
            act.wait_ge(sig("taps_zero"), 1)

            def tail_of(n):
                act.wait_ge(sig("conv_ready"), n + 1)
                act.wait_ge(sig("relu_read"), 3 * HI)
                A.activation(relu[:, n % 2, :], qkvT[:, n, :], ACT.Sigmoid).then_inc(sig("conv_sigm"), 1)
                if n < 8:
                    act.wait_ge(sig("silu_ready"), n + 1)
                    if n >= 2:
                        act.wait_ge(sig("qk_summed"), n - 1)
                    A.activation(square[:, n % 2, :], qkvT[:, n, :], ACT.Square).then_inc(sig("qk_squared"), 1)

            for n in range(12):
                act.wait_ge(sig("tile_done"), 6 + n)
                if n >= 2:
                    act.wait_ge(sig("conv_ready"), n - 1)
                A.activation(taps[:, n % 2, 3:S + 3], bank[(5 + n) % 2][:], ACT.Copy).then_inc(sig("tile_read"), 1)
                tail_of(n)
                if n >= 1 and n - 1 < 8:
                    rsqrt(n, inv, var)
            for n in range(12):
                i = 17 + n
                act.wait_ge(sig("tile_done"), i + 1)
                dst = (q_bT, z_a, z_b)[n // 4][:, n % 4, :]
                A.activation(dst, bank[i % 2][:], ACT.Copy).then_inc(sig("tile_read"), 1)
                if n >= 4:
                    j = n - 4
                    if j >= 2:
                        act.wait_ge(sig("z_ready"), j - 1)
                    act.wait_ge(sig("tile_read"), i + 1)
                    act.wait_ge(sig("qk_summed"), 8)
                    A.activation(square[:, j % 2, :], dst, ACT.Sigmoid).then_inc(sig("z_sigm"), 1)
            for h in range(HB):
                act.wait_ge(sig("bias_done"), h + 1)
                A.activation(bias[:, h, :], bank[4 + h % 2][:], ACT.Copy).then_inc(sig("bias_turned"), 1)
            for t in range(T):
                act.wait_ge(sig("diff_ready"), t + 1)
                if t >= 2:
                    act.wait_ge(sig("qg_ready"), t - 1)
                A.activation(decay_row[:, t % 2], bank[0 + 4 * (t % 2)][:].rearrange("p (h n) -> p h n", h=HA), ACT.Exp).then_inc(sig("decay_row_ready"), 1)
                A.activation(diff[:, t % 2], diff[:, t % 2], ACT.Exp).then_inc(sig("decay_ready"), 1)
                A.activation(egl[:, t, :], egl[:, t, :], ACT.Exp).then_inc(sig("egl_ready"), 1)
                if t == 0:
                    act.wait_ge(sig("gc_ready"), 1)
                    A.activation(eg, gc, ACT.Exp).then_inc(sig("eg_ready"), 1)
            for i in range(7 * T):
                act.wait_ge(sig("cross_done"), i + 1)
                if i >= 2:
                    act.wait_ge(sig("joined"), i - 1)
                else:
                    act.wait_ge(sig("qg_ready"), T)
                A.activation(cross[:, i % 2], bank[i % 2][:].rearrange("p (h n) -> p h n", h=HA), ACT.Copy).then_inc(sig("cross_ready"), 1)
            for t in range(T):
                act.wait_ge(sig("uw_done"), t + 1)
                A.activation(wT[:, t], bank[2 + t % 2][:].rearrange("p (h n) -> p h n", h=HA), ACT.Copy).then_inc(sig("wT_ready"), 1)
            for i in range(N_B):
                t = i // HB
                n = (t + 1) * P
                if delta_chunk(i, 2) is not None:
                    d = delta_chunk(i, 2)
                    act.wait_ge(sig("o_done"), d + 1)
                    A.activation(oT[:, :, d * P:(d + 1) * P], bank[2][:].rearrange("p (h n) -> p h n", h=HA), ACT.Copy).then_inc(sig("oT_ready"), 1)
                act.wait_ge(sig("rowmax_ready"), i + 1)
                if i >= 2:
                    act.wait_ge(sig("probs_turned"), i - 1)
                A.activation(probs[:, i % 2, 0:n], logits[:, i % 2, 0:n], ACT.Exp, bias=rowmax[:, i:i + 1], accum_out=rowsum[:, i:i + 1]).then_inc(sig("probs_exp"), 1)
                if i >= 1:
                    j = i - 1
                    nj = (j // HB + 1) * P
                    act.wait_ge(sig("probs_turned"), j + 1)
                    if j >= 2:
                        act.wait_ge(sig("weighed"), j - 1)
                    A.activation(probsT[:, j % 2, 0:nj], bank[5][:, 0:nj], ACT.Copy).then_inc(sig("probsT_ready"), 1)
            j = N_B - 1
            act.wait_ge(sig("probs_turned"), j + 1)
            act.wait_ge(sig("weighed"), j - 1)
            A.activation(probsT[:, j % 2, 0:S], bank[5][:, 0:S], ACT.Copy).then_inc(sig("probsT_ready"), 1)
            act.wait_ge(sig("oT_ready"), T)
            for h in range(HA):
                A.activation(flat(o_square, h), oT[:, h, :], ACT.Square).then_inc(sig("o_squared"), 1)
            for h in range(HA):
                act.wait_ge(sig("var_ready"), 10 + h)
                A.activation(flat(o_inv, h), flat(o_var, h), ACT.Ln).then_inc(sig("o_logs"), 1)
            for h in range(HA):
                act.wait_ge(sig("o_logs"), h + 1)
                A.activation(flat(o_inv, h), flat(o_inv, h), ACT.Exp, scale=-0.5).then_inc(sig("rsqrt_ready"), 1)
            for t in range(T):
                for c in range(2):
                    act.wait_ge(sig("mix_done"), 2 * t + c + 1)
                    A.activation(square[:, c, :], bank[2 * (t % 2) + c][:], ACT.Square, accum_out=(ss, ss2)[c][:, t:t + 1]).then_inc(sig("mix_squared"), 1)
                    act.wait_ge(sig("mix_squared"), 2 * t + c + 1)

        @block.tensor
        def _(pe):
            M = nc.tensor
            for n in range(2 * T):
                M.matmul(bank[n][:], m["gateT"][:, n // 2, :], m["b_down"][:, (n % 2) * 512:(n % 2 + 1) * 512], start=True, stop=True).then_inc(sig("expert_bias_done"), 1)
            for k in range(KT):
                if k >= 2:
                    pe.wait_ge(sig("hT_ready"), k - 1)
                for t in range(T):
                    if k == 0:
                        pe.wait_ge(sig("xn_ready"), t + 1)
                    ins = M.transpose(bank[k % 2][:, t * P:(t + 1) * P], xn[:, t, k * P:(k + 1) * P], ident)
                ins.then_inc(sig("hT_turned"), 1)
            pe.wait_ge(sig("buckets_loaded"), 32)
            M.matmul(bank[7][0:HB, :], rel_bias, bucket_rows[:, 0:S], start=True, stop=True)
            M.matmul(bank[6][0:HB, 0:P], rel_bias, bucket_rows[:, S:S + P], start=True, stop=True).then_inc(sig("bias_row_done"), 1)
            pe.wait_ge(sig("hT_ready"), KT)

            def tile(i, w, c0, n):
                if i >= 2:
                    pe.wait_ge(sig("tile_read"), i - 1)
                for k in range(KT):
                    ins = M.matmul(bank[i % 2][0:n, :], w[:, k, c0:c0 + n], hT[:, k, :], start=(k == 0), stop=(k == KT - 1))
                ins.then_inc(sig("tile_done"), 1)

            def group(n, i):
                pe.wait_ge(sig(f"slot_loaded{n % 3}"), 16 * (n // 3 + 1))
                for c in range(4):
                    tile(i + c, slots[n % 3], c * P, P)
                    yield c

            for _ in group(0, 0):
                pass
            pe.wait_ge(sig("w_small_loaded"), 48)
            tile(4, w_small, 0, DI)
            pe.wait_ge(sig("bias_row_ready"), 1)
            for t in range(T):
                o = bank[6 + t // 3][:, (t % 3) * 144:(t % 3) * 144 + 144]
                for k in range(KT):
                    ins = M.matmul(o, hT[:, k, t * P:(t + 1) * P], w_small[:, k, DI:208], start=(k == 0), stop=(k == KT - 1), skip_group_check=True)
                if t >= 2:
                    ins.then_inc(sig("small_done"), 1)
            pe.wait_ge(sig("tile_read"), 5)
            for i in range(3 * HI):
                t, h = 1 + i // HI, i % HI
                r = slice(64 * (h % 2), 64 * (h % 2) + 64)
                if i >= 2:
                    pe.wait_ge(sig("relu_ready"), i - 1)
                if i == 10:
                    pe.wait_ge(sig("ckv_ready"), 1)
                    for q in range(T):
                        ins = M.transpose(bank[4][:, q * P:(q + 1) * P], ckv[:, q, :], ident)
                    ins.then_inc(sig("ckv_turned"), 1)
                M.matmul(bank[2 + i % 2][:, 0:(t + 1) * P], iqT[r, h // 2, t * P:(t + 1) * P], ikT[r, 0:(t + 1) * P], start=True, stop=True).then_inc(sig("index_done"), 1)

            pe.wait_ge(sig("small_ready"), 1)

            def qk_sum(n):
                pe.wait_ge(sig("qk_squared"), n + 1)
                if n >= 1:
                    pe.wait_ge(sig("var_ready"), 1 + n)
                M.matmul(bank[7][:], ones, square[:, n % 2, :], start=True, stop=True).then_inc(sig("qk_summed"), 1)

            for gr in range(3):
                for c in group(1 + gr, 5 + 4 * gr):
                    n = 4 * gr + c
                    if 1 <= n <= 8:
                        qk_sum(n - 1)
            for gr in range(3):
                for c in group(4 + gr, 17 + 4 * gr):
                    pass
            pe.wait_ge(sig("levels_loaded"), 16)
            pe.wait_ge(sig("bias_loaded"), 64)
            pe.wait_ge(sig("ckvT_ready"), 1)
            for h in range(HB):
                if h >= 2:
                    pe.wait_ge(sig("bias_turned"), h - 1)
                M.matmul(bank[4 + h % 2][:], levels[:, 7, :], bias[:, h, :], start=True, stop=True).then_inc(sig("bias_done"), 1)
            pe.wait_ge(sig("g_ready"), 1)
            for t in range(T):
                ins = M.matmul(bank[6][:, 4 * t:4 * t + 4], upper, g[:, t, :], start=True, stop=True, skip_group_check=True)
            ins.then_inc(sig("gc_done"), 1)
            pe.wait_ge(sig("tile_read"), 29)
            pe.wait_ge(sig("qk_normed"), 8)
            pe.wait_ge(sig("relu_ready"), 3 * HI)
            pe.wait_ge(sig("bias_turned"), HB)
            pe.wait_ge(sig("silu_ready"), 12)
            pe.wait_ge(sig("gc_ready"), 1)

            def chunk_products(t):
                b0, b1 = 4 * (t % 2), 4 * (t % 2) + 1
                c = slice(t * P, (t + 1) * P)
                if t >= 1:
                    pe.wait_ge(sig("chunks_ready"), t)
                    pe.wait_ge(sig("kv_chunk_ready"), t)
                if t >= 2:
                    pe.wait_ge(sig("decay_row_ready"), t - 1)
                for h in range(HA):
                    o = slice(h * P, (h + 1) * P)
                    M.matmul(bank[b0][:, o], g[:, t, h:h + 1].broadcast_to([P, P]), upper, start=True, stop=True, skip_group_check=True)
                    ins = M.matmul(bank[b1][:, o], beta[:, t, h:h + 1].broadcast_to([P, P]), ident, start=True, stop=True, skip_group_check=True)
                ins.then_inc(sig("rows_done"), 1)
                for h in range(HA):
                    o = slice(h * P, (h + 1) * P)
                    M.matmul(bank[2][:, o], qkvT[:, 4 + h, c], qkvT[:, 4 + h, c], start=True, stop=True, skip_group_check=True)
                    ins = M.matmul(bank[3][:, o], qkvT[:, 4 + h, c], qkvT[:, h, c], start=True, stop=True, skip_group_check=True)
                ins.then_inc(sig("kk_done"), 1)
                for h in range(HA):
                    o = slice(h * P, (h + 1) * P)
                    M.transpose(bank[6][:, o], qkvT[:, 4 + h, c], ident)
                    ins = M.transpose(bank[7][:, o], qkvT[:, 8 + h, c], ident)
                ins.then_inc(sig("kv_turned"), 1)

            for t in range(T):
                chunk_products(t)
            pe.wait_ge(sig("chunks_ready"), T)
            pe.wait_ge(sig("kv_chunk_ready"), T)
            pe.wait_ge(sig("decay_row_ready"), T)
            for n in range(7):
                for t in range(T):
                    i = n * T + t
                    if i >= 2:
                        pe.wait_ge(sig("cross_ready"), i - 1)
                    pe.wait_ge(sig("step_ready"), i + 1)
                    if n:
                        pe.wait_ge(sig("inverse_step"), i - T + 1)
                    for h in range(HA):
                        ins = M.matmul(bank[i % 2][:, h * P:(h + 1) * P], step_L[:, i % 2, h, :], ident if n == 0 else inverse[:, t, h, :], start=True, stop=True, skip_group_check=True)
                    ins.then_inc(sig("cross_done"), 1)
                    if i >= 1:
                        join(nc, pe, m, i - 1, cross, inverse, inverseT, ident)
            join(nc, pe, m, 7 * T - 1, cross, inverse, inverseT, ident)
            pe.wait_ge(sig("inverseT_step"), 7 * T)
            for t in range(T):
                if t >= 2:
                    pe.wait_ge(sig("u_ready"), t - 1)
                    pe.wait_ge(sig("wT_ready"), t - 1)
                for h in range(HA):
                    o = slice(h * P, (h + 1) * P)
                    M.matmul(bank[t % 2][:, o], inverseT[:, t, h, :], u_sb[:, t, h, :], start=True, stop=True, skip_group_check=True)
                    ins = M.matmul(bank[2 + t % 2][:, o], wT[:, t, h, :], inverseT[:, t, h, :], start=True, stop=True, skip_group_check=True)
                ins.then_inc(sig("uw_done"), 1)
            pe.wait_ge(sig("wT_ready"), T)
            pe.wait_ge(sig("ckvT_ready"), 1)

            def b_logits(i):
                t, h = i // HB, i % HB
                if i >= 2:
                    pe.wait_ge(sig("logits_ready"), i - 1)
                M.matmul(bank[3 + i % 2][:, 0:(t + 1) * P], q_bT[:, h, t * P:(t + 1) * P], ckvT[:, 0:(t + 1) * P], start=True, stop=True).then_inc(sig("b_logits_done"), 1)

            def b_turn(i):
                pe.wait_ge(sig("probs_ready"), i + 1)
                if i >= 1:
                    pe.wait_ge(sig("probsT_ready"), i)
                for k in range(i // HB + 1):
                    ins = M.transpose(bank[5][:, k * P:(k + 1) * P], probs[:, i % 2, k * P:(k + 1) * P], ident)
                ins.then_inc(sig("probs_turned"), 1)

            def b_weigh(i):
                t, h = i // HB, i % HB
                pe.wait_ge(sig("probsT_ready"), i + 1)
                if h == 0 and t >= 2:
                    pe.wait_ge(sig("ob_ready"), t - 1)
                for k in range(t + 1):
                    ins = M.matmul(bank[6 + t % 2][:, h * P:(h + 1) * P], ckv[:, k, :], probsT[:, i % 2, k * P:(k + 1) * P], start=(k == 0), stop=(k == t), skip_group_check=True)
                ins.then_inc(sig("weighed"), 1)

            def delta_before(t):
                if t:
                    pe.wait_ge(sig("state_ready"), t)
                    for h in range(HA):
                        ins = M.matmul(bank[0][:, h * P:(h + 1) * P], wT[:, t, h, :], state[:, h, :], start=True, stop=True, skip_group_check=True)
                    ins.then_inc(sig("ws_done"), 1)

            def delta_outputs(t):
                pe.wait_ge(sig("v_new_ready"), t + 1)
                if t:
                    pe.wait_ge(sig("oT_ready"), t)
                for h in range(HA):
                    o = slice(h * P, (h + 1) * P)
                    if t:
                        M.matmul(bank[2][:, o], state[:, h, :], qgT[:, t, h, :], start=True, stop=False, skip_group_check=True)
                    ins = M.matmul(bank[2][:, o], v_new[:, h, :], AT[:, t, h, :], start=(t == 0), stop=True, skip_group_check=True)
                ins.then_inc(sig("o_done"), 1)
                if t < T - 1:
                    for h in range(HA):
                        ins = M.matmul(bank[1][:, h * P:(h + 1) * P], kg[:, t, h, :], v_new[:, h, :], start=True, stop=True, skip_group_check=True)
                    ins.then_inc(sig("gain_done"), 1)

            for i in range(N_B + 2):
                if i < N_B:
                    b_logits(i)
                if 1 <= i <= N_B:
                    b_turn(i - 1)
                if i >= 2:
                    b_weigh(i - 2)
                if delta_chunk(i, 0) is not None:
                    delta_before(delta_chunk(i, 0))
                if delta_chunk(i, 1) is not None:
                    delta_outputs(delta_chunk(i, 1))
            for h in range(HA):
                pe.wait_ge(sig("o_squared"), h + 1)
                M.matmul(bank[h][:], ones, flat(o_square, h), start=True, stop=True).then_inc(sig("o_summed"), 1)
            pe.wait_ge(sig("w_uv_loaded"), 16)
            pe.wait_ge(sig("ob_ready"), T)
            for h in range(HB):
                if h >= 2:
                    pe.wait_ge(sig("mixT_b"), h - 1)
                else:
                    pe.wait_ge(sig("oT_ready"), T)
                M.matmul(bank[4 + h % 2][:], w_uv[:, h, :], mixT[:, 4 + h, :], start=True, stop=True).then_inc(sig("uv_done"), 1)
            def mix(t, c, ks, first, last):
                for k in ks:
                    if t == 0 and c == 0 and k < 4:
                        pe.wait_ge(sig("mixT_a"), k + 1)
                    ins = M.matmul(bank[2 * (t % 2) + c][:], mixT[:, k, t * P:(t + 1) * P], w_out[:, k, c * 512:(c + 1) * 512], start=(first and k == ks[0]), stop=(last and k == ks[-1]), skip_group_check=True)
                if last:
                    ins.then_inc(sig("mix_done"), 1)

            pe.wait_ge(sig("w_out_loaded"), 16 * KT)
            pe.wait_ge(sig("mixT_b"), HB)
            pe.wait_ge(sig("var_ready"), 13)
            for n in range(4):
                mix(n // 2, n % 2, range(4, KT), True, False)
            for n in range(4):
                mix(n // 2, n % 2, range(4), False, True)
            for t in range(2, T):
                pe.wait_ge(sig("x_out"), t - 1)
                for c in range(2):
                    mix(t, c, range(KT), True, True)

        @block.vector
        def _(dve):
            chain = Chain(dve, sig("D_vector_own"))
            V = nc.vector

            def variance(v, s, scale):
                V.tensor_scalar(v, s, scale, EPS, ALU.mult, ALU.add).then_inc(sig("var_ready"), 1)

            def root(k, y, v, t):
                dve.wait_ge(sig("rsqrt_ready"), k + 1)
                chain.link(newton(nc, chain, y, v, t))

            V.memset(half, -0.5).then_inc(sig("half_ready"), 1)
            for n in range(2 * T):
                o = x[:, n // 2, (n % 2) * 512:(n % 2 + 1) * 512]
                dve.wait_ge(sig("expert_bias_done"), n + 1)
                V.tensor_tensor(o, bank[n][:], o, ALU.add).then_inc(sig("expert_bias_added"), 1)
            for t in range(T):
                dve.wait_ge(sig("expert_bias_added"), 2 * t + 2)
                dve.wait_ge(sig(f"rows_loaded{t}"), 16 * TOPK)
                for k in range(TOPK):
                    n = t * TOPK + k
                    if k:
                        dve.wait_ge(sig("combined"), n)
                    V.scalar_tensor_tensor(out=x[:, t, :], in0=rows[n], scalar=m["gates"][:, t, k:k + 1], in1=x[:, t, :], op0=ALU.mult, op1=ALU.add).then_inc(sig("combined"), 1)
            dve.wait_ge(sig("g_final_loaded"), 16)
            for t in range(T):
                dve.wait_ge(sig("root0"), t + 1)
                V.scalar_tensor_tensor(out=x[:, t, :], in0=x[:, t, :], scalar=ssi[:, t:t + 1], in1=g_final, op0=ALU.mult, op1=ALU.mult).then_inc(sig("x_normed"), 1)
            for t in range(T):
                dve.wait_ge(sig("root1"), t + 1)
                V.tensor_scalar(xn[:, t, :], x[:, t, :], sst[:, t:t + 1], None, ALU.mult).then_inc(sig("xn_ready"), 1)
            dve.wait_ge(sig("ckv_squares"), 1)
            variance(ssv, ss, 1.0 / P)
            dve.wait_ge(sig("small_ready"), 1)
            chain.link(V.tensor_scalar(w_index, small[:, :, 0:HI], HI ** -0.5 * DI ** -0.5, None, ALU.mult))
            for i in range(3 * HI):
                t, h = 1 + i // HI, i % HI
                n = (t + 1) * P
                if i == 6:
                    dve.wait_ge(sig("ckv_root"), 1)
                    dve.wait_ge(sig("g_kv_loaded"), 16)
                    for q in range(T):
                        src = bank[6 + q // 3][:, (q % 3) * 144 + 16:(q % 3) * 144 + 144]
                        ins = V.scalar_tensor_tensor(out=ckv[:, q, :], in0=src, scalar=ssi[:, q:q + 1], in1=g_kv, op0=ALU.mult, op1=ALU.mult)
                    ins.then_inc(sig("ckv_ready"), 1)
                dve.wait_ge(sig("relu_ready"), i + 1)
                if h == 0:
                    V.tensor_scalar(score[t], relu[:, i % 2, 0:n], w_index[:, t, 0:1], None, ALU.mult).then_inc(sig("relu_read"), 1)
                else:
                    dve.wait_ge(sig("relu_read"), i)
                    V.scalar_tensor_tensor(out=score[t], in0=relu[:, i % 2, 0:n], scalar=w_index[:, t, h:h + 1], in1=score[t], op0=ALU.mult, op1=ALU.add).then_inc(sig("relu_read"), 1)
                if h == HI - 1:
                    dve.wait_ge(sig("relu_read"), i + 1)
                    chain.link(V.tensor_tensor(score[t][:, t * P:n], score[t][:, t * P:n], negmask, ALU.add))

            dve.wait_ge(sig("decay_loaded"), 32)
            chain.link(V.tensor_tensor(s1, small[:, :, 12:16], repeat(dt_bias, T), ALU.add))
            chain.link(V.tensor_scalar(s3, s1, -1.0, None, ALU.mult))
            chain.link(V.tensor_tensor(s2, s1, s3, ALU.max))
            V.tensor_scalar(s1, s1, 0.0, None, ALU.max).then_inc(sig("ab_ready"), 1)
            dve.wait_ge(sig("b_exp"), 1)
            chain.link(V.tensor_scalar(beta, beta, 1.0, None, ALU.add))
            chain.link(V.reciprocal(beta, beta))
            dve.wait_ge(sig("ab_ready"), 1)
            dve.wait_ge(sig("ab_exp"), 1)
            dve.wait_ge(sig("a_exp"), 1)
            chain.link(V.tensor_scalar(s3, s2, 2.0, None, ALU.add))
            chain.link(V.reciprocal(s3, s3))
            chain.link(V.tensor_tensor(s2, s2, s3, ALU.mult))
            chain.link(V.tensor_tensor(s3, s2, s2, ALU.mult))
            chain.link(V.tensor_scalar(g, s3, 2.0 / 17.0, 2.0 / 15.0, ALU.mult, ALU.add))
            for n in (13, 11, 9, 7, 5, 3, 1):
                chain.link(V.tensor_tensor(g, g, s3, ALU.mult))
                chain.link(V.tensor_scalar(g, g, 2.0 / n, None, ALU.add))
            chain.link(V.tensor_tensor(g, g, s2, ALU.mult))
            chain.link(V.tensor_tensor(g, g, s1, ALU.add))
            chain.link(V.tensor_tensor(g, g, repeat(a_log, T), ALU.mult))
            V.tensor_scalar(g, g, -1.0, None, ALU.mult).then_inc(sig("g_ready"), 1)
            GONE = -3.0e38

            def choose(i):
                t, r = 1 + i // 16, i % 16
                chain.link(V.max(best, score[t]))
                chain.link(V.match_replace(score[t], best, score[t], GONE))
                if r == 15:
                    V.tensor_scalar(score[t], score[t], -2.0e38, NEG, ALU.is_gt, ALU.mult).then_inc(sig("chosen"), 1)

            rounds = iter(range(48))

            def l2(n):
                dve.wait_ge(sig("qk_summed"), n + 1)
                variance(var, bank[7][:], 1.0)

            def l2_end(n):
                root(n, inv, var, tmp)
                dve.wait_ge(sig("qk_squared"), n + 1)
                V.scalar_tensor_tensor(out=qkvT[:, n, :], in0=qkvT[:, n, :], scalar=(P ** -0.5 if n < 4 else 1.0), in1=inv, op0=ALU.mult, op1=ALU.mult).then_inc(sig("qk_normed"), 1)

            for n in range(12):
                dve.wait_ge(sig("tile_read"), 6 + n)
                dve.wait_ge(sig("taps_zero"), 1)
                w = [col(m, "conv", 12 * j + n) for j in range(CONV)]
                chain.link(V.tensor_scalar(qkvT[:, n, :], taps[:, n % 2, 0:S], w[0], None, ALU.mult))
                for j in range(1, CONV):
                    ins = V.scalar_tensor_tensor(out=qkvT[:, n, :], in0=taps[:, n % 2, j:j + S], scalar=w[j], in1=qkvT[:, n, :], op0=ALU.mult, op1=ALU.add)
                    if j < CONV - 1:
                        chain.link(ins)
                ins.then_inc(sig("conv_ready"), 1)
                choose(next(rounds))
                dve.wait_ge(sig("conv_sigm"), n + 1)
                V.tensor_tensor(qkvT[:, n, :], qkvT[:, n, :], relu[:, n % 2, :], ALU.mult).then_inc(sig("silu_ready"), 1)
                if 1 <= n <= 8:
                    l2(n - 1)
                choose(next(rounds))
                if 1 <= n <= 8:
                    l2_end(n - 1)
            for n in range(8):
                dst = (z_a, z_b)[n // 4][:, n % 4, :]
                for _ in range(3):
                    choose(next(rounds))
                dve.wait_ge(sig("z_sigm"), n + 1)
                V.tensor_tensor(dst, dst, square[:, n % 2, :], ALU.mult).then_inc(sig("z_ready"), 1)
            dve.wait_ge(sig("gc_done"), 1)
            V.tensor_copy(gc, bank[6][:, 0:16].rearrange("p (t h) -> p t h", t=T)).then_inc(sig("gc_ready"), 1)
            dve.wait_ge(sig("gc_ready"), 1)
            for t in range(T):
                b0, b1 = 4 * (t % 2), 4 * (t % 2) + 1
                dve.wait_ge(sig("rows_done"), t + 1)
                if t >= 2:
                    dve.wait_ge(sig("strict_ready"), t - 1)
                    dve.wait_ge(sig("upper_ready"), t - 1)
                last = bank[b0][:].rearrange("p (h n) -> p h n", h=HA)[:, :, P - 1]
                V.tensor_tensor(egl[:, t, :], last, gc[:, t, :], ALU.subtract)
                for h in range(HA):
                    ins = V.tensor_scalar(diff[:, t % 2, h, :], bank[b0][:, h * P:(h + 1) * P], gc[:, t, h:h + 1], 0.0, ALU.subtract, ALU.min)
                ins.then_inc(sig("diff_ready"), 1)
                if t == 0:
                    dve.wait_ge(sig("eg_ready"), 1)
                    chain.link(V.tensor_tensor(bg, beta, eg, ALU.mult))
                dve.wait_ge(sig("kk_done"), t + 1)
                dve.wait_ge(sig("strict_ready"), t + 1)
                chain.link(V.tensor_tensor(LT[:, t], heads(2), inv.rearrange("p (h n) -> p h n", h=HA), ALU.mult))
                chain.link(V.tensor_tensor(LT[:, t], LT[:, t], heads(b1), ALU.mult))
                dve.wait_ge(sig("upper_ready"), t + 1)
                V.tensor_tensor(AT[:, t], heads(3), tmp.rearrange("p (h n) -> p h n", h=HA), ALU.mult).then_inc(sig("chunks_ready"), 1)
                dve.wait_ge(sig("decay_row_ready"), t + 1)
                V.tensor_copy(gl[:, t, :], decay_row[:, t % 2, :, P - 1])
                V.tensor_tensor(qgT[:, t], qkvT[:, 0:4, t * P:(t + 1) * P], decay_row[:, t % 2], ALU.mult).then_inc(sig("qg_ready"), 1)
                dve.wait_ge(sig("kv_turned"), t + 1)
                dve.wait_ge(sig("egl_ready"), t + 1)
                V.tensor_tensor(kg[:, t], heads(6), spread(egl[:, t, :], P), ALU.mult)
                V.tensor_tensor(u_sb[:, t], heads(7), spread(beta[:, t, :], P), ALU.mult)
                V.tensor_tensor(wT[:, t], heads(6), spread(bg[:, t, :], P), ALU.mult).then_inc(sig("kv_chunk_ready"), 1)
            for i in range(7 * T):
                n, t = i // T, i % T
                one = repeat(ident, HA)
                dve.wait_ge(sig("joined"), i + 1)
                prev = one if n == 0 else inverse[:, t]
                prevT = one if n == 0 else inverseT[:, t]
                if n:
                    dve.wait_ge(sig("inverse_step"), i - T + 1)
                    dve.wait_ge(sig("inverseT_step"), i - T + 1)
                if n < 6:
                    V.tensor_tensor(inverse[:, t], prev, heads(2 + i % 2), ALU.subtract).then_inc(sig("inverse_step"), 1)
                V.tensor_tensor(inverseT[:, t], prevT, heads(4 + i % 2), ALU.subtract).then_inc(sig("inverseT_step"), 1)
            for t in range(T):
                dve.wait_ge(sig("uw_done"), t + 1)
                V.tensor_copy(u_sb[:, t], heads(t % 2)).then_inc(sig("u_ready"), 1)
            def delta_values(t):
                dve.wait_ge(sig("u_ready"), T)
                if t == 0:
                    V.tensor_copy(v_new, u_sb[:, 0]).then_inc(sig("v_new_ready"), 1)
                else:
                    dve.wait_ge(sig("ws_done"), t)
                    V.tensor_tensor(v_new, u_sb[:, t], heads(0), ALU.subtract).then_inc(sig("v_new_ready"), 1)

            def delta_state(t):
                dve.wait_ge(sig("gain_done"), t + 1)
                if t == 0:
                    ins = V.tensor_copy(state, heads(1))
                else:
                    dve.wait_ge(sig("state_ready"), t)
                    for h in range(HA):
                        ins = V.scalar_tensor_tensor(out=state[:, h, :], in0=state[:, h, :], scalar=gl[:, t, h:h + 1], in1=bank[1][:, h * P:(h + 1) * P], op0=ALU.mult, op1=ALU.add)
                ins.then_inc(sig("state_ready"), 1)

            for i in range(N_B + 3):
                if delta_chunk(i, 1) is not None:
                    delta_values(delta_chunk(i, 1))
                if delta_chunk(i, 2) is not None and delta_chunk(i, 2) < T - 1:
                    delta_state(delta_chunk(i, 2))
                if i < N_B:
                    t = i // HB
                    n = (t + 1) * P
                    dve.wait_ge(sig("b_logits_done"), i + 1)
                    dve.wait_ge(sig("bias_sum_ready"), i + 1)
                    if i >= 2:
                        dve.wait_ge(sig("probs_exp"), i - 1)
                    V.scalar_tensor_tensor(out=logits[:, i % 2, 0:n], in0=bank[3 + i % 2][:, 0:n], scalar=SCALE_B, in1=bias_sum[:, i % 2, 0:n], op0=ALU.mult, op1=ALU.add).then_inc(sig("logits_ready"), 1)
                    dve.wait_ge(sig("logits_ready"), i + 1)
                    chain.link(V.tensor_reduce(rowmax[:, i:i + 1], logits[:, i % 2, 0:n], AX, ALU.max))
                    V.tensor_scalar(rowmax[:, i:i + 1], rowmax[:, i:i + 1], -1.0, None, ALU.mult).then_inc(sig("rowmax_ready"), 1)
                if 1 <= i <= N_B:
                    j = i - 1
                    nj = (j // HB + 1) * P
                    dve.wait_ge(sig("probs_exp"), j + 1)
                    chain.link(V.reciprocal(rowinv[:, j:j + 1], rowsum[:, j:j + 1]))
                    V.tensor_scalar(probs[:, j % 2, 0:nj], probs[:, j % 2, 0:nj], rowinv[:, j:j + 1], None, ALU.mult).then_inc(sig("probs_ready"), 1)
                if i >= HB + 2 and (i - 2) % HB == 0:
                    t = (i - 2) // HB - 1
                    dve.wait_ge(sig("weighed"), HB * (t + 1))
                    V.tensor_copy(mixT[:, 4:8, t * P:(t + 1) * P], heads(6 + t % 2)).then_inc(sig("ob_ready"), 1)
            for h in range(HA):
                dve.wait_ge(sig("o_summed"), h + 1)
                variance(flat(o_var, h), bank[h][:], 1.0 / P)
            for h in range(HA):
                V.scalar_tensor_tensor(out=mixT[:, h, :], in0=oT[:, h, :], scalar=col(m, "g_gdn"), in1=z_a[:, h, :], op0=ALU.mult, op1=ALU.mult).then_inc(sig("mixT_gated"), 1)
            for h in range(HB):
                dve.wait_ge(sig("uv_done"), h + 1)
                V.tensor_tensor(mixT[:, 4 + h, :], bank[4 + h % 2][:], z_b[:, h, :], ALU.mult).then_inc(sig("mixT_b"), 1)
            for h in range(HA):
                root(8 + h, flat(o_inv, h), flat(o_var, h), flat(o_tmp, h))
                dve.wait_ge(sig("mixT_gated"), h + 1)
                V.tensor_tensor(mixT[:, h, :], mixT[:, h, :], flat(o_inv, h), ALU.mult).then_inc(sig("mixT_a"), 1)
            for t in range(T):
                c1 = slice(t, t + 1)
                dve.wait_ge(sig("mix_squared"), 2 * t + 2)
                chain.link(V.tensor_tensor(ss[:, c1], ss[:, c1], ss2[:, c1], ALU.add))
                V.tensor_scalar(ssv[:, c1], ss[:, c1], 1.0 / D, EPS, ALU.mult, ALU.add).then_inc(sig("post_var"), 1)
                dve.wait_ge(sig("post_root"), t + 1)
                for c in range(2):
                    o = slice(c * 512, (c + 1) * 512)
                    part = (inv, tmp)[c]
                    if t:
                        dve.wait_ge(sig("x_out"), t)
                    chain.link(V.scalar_tensor_tensor(out=part, in0=bank[2 * (t % 2) + c][:], scalar=ssi[:, c1], in1=m["gate_row"][:, o], op0=ALU.mult, op1=ALU.mult))
                    ins = V.tensor_tensor(x[:, t, o], x[:, t, o], part, ALU.add)
                ins.then_inc(sig("x_out"), 1)


def join(nc, pe, m, i, cross, inverse, inverseT, ident):
    sig, bank = m["sig"], m["bank"]
    n, t = i // T, i % T
    pe.wait_ge(sig("cross_ready"), i + 1)
    if i >= 2:
        pe.wait_ge(sig("inverseT_step"), i - 1)
    for h in range(HA):
        o = slice(h * P, (h + 1) * P)
        turned = ident if n == 0 else inverseT[:, t, h, :]
        if n < 6:
            nc.tensor.matmul(bank[2 + i % 2][:, o], turned, cross[:, i % 2, h, :], start=True, stop=True, skip_group_check=True)
        ins = nc.tensor.matmul(bank[4 + i % 2][:, o], cross[:, i % 2, h, :], turned, start=True, stop=True, skip_group_check=True)
    ins.then_inc(sig("joined"), 1)


INPUTS = ["x", "positions", "g_attn_norm", "w_in", "w_pool", "b_pool", "pool_scale", "g_q_a", "w_q_b", "g_kv_a",
          "w_kv_b", "g_out_pool", "g_out_attn", "w_out", "g_ffn_norm", "w_router", "b_router", "w_gate_up",
          "b_gate_up", "w_down", "b_down", "g_final", "c_2", "w_ada_2", "b_ada_2", "g_pre_2", "w_in_2",
          "conv_w_2", "a_log_2", "dt_bias_2", "g_gdn_2", "g_kv_2", "w_uv_2", "rel_bias_2", "w_out_2", "g_post_2"]


def kernel(**inputs):
    import numpy as _np
    import concourse.bacc as _bacc
    from concourse import mybir as _mybir
    from concourse.bass_utils import run_bass_kernel_spmd as _run

    nc = _bacc.Bacc("TRN2", target_bir_lowering=False, num_devices=1)
    arrays, aps = {}, {}
    table, levels, onehot = constants()
    for name, value in [(n, inputs[n]) for n in INPUTS] + [("constants", table), ("levels", levels), ("buckets", onehot)]:
        v = _np.ascontiguousarray(value)
        arrays[f"in_{name}"] = v
        aps[name] = nc.dram_tensor(f"in_{name}", v.shape, _mybir.dt.from_np(v.dtype), kind="ExternalInput").ap()
    out = nc.dram_tensor("out_x", (1, S, D), F32, kind="ExternalOutput").ap()
    build(nc, aps, out)
    return _run(nc, [arrays], core_ids=[0]).results[0]["out_x"]
```
